# Optimizing a Trainium2 kernel written in Bass

```python
import math
import jax, jax.numpy as jnp
from jax import lax
import numpy as np

D_MODEL = 1024
BATCH = 1
SEQ = 2048
DEPTH = 1

HEAD_DIM = 64
N_Q_HEADS = 8
N_KV_HEADS = 2
GQA_GROUP = N_Q_HEADS // N_KV_HEADS
ATTN_WIDTH = N_Q_HEADS * HEAD_DIM
KV_WIDTH = N_KV_HEADS * HEAD_DIM
WINDOW = 128
BLOCK = 128
POOL_WIDTH = D_MODEL - ATTN_WIDTH
POOL_SIZES = (2, 4, 8, 16)
N_POOL_GROUPS = len(POOL_SIZES)
POOL_GROUP_DIM = POOL_WIDTH // N_POOL_GROUPS
IN_WIDTH = ATTN_WIDTH + 2 * KV_WIDTH + POOL_WIDTH
MIX_WIDTH = ATTN_WIDTH + POOL_WIDTH
N_BUCKETS = 32
MAX_DISTANCE = 128
D_FF = -(-8 * D_MODEL // (3 * 256)) * 256
PLE_DIM = 256
EPS = 1e-6

kernel_name = "hymba_swa_sink_pool_hybrid"

def rmsnorm(x, g):
    xf = x.astype(jnp.float32)
    y = xf * lax.rsqrt(jnp.mean(xf * xf, axis=-1, keepdims=True) + EPS)
    return (y * g.astype(jnp.float32)).astype(x.dtype)

def t5_causal_bucket(dist):
    n = np.maximum(dist, 0)
    max_exact = N_BUCKETS // 2
    nf = np.maximum(n, 1).astype(np.float64)
    large = max_exact + (np.log(nf / max_exact) / math.log(MAX_DISTANCE / max_exact)
                         * (N_BUCKETS - max_exact)).astype(np.int64)
    large = np.minimum(large, N_BUCKETS - 1)
    return np.where(n < max_exact, n, large).astype(np.int32)

def sliding_window_sink_attention(q, k, v, sinks, rel_bias):
    B, S = q.shape[0], q.shape[1]
    nb = S // BLOCK
    qb = q.reshape(B, nb, BLOCK, N_KV_HEADS, GQA_GROUP, HEAD_DIM)
    kb = k.reshape(B, nb, BLOCK, N_KV_HEADS, HEAD_DIM)
    vb = v.reshape(B, nb, BLOCK, N_KV_HEADS, HEAD_DIM)
    pad = ((0, 0), (1, 0), (0, 0), (0, 0), (0, 0))
    k2 = jnp.concatenate([jnp.pad(kb, pad)[:, :-1], kb], axis=2)
    v2 = jnp.concatenate([jnp.pad(vb, pad)[:, :-1], vb], axis=2)

    logits = jnp.einsum('bnqhgd,bnkhd->bnhgqk', qb, k2).astype(jnp.float32) * (HEAD_DIM ** -0.5)

    i_idx = np.arange(BLOCK)[:, None]
    j_idx = np.arange(2 * BLOCK)[None, :]
    d = BLOCK + i_idx - j_idx
    bucket = t5_causal_bucket(d)
    bias = rel_bias.astype(jnp.float32)[bucket]
    bias = jnp.transpose(bias, (2, 0, 1)).reshape(N_KV_HEADS, GQA_GROUP, BLOCK, 2 * BLOCK)

    rel_ok = (d >= 0) & (d < WINDOW)
    blk_ok = (np.arange(nb)[:, None, None] > 0) | (j_idx[None] >= BLOCK)
    mask = jnp.asarray(rel_ok[None] & blk_ok)[None, :, None, None]

    logits = jnp.where(mask, logits + bias, -jnp.inf)
    sink = sinks.astype(jnp.float32).reshape(N_KV_HEADS, GQA_GROUP)[:, :, None, None]
    m = jnp.maximum(jnp.max(logits, axis=-1, keepdims=True), sink)
    pexp = jnp.exp(logits - m)
    probs = pexp / (jnp.sum(pexp, axis=-1, keepdims=True) + jnp.exp(sink - m))
    out = jnp.einsum('bnhgqk,bnkhd->bnqhgd', probs.astype(v.dtype), v2)
    return out.reshape(B, S, N_Q_HEADS * HEAD_DIM)

def multiscale_pool_mixer(u, w_pool, pool_scale):
    B, S = u.shape[0], u.shape[1]
    ug = u.reshape(B, S, N_POOL_GROUPS, POOL_GROUP_DIM).astype(jnp.float32)
    cs = jnp.cumsum(ug, axis=1)
    t1 = jnp.arange(1, S + 1, dtype=jnp.float32)
    outs = []
    for g, w in enumerate(POOL_SIZES):
        c = cs[:, :, g]
        lag = jnp.pad(c, ((0, 0), (w, 0), (0, 0)))[:, :S]
        cnt = jnp.minimum(t1, float(w))[None, :, None]
        outs.append((c - lag) / cnt - ug[:, :, g])
    pooled = jnp.stack(outs, axis=2)
    y = jnp.einsum('bsgc,gcd->bsgd', pooled, w_pool.astype(jnp.float32))
    y = y.reshape(B, S, POOL_WIDTH) * pool_scale.astype(jnp.float32)
    return y.astype(u.dtype)

def setup_inputs(seed: int = 0) -> dict:
    key = jax.random.key(seed)
    ks = jax.random.split(key, 20)
    f32 = jnp.float32
    nrm = lambda k, shape, s: jax.random.normal(k, shape, f32) * s
    return {
        "x": nrm(ks[0], (BATCH, SEQ, D_MODEL), 1.0),
        "p": nrm(ks[1], (DEPTH, BATCH, SEQ, PLE_DIM), 1.0),
        "w_in": nrm(ks[2], (DEPTH, D_MODEL, IN_WIDTH), D_MODEL ** -0.5),
        "w_out": nrm(ks[3], (DEPTH, MIX_WIDTH, D_MODEL), MIX_WIDTH ** -0.5),
        "g_attn_norm": 1.0 + nrm(ks[4], (DEPTH, D_MODEL), 0.05),
        "g_q": 1.0 + nrm(ks[5], (DEPTH, HEAD_DIM), 0.05),
        "g_k": 1.0 + nrm(ks[6], (DEPTH, HEAD_DIM), 0.05),
        "attn_sinks": nrm(ks[7], (DEPTH, N_Q_HEADS), 1.0),
        "rel_bias": nrm(ks[8], (N_BUCKETS, N_Q_HEADS), 0.3),
        "w_pool": nrm(ks[9], (DEPTH, N_POOL_GROUPS, POOL_GROUP_DIM, POOL_GROUP_DIM), POOL_GROUP_DIM ** -0.5),
        "pool_scale": 1.0 + nrm(ks[10], (DEPTH, POOL_WIDTH), 0.1),
        "g_ffn_norm": 1.0 + nrm(ks[11], (DEPTH, D_MODEL), 0.05),
        "w_gate": nrm(ks[12], (DEPTH, D_MODEL, D_FF), D_MODEL ** -0.5),
        "w_up": nrm(ks[13], (DEPTH, D_MODEL, D_FF), D_MODEL ** -0.5),
        "w_down": nrm(ks[14], (DEPTH, D_FF, D_MODEL), D_FF ** -0.5),
        "g_ple_norm": 1.0 + nrm(ks[15], (DEPTH, D_MODEL), 0.05),
        "w_ple_gate": nrm(ks[16], (DEPTH, D_MODEL, D_MODEL), D_MODEL ** -0.5),
        "w_ple_proj": nrm(ks[17], (DEPTH, PLE_DIM, D_MODEL), PLE_DIM ** -0.5),
    }

def reference(x, p, w_in, w_out, g_attn_norm, g_q, g_k, attn_sinks, rel_bias, w_pool, pool_scale,
              g_ffn_norm, w_gate, w_up, w_down, g_ple_norm, w_ple_gate, w_ple_proj):
    B, S = x.shape[0], x.shape[1]
    h = x
    for i in range(DEPTH):
        hn = rmsnorm(h, g_attn_norm[i])
        z = hn @ w_in[i]
        q = z[..., :ATTN_WIDTH]
        k = z[..., ATTN_WIDTH:ATTN_WIDTH + KV_WIDTH]
        v = z[..., ATTN_WIDTH + KV_WIDTH:ATTN_WIDTH + 2 * KV_WIDTH]
        u = z[..., ATTN_WIDTH + 2 * KV_WIDTH:]
        q = rmsnorm(q.reshape(B, S, N_Q_HEADS, HEAD_DIM), g_q[i])
        k = rmsnorm(k.reshape(B, S, N_KV_HEADS, HEAD_DIM), g_k[i])
        v = v.reshape(B, S, N_KV_HEADS, HEAD_DIM)
        a = sliding_window_sink_attention(q, k, v, attn_sinks[i], rel_bias)
        m = multiscale_pool_mixer(u, w_pool[i], pool_scale[i])
        h = h + jnp.concatenate([a, m], axis=-1) @ w_out[i]
        hn = rmsnorm(h, g_ffn_norm[i])
        h = h + (jax.nn.silu(hn @ w_gate[i]) * (hn @ w_up[i])) @ w_down[i]
        gate = jax.nn.sigmoid(rmsnorm(h, g_ple_norm[i]) @ w_ple_gate[i])
        h = h + gate * (p[i] @ w_ple_proj[i])
    return h


_drawn_inputs = setup_inputs


def setup_inputs(seed=0):
    import zlib

    import numpy as np

    out = dict(_drawn_inputs(seed))
    spreads = {}
    factors = {'g_q': 8.0, 'g_k': 8.0, 'attn_sinks': 200.0, 'g_ple_norm': 7.747, 'rel_bias': 3.402}
    for name, (base, spread) in spreads.items():
        noise = np.random.default_rng([zlib.crc32(name.encode()), seed]).standard_normal(out[name].shape)
        drawn = base * np.exp(spread * noise) if base else spread * noise
        out[name] = __import__('jax').numpy.asarray(drawn.astype(out[name].dtype))
    for name, factor in factors.items():
        out[name] = (out[name] * factor).astype(out[name].dtype)
    return out
```

```python
import numpy as np
from contextlib import ExitStack

import concourse.bass as bass
from concourse import mybir

F32 = mybir.dt.float32
F32R = mybir.dt.float32r
BF16 = mybir.dt.bfloat16
ALU = mybir.AluOpType
ACT = mybir.ActivationFunctionType
AX = mybir.AxisListType

P = 128
HEAD_DIM = 64
NQ = 8
NKV = 2
PAIRS = NQ // NKV
QW = NQ * HEAD_DIM
KVW = NKV * HEAD_DIM
QKW = QW + KVW
WINDOW = 128
POOL_SIZES = (2, 4, 8, 16)
NPOOL = len(POOL_SIZES)
CARRY = 16
N_BUCKETS = 32
MAX_DISTANCE = 128
EPS = 1e-6
MASKED = -1e30
BAND = 3 * P - 1
T = 512
NB = T // P
PANEL = 1024
GROUPS = (8, 8, 6)
OUT_P, Z_P, FFN_P, PROJ_P, GATE_P = 8, 10, 3 * sum(GROUPS), 2, 8
TILE_P = OUT_P + Z_P + FFN_P + PROJ_P + GATE_P


def build(nc, x, p, w_in, w_out, g_attn, g_q, g_k, sinks, rel_bias, w_pool, pool_scale, g_ffn,
          w_gate, w_up, w_down, g_ple, w_ple_gate, w_ple_proj, identity, onehot, edge, out):
    S, D = x.shape
    KC = D // P
    NT = S // T
    LAST = NT - 1
    NCH = sum(GROUPS)
    KP = w_ple_proj.shape[0] // P
    scratch = nc.dram_tensor("band_rows", (NQ, P * BAND), F32, kind="Internal")

    ctx = ExitStack()
    with ctx:
        base = [(nc.sbuf_base + 63) // 64 * 64]

        def sb(name, shape, dt=F32, at=None):
            size = int(np.prod(shape[1:])) * (2 if dt == BF16 else 4)
            where = at if at is not None else base[0]
            if at is None:
                base[0] += (size + 31) // 32 * 32
            return nc.alloc_sbuf_tensor_at(name, list(shape), dt, offset=where)

        def sem(name):
            return ctx.enter_context(nc.semaphore(name))

        wide_at = base[0]
        wide_hi = sb("wide_hi", [P, KC, T], F32R)
        wide_lo = sb("wide_lo", [P, KC, T], F32R)
        proj = sb("proj", [P, NB, D], F32, at=wide_at)
        mix_hi = sb("mix_hi", [P, KC, T], F32R)
        mix_lo = sb("mix_lo", [P, KC, T], F32R)
        hn_hi = sb("hn_hi", [P, KC, T], F32R)
        hn_lo = sb("hn_lo", [P, KC, T], F32R)
        h = sb("h", [P, NB, D])
        h_flat = h[:, :, :].rearrange("p b d -> p (b d)")
        rel_rows = h_flat[:, 0:NQ * P].rearrange("p (h q) -> p h q", h=NQ)
        band = h_flat[:, NQ * P:NQ * (P + BAND)].rearrange("p (h s) -> p h s", h=NQ)
        stage = sb("stage", [P, 2, D])
        squares = sb("squares", [P, D], BF16)
        gains = sb("gains", [P, 3, D])
        u = sb("u", [P, NPOOL, CARRY + T])
        sums = sb("sums", [P, 2 * (CARRY + T)])
        sum_a, sum_b = sums[:, 0:CARRY + T], sums[:, CARRY + T:2 * (CARRY + T)]
        qkv_at = base[0]
        qkv = sb("qkv", [P, NB, QKW + KVW])
        p_rows = qkv[:, :, :].rearrange("p b n -> p (b n)")[:, 0:NB * KP * P].rearrange(
            "p (b n) -> p b n", b=NB)
        p_hi = sb("p_hi", [P, KP, T], F32R, at=qkv_at + NB * KP * P * 4)
        p_lo = sb("p_lo", [P, KP, T], F32R, at=qkv_at + NB * KP * P * 4 + KP * T * 4)
        qk_sq = sums[:, 0:QKW]
        qkn = sb("qkn", [P, QKW])
        qz = sb("qz", [P, PAIRS, 2, P])
        kcat = sb("kcat", [P, 2 * P])
        vcat = sb("vcat", [P, 2, KVW])
        scores = sb("scores", [P, 2, 2 * P])
        probs = sb("probs", [P, 2, 2 * P])
        probsT = sb("probsT", [P, 2, 2 * P])
        bias = sb("bias", [P, PAIRS, 2, 2 * P])
        gqk = sb("gqk", [P, QKW])
        wp_hi = sb("wp_hi", [P, NPOOL, P], F32R)
        wp_lo = sb("wp_lo", [P, NPOOL, P], F32R)
        act_a = sb("act_a", [P, T])
        act_b = sb("act_b", [P, T])
        raw = sb("raw", [P, 2, PANEL])
        w_hi = sb("w_hi", [P, 2, PANEL], F32R)
        w_lo = sb("w_lo", [P, 2, PANEL], F32R)
        ident = sb("ident", [P, P])
        onehot_sb = qkv[0:N_BUCKETS + 1, 0, 0:3 * P]
        rel_sb = sb("rel_sb", [N_BUCKETS, NQ])
        edge_sb = sb("edge_sb", [P, NPOOL, CARRY])
        scale_sb = sb("scale_sb", [P, NPOOL])
        sink = sb("sink", [P, 2, PAIRS])
        neg_sink = sb("neg_sink", [P, 2, PAIRS])
        ss = sb("ss", [P, NB])
        ms = sb("ms", [P, NB])
        rstd = sb("rstd", [P, NB])
        minus_half = sb("minus_half", [P, 1])
        qss = sb("qss", [P, NB, NQ + NKV])
        qms = sb("qms", [P, NB, NQ + NKV])
        qrs = sb("qrs", [P, NB, NQ + NKV])
        neg_max = sb("neg_max", [P, 2])
        row_max = sb("row_max", [P, 2])
        row_sum = sb("row_sum", [P, 2])
        sink_exp = sb("sink_exp", [P, 2])
        den = sb("den", [P, 2])
        rden = sb("rden", [P, 2])
        assert base[0] <= nc.sbuf_usable_end, (base[0], nc.sbuf_usable_end)

        bank = [ctx.enter_context(nc.psum_tensor(f"bank{i}", [P, T], F32)) for i in range(8)]

        consts = sem("consts_landed")
        band_built, band_stored, bias_landed, bias_prev = (
            sem("band_built"), sem("band_stored"), sem("bias_landed"), sem("bias_prev_landed"))
        rel_ready, band_banks = sem("rel_ready"), sem("band_banks")
        half_ready, wp_landed, wp_hi_done, wp_lo_done = (
            sem("half_ready"), sem("wp_landed"), sem("wp_hi_done"), sem("wp_lo_done"))
        landed = [sem("panel_landed_even"), sem("panel_landed_odd")]
        hi_done, lo_done, panel_used = sem("panel_hi"), sem("panel_lo"), sem("panel_used")
        x_landed = [sem("x_landed_even"), sem("x_landed_odd")]
        sumsq, ms_done, rstd_done, xn_done, nT = (
            sem("sumsq"), sem("mean_square"), sem("rstd_done"), sem("normalised"), sem("norm_T"))
        nhi, nlo = sem("norm_hi"), sem("norm_lo")
        zq, zkv = sem("z_q_banks"), sem("z_kv_banks")
        qcopied, kvcopied, ucopied = sem("q_copied"), sem("kv_copied"), sem("u_copied")
        qsq, qred, qms_done, qrs_done, qscaled = (
            sem("qk_squares"), sem("qk_reduced"), sem("qk_ms"), sem("qk_rstd"), sem("qk_scaled"))
        qkn_done, carried, vstaged, tqk, kstaged, qstaged = (
            sem("qk_normalised"), sem("kv_carried"), sem("v_staged"), sem("qk_T"),
            sem("k_staged"), sem("q_staged"))
        logits, scaled, maxed, neg_maxed, exped, summed, rden_done, pnorm = (
            sem("logits"), sem("scaled"), sem("row_maxed"), sem("neg_maxed"), sem("exped"),
            sem("summed"), sem("rden_done"), sem("probs_normalised"))
        probs_T, probsT_copied, pv, attn_hi, attn_lo = (
            sem("probs_T"), sem("probsT_copied"), sem("pv"), sem("attn_hi"), sem("attn_lo"))
        level, edged, pooled, pool_hi, pool_lo, y_done, y_hi, y_lo, u_carried = (
            sem("pool_level"), sem("pool_edge"), sem("pooled"), sem("pool_hi"), sem("pool_lo"),
            sem("pool_y"), sem("pool_y_hi"), sem("pool_y_lo"), sem("u_carried"))
        tanhed, gated, glu_free, act_hi_done, act_lo_done = (
            sem("tanhed"), sem("gated"), sem("glu_banks_free"), sem("act_hi"), sem("act_lo"))
        down, down_added = sem("down_banks"), sem("down_added")
        p_landed, pT, pT_hi, pT_lo = sem("p_landed"), sem("p_T"), sem("p_T_hi"), sem("p_T_lo")
        pp, pp_copied = sem("proj_banks"), sem("proj_copied")
        gt, sig, ple_mul, ple_out = (
            sem("gate_banks"), sem("gate_tanh"), sem("ple_multiplied"), sem("ple_added"))
        out_stored, h_landed = sem("out_stored"), sem("h_landed")
        outp, out_added = sem("out_banks"), sem("out_added")

        CONSTS = 9 * 16
        HALF_SUMS = 3

        def iter_base(t):
            return Z_P + TILE_P * t

        def ffn_base(t, last):
            return iter_base(t) + OUT_P + (0 if last else Z_P)

        def norm2_no(t, last):
            return 3 * t + (1 if last else 2)

        def table(j, half):
            return bass.AP(scratch, j * PAIRS * P * BAND + P - 1 + half * P,
                           [[BAND - 1, P], [P * BAND, PAIRS], [1, P]])

        block = ctx.enter_context(nc.Block())

        @block.sync
        def _(sp):
            sp.dma_start(ident[:, :], identity).then_inc(consts, 16)

            def load(i, parity, halves):
                if not (isinstance(i, int) and i < 2):
                    sp.wait_ge(lo_done, i - 1)
                for half, src in enumerate(halves):
                    n = src.shape[1]
                    dst = raw[64 * half:64 * half + 64, parity, :].rearrange("p (k n) -> p k n", k=n)
                    sp.dma_start(dst, src).then_inc(landed[parity], 16)

            def rows(w, k0, k1, cols):
                v = w.rearrange("(k h p) n -> h p k n", h=2, p=64)
                return [v[half, :, k0:k1, cols] for half in range(2)]

            def load_z(at, first):
                for c in range(4):
                    if c == 2 and first:
                        load_bias()
                    load(at + c, c % 2, rows(w_in, 2 * c, 2 * c + 2, slice(0, QW)))
                for c in range(2):
                    load(at + 4 + c, c % 2, rows(w_in, 4 * c, 4 * c + 4, slice(QW, QW + 2 * KVW)))
                for g in range(NPOOL):
                    c0 = QW + 2 * KVW + g * P
                    load(at + 6 + g, g % 2, rows(w_in, 0, KC, slice(c0, c0 + P)))

            def load_out(at):
                heads = w_out[0:QW, :].rearrange("(j c p) n -> j p c n", j=2, p=HEAD_DIM)
                for e in range(2):
                    cols = slice(e * T, (e + 1) * T)
                    for r in range(4):
                        src = ([heads[j, :, 2 * r:2 * r + 2, cols] for j in range(2)] if r < 2
                               else rows(w_out, 2 * r, 2 * r + 2, cols))
                        load(at + 4 * e + r, r % 2, src)

            def load_gate_up(at, m):
                for n, w in enumerate((w_gate, w_up)):
                    v = w.rearrange("(k h p) (m n) -> h p k m n", h=2, p=64, n=P)
                    load(at + n, n, [v[half, :, :, m, :] for half in range(2)])

            def load_ffn(at):
                first, chunk0 = 0, 0
                for g, nk in enumerate(GROUPS):
                    if g < 2:
                        with sp.Fori(0, 2) as it:
                            for c in range(4):
                                load_gate_up(at + first + 2 * c + it * 8, it * 4 + (chunk0 + c))
                    else:
                        for c in range(nk):
                            load_gate_up(at + first + 2 * c, chunk0 + c)
                    for e in range(2):
                        for r in range(nk // 2):
                            n = e * (nk // 2) + r
                            load(at + first + 2 * nk + n, n % 2,
                                 rows(w_down, chunk0 + 2 * r, chunk0 + 2 * r + 2,
                                      slice(e * T, (e + 1) * T)))
                    first += 3 * nk
                    chunk0 += nk

            def load_ple(at):
                for e in range(2):
                    load(at + e, e, rows(w_ple_proj, 0, KP, slice(e * T, (e + 1) * T)))
                for e in range(2):
                    for r in range(4):
                        load(at + PROJ_P + 4 * e + r, r % 2,
                             rows(w_ple_gate, 2 * r, 2 * r + 2, slice(e * T, (e + 1) * T)))

            def load_bias():
                sp.wait_ge(band_built, NQ)
                sp.dma_start(scratch[:, :].rearrange("h (p s) -> p h s", s=BAND),
                             band[:, :, :]).then_inc(band_stored, 16)
                sp.wait_ge(band_stored, 16)
                for j in range(2):
                    sp.dma_start(bias[:, :, j, P:2 * P], table(j, 1)).then_inc(bias_landed, 16)

            load_z(0, True)
            with sp.Fori(0, LAST) as t:
                load_out(iter_base(t))
                load_z(iter_base(t) + OUT_P, False)
                load_ffn(ffn_base(t, False))
                load_ple(ffn_base(t, False) + FFN_P)
            load_out(iter_base(LAST))
            load_ffn(ffn_base(LAST, True))
            load_ple(ffn_base(LAST, True) + FFN_P)

        @block.gpsimd
        def _(pool):
            def alone(value):
                value = value if isinstance(value, int) else pool.to_reg(value)
                pool.wait_ge(half_ready, 1)
                return value

            def x_block(s, b):
                return x[s * T:(s + 1) * T, :] if b is None else \
                    x.rearrange("(s b p) d -> s b p d", b=NB, p=P)[s, b]

            def load_x(s, b, n_norm):
                if not (isinstance(n_norm, int) and n_norm == 0 and b < 2):
                    pool.wait_ge(nT, alone(8 * n_norm + 2 * b - 2))
                pool.dma_start(stage[:, b % 2, :], x_block(s, b)).then_inc(x_landed[b % 2], 16)

            def powers(n_norm, b):
                pool.wait_ge(ms_done, 4 * n_norm + b + 1)
                nc.gpsimd.tensor_tensor(rstd[:, b:b + 1], ms[:, b:b + 1], minus_half[:, :],
                                        ALU.pow).then_inc(rstd_done, 1)

            def squares_qk(s, b):
                pool.wait_ge(kvcopied, 4 * s + b + 1)
                pool.wait_ge(qcopied, 4 * s + b + 1)
                if not (isinstance(s, int) and s == 0 and b == 0):
                    pool.wait_ge(qred, 4 * s + b)
                nc.gpsimd.tensor_tensor(qk_sq[:, :], qkv[:, b, 0:QKW], qkv[:, b, 0:QKW],
                                        ALU.mult).then_inc(qsq, 1)

            def powers_qk(s, b):
                pool.wait_ge(qms_done, 4 * s + b + 1)
                nc.gpsimd.tensor_tensor(qrs[:, b, :], qms[:, b, :],
                                        minus_half[:, :].to_broadcast([P, NQ + NKV]),
                                        ALU.pow).then_inc(qrs_done, 1)

            def prep_qk(s):
                squares_qk(s, 0)
                squares_qk(s, 1)
                for b in range(NB):
                    powers_qk(s, b)
                    if b + 2 < NB:
                        squares_qk(s, b + 2)

            def normalise(n):
                pool.wait_ge(rden_done, n + 1)
                pool.wait_ge(probs_T, n)
                nc.gpsimd.tensor_tensor(probs[:, :, :], scores[:, :, :],
                                        rden[:, :].unsqueeze(2).to_broadcast([P, 2, 2 * P]),
                                        ALU.mult).then_inc(pnorm, 1)

            def pool_sums(s, g):
                levels = g + 1
                done = s * 10 + g * (g + 1) // 2
                src = u[:, g, :]
                pair = (sum_a, sum_b) if levels % 2 else (sum_b, sum_a)
                if g == 0:
                    pool.wait_ge(ucopied, 4 * s + 4)
                if not (isinstance(s, int) and s == 0 and g == 0):
                    pool.wait_ge(pool_lo, 4 * s + g)
                lead = 0
                for n in range(levels):
                    step = 1 << n
                    dst = pair[n % 2]
                    lo = lead + step
                    if n:
                        pool.wait_ge(level, done + n)
                    nc.gpsimd.tensor_tensor(dst[:, lo:], src[:, lo:],
                                            src[:, lo - step:CARRY + T - step],
                                            ALU.add).then_inc(level, 1)
                    src, lead = dst, lo

            def pool_rest(s, g):
                pool.wait_ge(pool_hi, 4 * s + g + 1)
                nc.gpsimd.tensor_tensor(mix_lo[:, 4 + g, :], sum_a[:, CARRY:],
                                        mix_hi[:, 4 + g, :].bitcast(F32),
                                        ALU.subtract).then_inc(pool_lo, 1)

            def carry_u(s):
                pool.wait_ge(pool_lo, alone(4 * s + 4))
                nc.gpsimd.tensor_copy(u[:, :, 0:CARRY], u[:, :, T:T + CARRY]).then_inc(u_carried, 1)

            def act_rest(n, k):
                pool.wait_ge(act_hi_done, n + 1)
                nc.gpsimd.tensor_tensor(wide_lo[:, k, :], act_b[:, :],
                                        wide_hi[:, k, :].bitcast(F32),
                                        ALU.subtract).then_inc(act_lo_done, 1)

            def out_rows(t, e, b):
                pool.wait_ge(ple_out, alone(8 * t + 4 * e + b + 1))
                dst = out.rearrange("(t b p) d -> t b p d", b=NB, p=P)[t, b, :, e * T:(e + 1) * T]
                pool.dma_start(dst, h[:, b, e * T:(e + 1) * T]).then_inc(out_stored, 16)

            def load_h(t):
                pool.wait_ge(out_stored, 128 * t)
                pool.wait_ge(band_stored, 16)
                for b in range(NB):
                    pool.dma_start(h[:, b, :], x_block(t, b)).then_inc(h_landed, 16)

            def out_section(t, norm1):
                if norm1:
                    load_x(t + 1, 0, 3 * t + 1)
                    load_x(t + 1, 1, 3 * t + 1)
                load_h(t)
                if norm1:
                    for b in range(NB):
                        powers(3 * t + 1, b)
                        if b < 2:
                            load_x(t + 1, b + 2, 3 * t + 1)

            def ffn_section(t, last):
                s = t + 1
                n0 = NCH * t
                for g in range(2):
                    with pool.Fori(0, 2) as it:
                        for beat in range(8):
                            if not last and 2 <= beat < 6:
                                normalise(16 * s + 8 * g + 4 * it + (beat - 2))
                            if beat % 2:
                                act_rest(n0 + 8 * g + 4 * it + beat // 2, 4 * it + beat // 2)
                if last:
                    pool.wait_ge(out_stored, alone(128 * t))
                else:
                    pool.wait_ge(vstaged, alone(4 * s + 4))
                for b in range(NB):
                    src = p.rearrange("(t b p) d -> t b p d", b=NB, p=P)[t, b]
                    pool.dma_start(p_rows[:, b, :], src).then_inc(p_landed, 16)
                for beat in range(12):
                    if not last and beat < 8:
                        (pool_rest if beat % 2 else pool_sums)(s, beat // 2)
                    if not last and beat == 8:
                        carry_u(s)
                    if beat % 2:
                        act_rest(n0 + 16 + beat // 2, beat // 2)

            def ple_section(t, last):
                for b in range(NB):
                    powers(norm2_no(t, last) + 1, b)
                for e in range(2):
                    for b in range(NB):
                        out_rows(t, e, b)

            nc.gpsimd.memset(minus_half[:, :], -0.5).then_inc(half_ready, 1)
            pool.wait_ge(half_ready, 1)
            load_x(0, 0, 0)
            load_x(0, 1, 0)
            for b in range(NB):
                powers(0, b)
                if b < 2:
                    load_x(0, b + 2, 0)
            prep_qk(0)
            for g in range(NPOOL):
                pool_sums(0, g)
                pool_rest(0, g)
            carry_u(0)
            for c in range(PAIRS):
                normalise(c)
            pool.wait_ge(band_stored, 16)
            for j in range(2):
                pool.dma_start(bias[:, :, j, 0:P], table(j, 0)).then_inc(bias_prev, 16)
            with pool.Fori(1, NB) as b:
                for c in range(PAIRS):
                    normalise(4 * b + c)

            with pool.Fori(0, LAST) as t:
                out_section(t, True)
                for b in range(NB):
                    powers(3 * t + 2, b)
                prep_qk(t + 1)
                ffn_section(t, False)
                ple_section(t, False)
            out_section(LAST, False)
            for b in range(NB):
                powers(3 * LAST + 1, b)
            ffn_section(LAST, True)
            ple_section(LAST, True)
            pool.wait_ge(out_stored, 128 * NT)

        @block.scalar
        def _(act):
            def bcast(v, n):
                return v.rearrange("(o n) -> o n", o=1).to_broadcast([P, n])

            act.dma_start(rel_sb[:, :], rel_bias).then_inc(consts, 16)
            act.dma_start(onehot_sb[:, :], onehot).then_inc(consts, 16)
            for n, g in enumerate((g_attn, g_ffn, g_ple)):
                act.dma_start(gains[:, n, :], bcast(g, D)).then_inc(consts, 16)
            act.dma_start(sink[:, :, :],
                          bass.AP(sinks.tensor, sinks.offset, [[0, P], [PAIRS, 2], [1, PAIRS]])
                          ).then_inc(consts, 16)
            act.dma_start(edge_sb[:, :, :],
                          bass.AP(edge.tensor, edge.offset, [[0, P], [CARRY, NPOOL], [1, CARRY]])
                          ).then_inc(consts, 16)
            act.dma_start(scale_sb[:, :], pool_scale.rearrange("(g p) -> p g", p=P),
                          allow_slow_non_contiguous=True).then_inc(consts, 16)
            act.dma_start(gqk[:, 0:QW].rearrange("p (h d) -> p h d", d=HEAD_DIM),
                          bass.AP(g_q.tensor, g_q.offset, [[0, P], [0, NQ], [1, HEAD_DIM]])
                          ).then_inc(wp_landed, 16)
            act.dma_start(gqk[:, QW:QKW].rearrange("p (h d) -> p h d", d=HEAD_DIM),
                          bass.AP(g_k.tensor, g_k.offset, [[0, P], [0, NKV], [1, HEAD_DIM]])
                          ).then_inc(wp_landed, 16)
            act.dma_start(act_a[:, :].rearrange("p (g d) -> p g d", g=NPOOL),
                          w_pool.rearrange("g c d -> c g d")).then_inc(wp_landed, 16)

            def split(i, parity):
                act.wait_ge(landed[parity], 16 * (i - parity) + 32)
                if not (isinstance(i, int) and i < 2):
                    act.wait_ge(panel_used, i - 1)
                nc.scalar.activation(w_hi[:, parity, :], raw[:, parity, :], ACT.Copy).then_inc(hi_done, 1)

            def sum_squares(n_norm, b, src):
                n = 4 * n_norm + b
                if not (isinstance(n_norm, int) and n == 0):
                    act.wait_ge(sumsq, n)
                if not (isinstance(n_norm, int) and n < 4):
                    act.wait_ge(ms_done, n - 3)
                nc.scalar.activation(squares[:, :], src, ACT.Square,
                                     accum_out=ss[:, b:b + 1]).then_inc(sumsq, 1)

            def norm_hi(n_norm, b, dst):
                for e in range(2):
                    n = 8 * n_norm + 2 * b + e
                    act.wait_ge(nT, n + 1)
                    src = bank[4 + (2 * b + e) % 4][:, :].rearrange("p (k t) -> p k t", k=4)
                    nc.scalar.activation(dst[:, 4 * e:4 * e + 4, b * P:(b + 1) * P], src,
                                         ACT.Copy).then_inc(nhi, 1)

            def copy_q(s, b, at):
                if b < HALF_SUMS:
                    act.wait_ge(zq, HALF_SUMS * s + b + 1)
                else:
                    act.wait_ge(panel_used, at + 4)
                nc.scalar.activation(qkv[:, b, 0:QW], bank[b][:, :], ACT.Copy).then_inc(qcopied, 1)

            def copy_u(s, g, at):
                act.wait_ge(panel_used, at + 7 + g)
                if g == 0:
                    act.wait_ge(u_carried, s + 1)
                nc.scalar.activation(u[:, g, CARRY:], bank[g][:, :], ACT.Copy).then_inc(ucopied, 1)

            def stage_q(s, b):
                act.wait_ge(tqk, 2 * (4 * s + b) + 1)
                act.wait_ge(logits, 16 * s + 4 * b)
                src = bank[7][:, :].rearrange("p (c q) -> p c q", c=PAIRS)
                nc.scalar.activation(qz[0:64, :, 0, :], src[0:64], ACT.Copy)
                nc.scalar.activation(qz[64:128, :, 1, :], src[64:128], ACT.Copy).then_inc(qstaged, 1)

            def exps(n, c):
                act.wait_ge(neg_maxed, n + 1)
                act.wait_ge(summed, n)
                for j in range(2):
                    nc.scalar.activation(scores[:, j, :], scores[:, j, :], ACT.Exp,
                                         bias=neg_max[:, j:j + 1], accum_out=row_sum[:, j:j + 1])
                for j in range(2):
                    last = nc.scalar.activation(sink_exp[:, j:j + 1], sink[:, j, c:c + 1], ACT.Exp,
                                                bias=neg_max[:, j:j + 1])
                last.then_inc(exped, 1)

            def copy_probsT(n):
                act.wait_ge(probs_T, n + 1)
                act.wait_ge(pv, n)
                nc.scalar.activation(probsT[:, :, :].rearrange("p a b -> p (a b)"), bank[5][:, :],
                                     ACT.Copy).then_inc(probsT_copied, 1)

            def attention_hi(n, b, c):
                act.wait_ge(pv, n + 1)
                for j in range(2):
                    rows = slice(64 * j, 64 * j + 64)
                    last = nc.scalar.activation(mix_hi[rows, c, bass.ts(b, P)],
                                                bank[6][rows, j * P:(j + 1) * P], ACT.Copy)
                last.then_inc(attn_hi, 1)

            def attention_beat(s, b, beat):
                n = 16 * s + 4 * b
                if beat == 1:
                    stage_q(s, b)
                if 4 <= beat:
                    copy_probsT(n + beat - 4)
                if 2 <= beat < 6:
                    exps(n + beat - 2, beat - 2)
                if 5 <= beat:
                    attention_hi(n + beat - 5, b, beat - 5)

            def pooled_hi(s, g):
                act.wait_ge(pooled, 4 * s + g + 1)
                nc.scalar.activation(mix_hi[:, 4 + g, :], sum_a[:, CARRY:], ACT.Copy).then_inc(pool_hi, 1)

            def pool_y_hi(s, g):
                act.wait_ge(y_done, 4 * s + g + 1)
                nc.scalar.activation(mix_hi[:, 4 + g, :], bank[4 + g][:, :], ACT.Copy,
                                     scale=scale_sb[:, g:g + 1]).then_inc(y_hi, 1)

            def tanh_gate(n, i, parity):
                act.wait_ge(panel_used, i + 1)
                act.wait_ge(glu_free, n + 2)
                nc.scalar.activation(act_a[:, :], bank[2 * parity][:, :], ACT.Tanh,
                                     scale=0.5).then_inc(tanhed, 1)

            def p_hi_part(t, kk):
                act.wait_ge(pT, 2 * t + kk + 1)
                nc.scalar.activation(p_hi[:, kk, :], bank[4 + kk][:, :], ACT.Copy).then_inc(pT_hi, 1)

            def ffn_section(t, last):
                at, s, n0 = ffn_base(t, last), t + 1, NCH * t
                first = 0
                for g in range(2):
                    with act.Fori(0, 2) as it:
                        for beat in range(8):
                            i = at + first + beat + it * 8
                            split(i + 1, (beat + 1) % 2)
                            if not last:
                                attention_beat(s, it + 2 * g, beat)
                            if beat % 2:
                                tanh_gate(n0 + 8 * g + 4 * it + beat // 2, i - 1, beat // 2 % 2)
                            if not last and beat == 7:
                                attention_hi(16 * s + 4 * (it + 2 * g) + 3, it + 2 * g, 3)
                    for n in range(8):
                        split(at + first + 16 + n + 1, (n + 1) % 2)
                    first += 24
                for beat in range(12):
                    i = at + first + beat
                    split(i + 1, (beat + 1) % 2)
                    if not last and beat % 2 and beat < 8:
                        pooled_hi(s, beat // 2)
                    if not last and beat % 2 and 2 < beat < 10:
                        pool_y_hi(s, beat // 2 - 1)
                    if beat >= 10:
                        p_hi_part(t, beat - 10)
                    if beat % 2:
                        tanh_gate(n0 + 16 + beat // 2, i - 1, beat // 2 % 2)
                for n in range(6):
                    split(at + first + 12 + n + 1, (n + 1) % 2)

            def copy_proj(t, e, b, i):
                if b < HALF_SUMS:
                    act.wait_ge(pp, 2 * HALF_SUMS * t + HALF_SUMS * e + b + 1)
                else:
                    act.wait_ge(panel_used, i + 1)
                nc.scalar.activation(proj[:, b, e * T:(e + 1) * T], bank[b][:, :],
                                     ACT.Copy).then_inc(pp_copied, 1)

            def ple_section(t, last):
                at = ffn_base(t, last) + FFN_P
                n3 = norm2_no(t, last) + 1
                split(at + 1, 1)
                for b in range(NB):
                    act.wait_ge(down_added, 24 * t + 20 + b + 1)
                    sum_squares(n3, b, h[:, b, :])
                for b in range(NB):
                    copy_proj(t, 0, b, at)
                split(at + 2, 0)
                norm_hi(n3, 0, hn_hi)
                for b in range(NB):
                    copy_proj(t, 1, b, at + 1)
                for b in range(1, NB):
                    norm_hi(n3, b, hn_hi)
                for e in range(2):
                    for r in range(4):
                        i = at + PROJ_P + 4 * e + r
                        if not (last and e == 1 and r == 3):
                            split(i + 1, (r + 1) % 2)
                    for b in range(NB):
                        if b < HALF_SUMS:
                            act.wait_ge(gt, 2 * HALF_SUMS * t + HALF_SUMS * e + b + 1)
                        else:
                            act.wait_ge(panel_used, i + 1)
                        n = 8 * t + 4 * e + b
                        buf = (act_a, act_b)[b % 2]
                        if e or b >= 2:
                            act.wait_ge(ple_out, n - 1)
                        nc.scalar.activation(buf[:, :], bank[4 * e + b][:, :], ACT.Tanh,
                                             scale=0.5).then_inc(sig, 1)

            def out_section(t, norm1):
                at = iter_base(t)
                n1 = 3 * t + 1
                for beat in range(8):
                    split(at + beat + 1, (beat + 1) % 2)
                    if norm1 and 1 <= beat < 5:
                        if beat == 1:
                            act.wait_ge(ple_mul, 8 * t)
                        norm_hi(n1, beat - 1, wide_hi)
                    if norm1 and beat < 4:
                        act.wait_ge(x_landed[beat % 2], 32 * (t + 1) + 16 * (beat // 2 + 1))
                        sum_squares(n1, beat, stage[:, beat % 2, :])

            def z_section(s, at, n2):
                for beat in range(10):
                    split(at + beat + 1, (beat + 1) % 2)
                    if n2 is not None and 2 <= beat < 4:
                        norm_hi(n2, beat - 2, hn_hi)
                    if n2 is not None and beat == 4:
                        norm_hi(n2, 2, hn_hi)
                        norm_hi(n2, 3, hn_hi)
                    if n2 is not None and beat < 4:
                        act.wait_ge(out_added, 8 * (s - 1) + 4 + beat + 1)
                        sum_squares(n2, beat, h[:, beat, :])
                    if beat == 4:
                        for b in range(NB):
                            copy_q(s, b, at)
                    if 7 <= beat:
                        copy_u(s, beat - 7, at)
                copy_u(s, 3, at)

            act.wait_ge(consts, CONSTS)
            act.wait_ge(wp_landed, 48)
            nc.scalar.activation(wp_hi[:, :, :].rearrange("p g d -> p (g d)"), act_a[:, :],
                                 ACT.Copy).then_inc(wp_hi_done, 1)
            split(0, 0)
            for b in range(NB):
                act.wait_ge(x_landed[b % 2], 16 * (b // 2 + 1))
                sum_squares(0, b, stage[:, b % 2, :])
                if b:
                    norm_hi(0, b - 1, wide_hi)
            norm_hi(0, 3, wide_hi)
            z_section(0, 0, None)
            for g in range(NPOOL):
                pooled_hi(0, g)
                if g:
                    pool_y_hi(0, g - 1)
            pool_y_hi(0, 3)
            for beat in range(8):
                attention_beat(0, 0, beat)
            attention_hi(3, 0, 3)
            with act.Fori(1, NB) as b:
                for beat in range(8):
                    attention_beat(0, b, beat)
                attention_hi(4 * b + 3, b, 3)

            with act.Fori(0, LAST) as t:
                out_section(t, True)
                z_section(t + 1, iter_base(t) + OUT_P, 3 * t + 2)
                ffn_section(t, False)
                ple_section(t, False)
            out_section(LAST, False)
            for b in range(NB):
                act.wait_ge(out_added, 8 * LAST + 4 + b + 1)
                sum_squares(3 * LAST + 1, b, h[:, b, :])
                if b:
                    norm_hi(3 * LAST + 1, b - 1, hn_hi)
            norm_hi(3 * LAST + 1, 3, hn_hi)
            ffn_section(LAST, True)
            ple_section(LAST, True)

        @block.vector
        def _(dve):
            def split(i, parity):
                dve.wait_ge(hi_done, i + 1)
                nc.vector.tensor_tensor(w_lo[:, parity, :], raw[:, parity, :],
                                        w_hi[:, parity, :].bitcast(F32),
                                        ALU.subtract).then_inc(lo_done, 1)

            def mean_square(n_norm, b):
                n = 4 * n_norm + b
                dve.wait_ge(sumsq, n + 1)
                if not (isinstance(n_norm, int) and n < 4):
                    dve.wait_ge(rstd_done, n - 3)
                nc.vector.tensor_scalar(out=ms[:, b:b + 1], in0=ss[:, b:b + 1], scalar1=1.0 / D,
                                        scalar2=EPS, op0=ALU.mult, op1=ALU.add).then_inc(ms_done, 1)

            def normalise(n_norm, b, src, gain):
                n = 4 * n_norm + b
                dve.wait_ge(rstd_done, n + 1)
                if not (isinstance(n_norm, int) and n < 2):
                    dve.wait_ge(nT, 2 * n - 2)
                nc.vector.scalar_tensor_tensor(out=stage[:, b % 2, :], in0=src, scalar=rstd[:, b:b + 1],
                                               in1=gains[:, gain, :], op0=ALU.mult,
                                               op1=ALU.mult).then_inc(xn_done, 1)

            def norm_lo(n_norm, b, hi, lo):
                for e in range(2):
                    dve.wait_ge(nhi, 8 * n_norm + 2 * b + e + 1)
                    src = bank[4 + (2 * b + e) % 4][:, :].rearrange("p (k t) -> p k t", k=4)
                    at = (slice(None), slice(4 * e, 4 * e + 4), slice(b * P, (b + 1) * P))
                    nc.vector.tensor_tensor(lo[at], src, hi[at].bitcast(F32),
                                            ALU.subtract).then_inc(nlo, 1)

            def copy_kv(s, b, at):
                if b < HALF_SUMS:
                    dve.wait_ge(zkv, HALF_SUMS * s + b + 1)
                else:
                    dve.wait_ge(panel_used, at + 6)
                nc.vector.tensor_copy(qkv[:, b, QW:], bank[4 + b][:, 0:2 * KVW]).then_inc(kvcopied, 1)

            def qk_mean(s, b):
                n = 4 * s + b
                heads = NQ + NKV
                dve.wait_ge(qsq, n + 1)
                nc.vector.tensor_reduce(out=qss[:, b, :],
                                        in_=qk_sq[:, :].rearrange("p (h d) -> p h d", h=heads),
                                        axis=AX.X, op=ALU.add).then_inc(qred, 1)
                dve.wait_ge(qred, n + 1)
                nc.vector.tensor_scalar(out=qms[:, b, :], in0=qss[:, b, :], scalar1=1.0 / HEAD_DIM,
                                        scalar2=EPS, op0=ALU.mult, op1=ALU.add).then_inc(qms_done, 1)

            def qk_scale(s, b):
                dve.wait_ge(qrs_done, 4 * s + b + 1)
                v = qkv[:, b, 0:QKW].rearrange("p (h d) -> p h d", d=HEAD_DIM)
                nc.vector.tensor_tensor(v, v, qrs[:, b, :].unsqueeze(2).to_broadcast([P, NQ + NKV, HEAD_DIM]),
                                        ALU.mult).then_inc(qscaled, 1)

            def qk_gain(s, b):
                n = 4 * s + b
                dve.wait_ge(qscaled, n + 1)
                dve.wait_ge(tqk, 2 * n)
                q = qkv[:, b, 0:QW].rearrange("p (j c d) -> p c j d", j=2, d=HEAD_DIM)
                nc.vector.tensor_tensor(qkn[:, 0:QW].rearrange("p (c j d) -> p c j d", j=2, d=HEAD_DIM), q,
                                        gqk[:, 0:QW].rearrange("p (c j d) -> p c j d", j=2, d=HEAD_DIM),
                                        ALU.mult)
                nc.vector.tensor_tensor(qkn[:, QW:QKW], qkv[:, b, QW:QKW], gqk[:, QW:QKW],
                                        ALU.mult).then_inc(qkn_done, 1)
                dve.wait_ge(logits, 4 * n)
                dve.wait_ge(kstaged, n)
                nc.vector.tensor_copy(kcat[:, 0:P], kcat[:, P:2 * P]).then_inc(carried, 1)
                dve.wait_ge(pv, 4 * n)
                dve.wait_ge(vstaged, n)
                nc.vector.tensor_copy(vcat[:, 0, :], vcat[:, 1, :]).then_inc(carried, 1)
                dve.wait_ge(carried, 2 * n + 2)
                nc.vector.tensor_copy(vcat[:, 1, :], qkv[:, b, QKW:]).then_inc(vstaged, 1)

            def stage_k(s, b):
                dve.wait_ge(tqk, 2 * (4 * s + b) + 2)
                nc.vector.tensor_copy(kcat[:, P:2 * P], bank[6][:, 0:P]).then_inc(kstaged, 1)

            def softmax_in(n, c):
                dve.wait_ge(logits, n + 1)
                dve.wait_ge(pnorm, n)
                nc.vector.scalar_tensor_tensor(out=scores[:, :, :].rearrange("p j k -> p (j k)"),
                                               in0=bank[4][:, :], scalar=HEAD_DIM ** -0.5,
                                               in1=bias[:, c, :, :].rearrange("p j k -> p (j k)"),
                                               op0=ALU.mult, op1=ALU.add).then_inc(scaled, 1)
                dve.wait_ge(scaled, n + 1)
                nc.vector.tensor_reduce(out=row_max[:, :], in_=scores[:, :, :], axis=AX.X,
                                        op=ALU.max).then_inc(maxed, 1)
                dve.wait_ge(maxed, n + 1)
                nc.vector.scalar_tensor_tensor(out=neg_max[:, :], in0=row_max[:, :], scalar=-1.0,
                                               in1=neg_sink[:, :, c], op0=ALU.mult,
                                               op1=ALU.min).then_inc(neg_maxed, 1)

            def softmax_den(n):
                dve.wait_ge(exped, n + 1)
                nc.vector.tensor_tensor(den[:, :], row_sum[:, :], sink_exp[:, :], ALU.add).then_inc(summed, 1)
                dve.wait_ge(summed, n + 1)
                nc.vector.reciprocal(rden[:, :], den[:, :]).then_inc(rden_done, 1)

            def attention_rest(n, b, c):
                dve.wait_ge(attn_hi, n + 1)
                for j in range(2):
                    rows = slice(64 * j, 64 * j + 64)
                    last = nc.vector.tensor_tensor(mix_lo[rows, c, bass.ts(b, P)],
                                                   bank[6][rows, j * P:(j + 1) * P],
                                                   mix_hi[rows, c, bass.ts(b, P)].bitcast(F32),
                                                   ALU.subtract)
                last.then_inc(attn_lo, 1)

            def attention_beat(s, b, beat):
                n = 16 * s + 4 * b
                if beat == 0:
                    qk_gain(s, b)
                if beat == 1:
                    stage_k(s, b)
                if 2 <= beat < 6:
                    softmax_in(n + beat - 2, beat - 2)
                if 5 <= beat:
                    attention_rest(n + beat - 5, b, beat - 5)
                if 2 <= beat < 6:
                    softmax_den(n + beat - 2)

            def pool_mean(s, g):
                dve.wait_ge(level, 10 * s + (g + 1) * (g + 2) // 2)
                if isinstance(s, int) and s == 0:
                    nc.vector.tensor_tensor(sum_a[:, CARRY:2 * CARRY], sum_a[:, CARRY:2 * CARRY],
                                            edge_sb[:, g, :], ALU.mult).then_inc(edged, 1)
                    dve.wait_ge(edged, g + 1)
                nc.vector.scalar_tensor_tensor(out=sum_a[:, CARRY:], in0=sum_a[:, CARRY:],
                                               scalar=1.0 / POOL_SIZES[g], in1=u[:, g, CARRY:],
                                               op0=ALU.mult, op1=ALU.subtract).then_inc(pooled, 1)

            def pool_y_rest(s, g):
                dve.wait_ge(y_hi, 4 * s + g + 1)
                nc.vector.scalar_tensor_tensor(out=mix_lo[:, 4 + g, :], in0=bank[4 + g][:, :],
                                               scalar=scale_sb[:, g:g + 1],
                                               in1=mix_hi[:, 4 + g, :].bitcast(F32), op0=ALU.mult,
                                               op1=ALU.subtract).then_inc(y_lo, 1)

            def gate_in(n, parity):
                dve.wait_ge(tanhed, n + 1)
                nc.vector.scalar_tensor_tensor(out=act_a[:, :], in0=act_a[:, :], scalar=1.0,
                                               in1=bank[2 * parity][:, :], op0=ALU.add,
                                               op1=ALU.mult).then_inc(gated, 1)

            def gate_up(n, i, parity, k):
                dve.wait_ge(panel_used, i + 1)
                dve.wait_ge(gated, n + 1)
                dve.wait_ge(act_lo_done, n)
                nc.vector.scalar_tensor_tensor(out=act_b[:, :], in0=act_a[:, :], scalar=0.5,
                                               in1=bank[2 * parity + 1][:, :], op0=ALU.mult,
                                               op1=ALU.mult).then_inc(glu_free, 1)
                dve.wait_ge(glu_free, n + 3)
                nc.vector.tensor_copy(wide_hi[:, k, :], act_b[:, :]).then_inc(act_hi_done, 1)

            def add_down(t, g, e, i):
                for b in range(NB):
                    if b < HALF_SUMS:
                        dve.wait_ge(down, 6 * HALF_SUMS * t + HALF_SUMS * (2 * g + e) + b + 1)
                    else:
                        dve.wait_ge(panel_used, i + 1)
                    v = h[:, b, e * T:(e + 1) * T]
                    nc.vector.tensor_tensor(v, bank[4 * e + b][:, :], v, ALU.add).then_inc(down_added, 1)

            def p_lo_part(t, kk):
                dve.wait_ge(pT_hi, 2 * t + kk + 1)
                nc.vector.tensor_tensor(p_lo[:, kk, :], bank[4 + kk][:, :], p_hi[:, kk, :].bitcast(F32),
                                        ALU.subtract).then_inc(pT_lo, 1)

            def ffn_section(t, last):
                at, s, n0 = ffn_base(t, last), t + 1, NCH * t
                first = 0
                for g, nk in enumerate(GROUPS):
                    if g < 2:
                        with dve.Fori(0, 2) as it:
                            for beat in range(8):
                                i = at + first + beat + it * 8
                                split(i + 1, (beat + 1) % 2)
                                if not last:
                                    attention_beat(s, it + 2 * g, beat)
                                if beat % 2:
                                    c = beat // 2
                                    n = n0 + 8 * g + c + 4 * it
                                    gate_in(n, c % 2)
                                    gate_up(n, i, c % 2, 4 * it + c)
                                if not last and beat == 7:
                                    attention_rest(16 * s + 4 * (it + 2 * g) + 3, it + 2 * g, 3)
                    else:
                        for beat in range(12):
                            i = at + first + beat
                            split(i + 1, (beat + 1) % 2)
                            if not last and beat % 2 and beat < 8:
                                pool_mean(s, beat // 2)
                            if not last and beat % 2 and 2 < beat < 10:
                                pool_y_rest(s, beat // 2 - 1)
                            if beat >= 10:
                                p_lo_part(t, beat - 10)
                            if beat % 2:
                                c = beat // 2
                                n = n0 + 16 + c
                                gate_in(n, c % 2)
                                gate_up(n, i, c % 2, c)
                    for n in range(nk):
                        i = at + first + 2 * nk + n
                        split(i + 1, (n + 1) % 2)
                        if n % (nk // 2) == nk // 2 - 1:
                            add_down(t, g, n // (nk // 2), i)
                    first += 3 * nk

            def ple_section(t, last):
                at = ffn_base(t, last) + FFN_P
                n3 = norm2_no(t, last) + 1
                split(at + 1, 1)
                for b in range(2):
                    mean_square(n3, b)
                    normalise(n3, b, h[:, b, :], 2)
                for b in range(2, NB):
                    mean_square(n3, b)
                split(at + 2, 0)
                norm_lo(n3, 0, hn_hi, hn_lo)
                normalise(n3, 2, h[:, 2, :], 2)
                norm_lo(n3, 1, hn_hi, hn_lo)
                normalise(n3, 3, h[:, 3, :], 2)
                norm_lo(n3, 2, hn_hi, hn_lo)
                norm_lo(n3, 3, hn_hi, hn_lo)
                for e in range(2):
                    for r in range(4):
                        if not (last and e == 1 and r == 3):
                            split(at + PROJ_P + 4 * e + r + 1, (r + 1) % 2)
                    for b in range(NB):
                        n = 8 * t + 4 * e + b
                        buf = (act_a, act_b)[b % 2]
                        dve.wait_ge(sig, n + 1)
                        dve.wait_ge(pp_copied, 8 * t + 4 * e + b + 1)
                        nc.vector.scalar_tensor_tensor(out=buf[:, :], in0=buf[:, :], scalar=1.0,
                                                       in1=proj[:, b, e * T:(e + 1) * T], op0=ALU.add,
                                                       op1=ALU.mult).then_inc(ple_mul, 1)
                        dve.wait_ge(ple_mul, n + 1)
                        v = h[:, b, e * T:(e + 1) * T]
                        nc.vector.scalar_tensor_tensor(out=v, in0=buf[:, :], scalar=0.5, in1=v,
                                                       op0=ALU.mult, op1=ALU.add).then_inc(ple_out, 1)

            def add_out(t, e, at):
                for b in range(NB):
                    if b < HALF_SUMS:
                        dve.wait_ge(outp, 2 * HALF_SUMS * t + HALF_SUMS * e + b + 1)
                    else:
                        dve.wait_ge(panel_used, at + 4 * e + 4)
                    v = h[:, b, e * T:(e + 1) * T]
                    nc.vector.tensor_tensor(v, bank[4 * e + b][:, :], v, ALU.add).then_inc(out_added, 1)

            def out_section(t, norm1):
                at = iter_base(t)
                n1 = 3 * t + 1
                for beat in range(8):
                    split(at + beat + 1, (beat + 1) % 2)
                    if norm1 and 1 <= beat < 5:
                        norm_lo(n1, beat - 1, wide_hi, wide_lo)
                    if norm1 and beat < 4:
                        mean_square(n1, beat)
                        normalise(n1, beat, stage[:, beat % 2, :], 0)
                    if beat == 3:
                        dve.wait_ge(h_landed, 64 * (t + 1))
                        add_out(t, 0, at)
                add_out(t, 1, at)

            def z_section(s, at, n2):
                for beat in range(10):
                    split(at + beat + 1, (beat + 1) % 2)
                    if n2 is not None and 2 <= beat < 4:
                        norm_lo(n2, beat - 2, hn_hi, hn_lo)
                    if n2 is not None and beat == 4:
                        norm_lo(n2, 2, hn_hi, hn_lo)
                        norm_lo(n2, 3, hn_hi, hn_lo)
                    if n2 is not None and beat < 4:
                        mean_square(n2, beat)
                        normalise(n2, beat, h[:, beat, :], 1)
                    if beat == 6:
                        for b in range(NB):
                            copy_kv(s, b, at)
                    if beat == 7:
                        qk_mean(s, 0)
                        qk_mean(s, 1)
                    if beat == 8:
                        qk_scale(s, 0)
                        qk_mean(s, 2)
                        qk_scale(s, 1)
                    if beat == 9:
                        qk_mean(s, 3)
                        qk_scale(s, 2)
                        qk_scale(s, 3)

            nc.vector.memset(bias[:, :, :, :], MASKED)
            nc.vector.memset(qz[:, :, :, :], 0.0)
            nc.vector.memset(kcat[:, :], 0.0)
            nc.vector.memset(vcat[:, :, :], 0.0)
            nc.vector.memset(rel_rows[N_BUCKETS:N_BUCKETS + 1, :, :], MASKED)
            nc.vector.memset(u[:, :, 0:CARRY], 0.0).then_inc(u_carried, 1)
            dve.wait_ge(consts, CONSTS)
            nc.vector.tensor_copy(rel_rows[0:N_BUCKETS, :, :],
                                  rel_sb[:, :].unsqueeze(2).to_broadcast([N_BUCKETS, NQ, P])
                                  ).then_inc(rel_ready, 1)
            nc.vector.tensor_scalar(out=neg_sink[:, :, :], in0=sink[:, :, :], scalar1=-1.0, scalar2=None,
                                    op0=ALU.mult).then_inc(glu_free, 2)
            dve.wait_ge(wp_hi_done, 1)
            nc.vector.tensor_tensor(wp_lo[:, :, :].rearrange("p g d -> p (g d)"), act_a[:, :],
                                    wp_hi[:, :, :].rearrange("p g d -> p (g d)").bitcast(F32),
                                    ALU.subtract).then_inc(wp_lo_done, 1)
            for n in range(NQ):
                dve.wait_ge(band_banks, n + 1)
                nc.vector.tensor_copy(band[:, n, :], bank[n][:, 0:BAND]).then_inc(band_built, 1)
            split(0, 0)
            for b in range(NB):
                mean_square(0, b)
                normalise(0, b, stage[:, b % 2, :], 0)
                if b:
                    norm_lo(0, b - 1, wide_hi, wide_lo)
            norm_lo(0, 3, wide_hi, wide_lo)
            z_section(0, 0, None)
            for g in range(NPOOL):
                pool_mean(0, g)
                if g:
                    pool_y_rest(0, g - 1)
            pool_y_rest(0, 3)
            dve.wait_ge(bias_landed, 32)
            for beat in range(8):
                attention_beat(0, 0, beat)
            attention_rest(3, 0, 3)
            dve.wait_ge(bias_prev, 32)
            with dve.Fori(1, NB) as b:
                for beat in range(8):
                    attention_beat(0, b, beat)
                attention_rest(4 * b + 3, b, 3)

            with dve.Fori(0, LAST) as t:
                out_section(t, True)
                z_section(t + 1, iter_base(t) + OUT_P, 3 * t + 2)
                ffn_section(t, False)
                ple_section(t, False)
            out_section(LAST, False)
            for b in range(NB):
                mean_square(3 * LAST + 1, b)
                normalise(3 * LAST + 1, b, h[:, b, :], 1)
                if b:
                    norm_lo(3 * LAST + 1, b - 1, hn_hi, hn_lo)
            norm_lo(3 * LAST + 1, 3, hn_hi, hn_lo)
            ffn_section(LAST, True)
            ple_section(LAST, True)

        @block.tensor
        def _(pe):
            mm = nc.tensor.matmul

            def alone(value):
                value = value if isinstance(value, int) else pe.to_reg(value)
                pe.wait_ge(rel_ready, 1)
                return value

            def rows_panel(i, parity, xh, xl, ks, banks, first, last, signal, free=None, width=T):
                pe.wait_ge(lo_done, i + 1)
                for b in range(NB):
                    if first and free is not None:
                        free(b)
                    out_ap = banks[b][:, 0:width]
                    tok = slice(b * P, (b + 1) * P)
                    for kk, k in enumerate(ks):
                        cols = slice(kk * width, (kk + 1) * width)
                        wh, wl = w_hi[:, parity, cols], w_lo[:, parity, cols]
                        mm(out_ap, xh[:, k, tok], wh, start=first and kk == 0, stop=False)
                        mm(out_ap, xh[:, k, tok], wl, start=False, stop=False)
                        ins = mm(out_ap, xl[:, k, tok], wh, start=False,
                                 stop=last and kk == len(ks) - 1)
                    if last and b < HALF_SUMS:
                        ins.then_inc(signal, 1)
                ins.then_inc(panel_used, 1)

            def features_panel(i, parity, xh, xl, dst):
                pe.wait_ge(lo_done, i + 1)
                for k in range(KC):
                    cols = slice(k * P, (k + 1) * P)
                    wh, wl = w_hi[:, parity, cols], w_lo[:, parity, cols]
                    mm(dst[:, :], wh, xh[:, k, :], start=k == 0, stop=False)
                    mm(dst[:, :], wh, xl[:, k, :], start=False, stop=False)
                    ins = mm(dst[:, :], wl, xh[:, k, :], start=False, stop=k == KC - 1)
                ins.then_inc(panel_used, 1)

            def transpose_norm(n_norm, b, free=None):
                pe.wait_ge(xn_done, 4 * n_norm + b + 1)
                for e in range(2):
                    if b < 2:
                        if free is not None:
                            free((2 * b + e) % 4)
                    else:
                        pe.wait_ge(nlo, 8 * n_norm + 2 * b + e - 3)
                    dst = bank[4 + (2 * b + e) % 4]
                    for k in range(4):
                        c = (4 * e + k) * P
                        ins = nc.tensor.transpose(dst[:, k * P:(k + 1) * P],
                                                  stage[:, b % 2, c:c + P], ident[:, :])
                    ins.then_inc(nT, 1)

            def transpose_qk(s, b):
                n = 4 * s + b
                pe.wait_ge(qkn_done, n + 1)
                pe.wait_ge(qstaged, n)
                for c in range(PAIRS):
                    ins = nc.tensor.transpose(bank[7][:, c * P:(c + 1) * P], qkn[:, c * P:(c + 1) * P],
                                              ident[:, :])
                ins.then_inc(tqk, 1)
                pe.wait_ge(attn_lo, 4 * n)
                nc.tensor.transpose(bank[6][:, 0:P], qkn[:, QW:QKW], ident[:, :]).then_inc(tqk, 1)

            def logits_of(s, b, c):
                n = 16 * s + 4 * b + c
                if c == 0:
                    pe.wait_ge(qstaged, 4 * s + b + 1)
                    pe.wait_ge(kstaged, 4 * s + b + 1)
                pe.wait_ge(scaled, n)
                for j in range(2):
                    ins = mm(bank[4][:, j * 2 * P:(j + 1) * 2 * P], qz[:, c, j, :], kcat[:, :],
                             start=True, stop=True)
                ins.then_inc(logits, 1)

            def transpose_probs(n):
                pe.wait_ge(pnorm, n + 1)
                pe.wait_ge(probsT_copied, n)
                for half in range(2):
                    for j in range(2):
                        c = (2 * half + j) * P
                        ins = nc.tensor.transpose(bank[5][:, c:c + P],
                                                  probs[:, j, half * P:(half + 1) * P], ident[:, :])
                ins.then_inc(probs_T, 1)

            def attend(n):
                pe.wait_ge(probsT_copied, n + 1)
                pe.wait_ge(attn_lo, n)
                for half in range(2):
                    ins = mm(bank[6][:, 0:2 * P], vcat[:, half, :], probsT[:, half, :],
                             start=half == 0, stop=half == 1)
                ins.then_inc(pv, 1)

            def attention_beat(s, b, beat):
                n = 16 * s + 4 * b
                if beat == 0:
                    transpose_qk(s, b)
                if 4 <= beat:
                    if beat == 4:
                        pe.wait_ge(vstaged, 4 * s + b + 1)
                    attend(n + beat - 4)
                if 3 <= beat < 7:
                    transpose_probs(n + beat - 3)
                if 1 <= beat < 5:
                    logits_of(s, b, beat - 1)

            def pool_y(s, g):
                pe.wait_ge(pool_lo, 4 * s + g + 1)
                mm(bank[4 + g][:, :], wp_hi[:, g, :], mix_hi[:, 4 + g, :], start=True, stop=False)
                mm(bank[4 + g][:, :], wp_hi[:, g, :], mix_lo[:, 4 + g, :], start=False, stop=False)
                mm(bank[4 + g][:, :], wp_lo[:, g, :], mix_hi[:, 4 + g, :], start=False,
                   stop=True).then_inc(y_done, 1)

            def transpose_p(t, kk):
                pe.wait_ge(p_landed, 64 * (t + 1))
                for b in range(NB):
                    ins = nc.tensor.transpose(bank[4 + kk][:, b * P:(b + 1) * P],
                                              p_rows[:, b, kk * P:(kk + 1) * P], ident[:, :])
                ins.then_inc(pT, 1)

            def attention_banks_free(s, blocks, b):
                if b == 0:
                    pe.wait_ge(scaled, 16 * s + 4 * blocks)
                elif b == 1:
                    pe.wait_ge(probsT_copied, 16 * s + 4 * blocks)
                elif b == 2:
                    pe.wait_ge(attn_lo, 16 * s + 4 * blocks)
                else:
                    pe.wait_ge(qstaged, 4 * s + blocks)

            def ffn_section(t, last):
                at, s, n0 = ffn_base(t, last), t + 1, NCH * t
                first = 0
                if last:
                    pe.wait_ge(out_added, alone(8 * t + 4))
                else:
                    pe.wait_ge(ucopied, alone(4 * s + 4))
                    pe.wait_ge(kvcopied, 4 * s + 4)
                pe.wait_ge(nlo, 8 * norm2_no(t, last) + 8)
                for g, nk in enumerate(GROUPS):
                    if g:
                        pe.wait_ge(down_added, alone(24 * t + 8 * g))
                    if g < 2:
                        with pe.Fori(0, 2) as it:
                            for beat in range(8):
                                c = beat // 2
                                n = n0 + 8 * g + c + 4 * it
                                if beat % 2 == 0:
                                    pe.wait_ge(glu_free, n + 1)
                                features_panel(at + first + beat + it * 8, beat % 2, hn_hi, hn_lo,
                                               bank[2 * (c % 2) + beat % 2])
                                if not last:
                                    attention_beat(s, it + 2 * g, beat)
                    else:
                        for beat in range(12):
                            c = beat // 2
                            if beat % 2 == 0:
                                pe.wait_ge(glu_free, n0 + 16 + c + 1)
                            features_panel(at + first + beat, beat % 2, hn_hi, hn_lo,
                                           bank[2 * (c % 2) + beat % 2])
                            if not last and beat % 2 == 0 and 2 <= beat <= 8:
                                pool_y(s, beat // 2 - 1)
                            if beat >= 9 and beat < 11:
                                if not last:
                                    pe.wait_ge(y_lo, 4 * s + beat - 9 + 1)
                                transpose_p(t, beat - 9)
                    done = n0 + 8 * g + nk
                    for e in range(2):
                        for r in range(nk // 2):
                            n = e * (nk // 2) + r
                            if e == 0:
                                pe.wait_ge(act_lo_done, n0 + 8 * g + 2 * r + 2)

                            def free(b):
                                if e == 0:
                                    pe.wait_ge(glu_free, done + 2 - (1 if b < 2 else 0))
                                elif g < 2 and not last:
                                    attention_banks_free(s, 2 * g + 2, b)
                                elif g == 2 and b < 2:
                                    pe.wait_ge(pT_lo, 2 * t + b + 1)
                                elif g == 2 and not last:
                                    pe.wait_ge(y_lo, 4 * s + b + 1)

                            rows_panel(at + first + 2 * nk + n, n % 2, wide_hi, wide_lo,
                                       (2 * r, 2 * r + 1), bank[4 * e:4 * e + 4], r == 0,
                                       r == nk // 2 - 1, down, free)
                    first += 3 * nk

            def ple_section(t, last):
                at = ffn_base(t, last) + FFN_P
                n3 = norm2_no(t, last) + 1
                pe.wait_ge(pT_lo, 2 * t + 2)
                for e in range(2):
                    def free(b):
                        pe.wait_ge(*((down_added, 24 * t + 16 + b + 1) if e == 0
                                     else (pp_copied, 8 * t + b + 1)))
                    rows_panel(at + e, e, p_hi, p_lo, range(KP), bank[0:4], True, True, pp, free)
                    if e == 0:
                        transpose_norm(n3, 0, lambda q: pe.wait_ge(down_added, 24 * t + 20 + q + 1))
                for b in range(1, NB):
                    transpose_norm(n3, b, lambda q: pe.wait_ge(down_added, 24 * t + 20 + q + 1))
                pe.wait_ge(nlo, 8 * n3 + 8)
                for e in range(2):
                    for r in range(4):
                        def free(b):
                            if e == 0:
                                pe.wait_ge(pp_copied, 8 * t + 4 + b + 1)
                        rows_panel(at + PROJ_P + 4 * e + r, r % 2, hn_hi, hn_lo, (2 * r, 2 * r + 1),
                                   bank[4 * e:4 * e + 4], r == 0, r == 3, gt, free)

            def out_section(t, norm1):
                at = iter_base(t)
                n1 = 3 * t + 1
                pe.wait_ge(attn_lo, 16 * t + 16)
                pe.wait_ge(y_lo, 4 * t + 4)
                pe.wait_ge(ucopied, 4)
                pe.wait_ge(sig, 8 * t)
                for e in range(2):
                    for r in range(4):
                        def free(b):
                            if e == 1 and norm1:
                                pe.wait_ge(nlo, 8 * n1 + 4 + b + 1)
                        rows_panel(at + 4 * e + r, r % 2, mix_hi, mix_lo, (2 * r, 2 * r + 1),
                                   bank[4 * e:4 * e + 4], r == 0, r == 3, outp, free)
                        if norm1 and e == 0:
                            transpose_norm(n1, r)

            def z_section(s, at, n2, n_before):
                for c in range(4):
                    def free(b):
                        if n2 is not None:
                            pe.wait_ge(out_added, 8 * (s - 1) + b + 1)
                    rows_panel(at + c, c % 2, wide_hi, wide_lo, (2 * c, 2 * c + 1), bank[0:4],
                               c == 0, c == 3, zq, free)
                    if n2 is not None:
                        for b in {1: (0,), 2: (1,), 3: (2, 3)}.get(c, ()):
                            transpose_norm(n2, b,
                                           lambda q: pe.wait_ge(out_added, 8 * (s - 1) + 4 + q + 1))
                for c in range(2):
                    def free(b):
                        pe.wait_ge(nlo, 8 * n_before + 4 + b + 1)
                    rows_panel(at + 4 + c, c % 2, wide_hi, wide_lo, range(4 * c, 4 * c + 4), bank[4:8],
                               c == 0, c == 1, zkv, free, width=2 * KVW)
                for g in range(NPOOL):
                    pe.wait_ge(qcopied, 4 * s + g + 1)
                    features_panel(at + 6 + g, g % 2, wide_hi, wide_lo, bank[g])

            pe.wait_ge(rel_ready, 1)
            for n in range(NQ):
                mm(bank[n][:, 0:3 * P], rel_rows[0:N_BUCKETS + 1, n, :], onehot_sb[:, :], start=True,
                   stop=True).then_inc(band_banks, 1)
            for b in range(NB):
                transpose_norm(0, b, lambda q: pe.wait_ge(band_built, 5 + q))
            pe.wait_ge(nlo, 8)
            pe.wait_ge(wp_lo_done, 1)
            z_section(0, 0, None, 0)
            for g in range(NPOOL):
                pe.wait_ge(kvcopied, g + 1)
                pool_y(0, g)
            pe.wait_ge(y_lo, 4)
            for beat in range(8):
                attention_beat(0, 0, beat)
            with pe.Fori(1, NB) as b:
                for beat in range(8):
                    attention_beat(0, b, beat)

            with pe.Fori(0, LAST) as t:
                out_section(t, True)
                z_section(t + 1, iter_base(t) + OUT_P, 3 * t + 2, 3 * t + 2)
                ffn_section(t, False)
                ple_section(t, False)
            out_section(LAST, False)
            for b in range(NB):
                transpose_norm(3 * LAST + 1, b,
                               lambda q: pe.wait_ge(out_added, 8 * LAST + 4 + q + 1))
            ffn_section(LAST, True)
            ple_section(LAST, True)


def bucket_of(dist):
    n = np.maximum(dist, 0)
    exact = N_BUCKETS // 2
    far = exact + (np.log(np.maximum(n, 1).astype(np.float64) / exact)
                   / np.log(MAX_DISTANCE / exact) * (N_BUCKETS - exact)).astype(np.int64)
    return np.where(n < exact, n, np.minimum(far, N_BUCKETS - 1))


def kernel(**inputs):
    import concourse.bacc as _bacc
    from concourse.bass_utils import run_bass_kernel_spmd as _run

    nc = _bacc.Bacc("TRN2", target_bir_lowering=False, num_devices=1, dynamic_dma_scratch_size=4096)
    names = ["x", "p", "w_in", "w_out", "g_attn_norm", "g_q", "g_k", "attn_sinks", "rel_bias", "w_pool",
             "pool_scale", "g_ffn_norm", "w_gate", "w_up", "w_down", "g_ple_norm", "w_ple_gate",
             "w_ple_proj"]
    arrays = {}
    for name in names:
        a = np.ascontiguousarray(inputs[name])
        if name == "p":
            a = a[0, 0]
        elif name != "rel_bias":
            a = a[0]
        arrays[name] = a
    dist = 2 * P - 1 - np.arange(3 * P)
    inside = (dist >= 0) & (dist < WINDOW)
    row = np.where(inside, bucket_of(dist), N_BUCKETS)
    arrays["onehot"] = (row[None, :] == np.arange(N_BUCKETS + 1)[:, None]).astype(np.float32)
    arrays["identity"] = np.eye(P, dtype=np.float32)
    arrays["edge"] = np.array([[w / min(i + 1, w) for i in range(CARRY)] for w in POOL_SIZES],
                              dtype=np.float32)
    aps = [nc.dram_tensor(f"in_{n}", a.shape, F32, kind="ExternalInput").ap()
           for n, a in arrays.items()]
    out = nc.dram_tensor("out_h", arrays["x"].shape, F32, kind="ExternalOutput").ap()
    by = dict(zip(arrays, aps))
    build(nc, by["x"], by["p"], by["w_in"], by["w_out"], by["g_attn_norm"], by["g_q"], by["g_k"],
          by["attn_sinks"], by["rel_bias"], by["w_pool"], by["pool_scale"], by["g_ffn_norm"],
          by["w_gate"], by["w_up"], by["w_down"], by["g_ple_norm"], by["w_ple_gate"],
          by["w_ple_proj"], by["identity"], by["onehot"], by["edge"], out)
    r = _run(nc, [{f"in_{n}": a for n, a in arrays.items()}], core_ids=[0])
    return r.results[0]["out_h"][None]
```

```python
import numpy as np
from contextlib import ExitStack

import concourse.bass as bass
from concourse import mybir

F32 = mybir.dt.float32
F32R = mybir.dt.float32r
BF16 = mybir.dt.bfloat16
ALU = mybir.AluOpType
ACT = mybir.ActivationFunctionType
AX = mybir.AxisListType

P = 128
HEAD_DIM = 64
NQ = 8
NKV = 2
PAIRS = NQ // NKV
QW = NQ * HEAD_DIM
KVW = NKV * HEAD_DIM
QKW = QW + KVW
WINDOW = 128
POOL_SIZES = (2, 4, 8, 16)
NPOOL = len(POOL_SIZES)
CARRY = 16
N_BUCKETS = 32
MAX_DISTANCE = 128
EPS = 1e-6
MASKED = -1e30
BAND = 3 * P - 1
T = 512
NB = T // P
PANEL = 1024
GROUPS = (8, 8, 6)
OUT_P, Z_P, FFN_P, PROJ_P, GATE_P = 8, 10, 3 * sum(GROUPS), 2, 8
TILE_P = OUT_P + Z_P + FFN_P + PROJ_P + GATE_P


def build(nc, x, p, w_in, w_out, g_attn, g_q, g_k, sinks, rel_bias, w_pool, pool_scale, g_ffn,
          w_gate, w_up, w_down, g_ple, w_ple_gate, w_ple_proj, identity, onehot, edge, out):
    S, D = x.shape
    KC = D // P
    NT = S // T
    LAST = NT - 1
    NCH = sum(GROUPS)
    KP = w_ple_proj.shape[0] // P
    scratch = nc.dram_tensor("band_rows", (NQ, P * BAND), F32, kind="Internal")

    ctx = ExitStack()
    with ctx:
        base = [(nc.sbuf_base + 63) // 64 * 64]

        def sb(name, shape, dt=F32, at=None):
            size = int(np.prod(shape[1:])) * (2 if dt == BF16 else 4)
            where = at if at is not None else base[0]
            if at is None:
                base[0] += (size + 31) // 32 * 32
            return nc.alloc_sbuf_tensor_at(name, list(shape), dt, offset=where)

        def sem(name):
            return ctx.enter_context(nc.semaphore(name))

        wide_at = base[0]
        wide_hi = sb("wide_hi", [P, KC, T], F32R)
        wide_lo = sb("wide_lo", [P, KC, T], F32R)
        proj = sb("proj", [P, NB, D], F32, at=wide_at)
        mix_hi = sb("mix_hi", [P, KC, T], F32R)
        mix_lo = sb("mix_lo", [P, KC, T], F32R)
        hn_at = base[0]
        hn_hi = sb("hn_hi", [P, KC, T], F32R)
        hn_lo = sb("hn_lo", [P, KC, T], F32R)
        h = sb("h", [P, NB, D])
        rel_rows = sb("rel_rows", [P, NQ, P], at=hn_at)
        band = sb("band", [P, NQ, BAND], at=hn_at + NQ * P * 4)
        stage = sb("stage", [P, 2, D])
        scores = stage[:, :, :].rearrange("p b (c j k) -> p (b c) j k", j=2, k=2 * P)
        squares = sb("squares", [P, D], BF16)
        gains = sb("gains", [P, 3, D])
        u = sb("u", [P, NPOOL, CARRY + T])
        sums = sb("sums", [P, 2 * (CARRY + T)])
        sum_a, sum_b = sums[:, 0:CARRY + T], sums[:, CARRY + T:2 * (CARRY + T)]
        qkv_at = base[0]
        qkv = sb("qkv", [P, NB, QKW + KVW])
        p_rows = qkv[:, :, :].rearrange("p b n -> p (b n)")[:, 0:NB * KP * P].rearrange(
            "p (b n) -> p b n", b=NB)
        p_hi = sb("p_hi", [P, KP, T], F32R, at=qkv_at + NB * KP * P * 4)
        p_lo = sb("p_lo", [P, KP, T], F32R, at=qkv_at + NB * KP * P * 4 + KP * T * 4)
        qk_sq = sums[:, 0:QKW]
        qkn = sb("qkn", [P, QKW])
        qz = sb("qz", [P, PAIRS, 2, P])
        kcat = sb("kcat", [P, 2 * P])
        vcat = sb("vcat", [P, 2, KVW])
        probsT = sb("probsT", [P, 2, 2, 2 * P])
        bias = sb("bias", [P, PAIRS, 2, 2 * P])
        gqk = sb("gqk", [P, QKW])
        wp_hi = sb("wp_hi", [P, NPOOL, P], F32R)
        wp_lo = sb("wp_lo", [P, NPOOL, P], F32R)
        act_a = sb("act_a", [P, T])
        act_b = sb("act_b", [P, T])
        raw = sb("raw", [P, 2, PANEL])
        w_hi = sb("w_hi", [P, 2, PANEL], F32R)
        w_lo = sb("w_lo", [P, 2, PANEL], F32R)
        ident = sb("ident", [P, P])
        onehot_sb = qkv[0:N_BUCKETS + 1, 0, 0:3 * P]
        rel_sb = sb("rel_sb", [N_BUCKETS, NQ])
        edge_sb = sb("edge_sb", [P, NPOOL, CARRY])
        scale_sb = sb("scale_sb", [P, NPOOL])
        sink = sb("sink", [P, 2, PAIRS])
        neg_sink = sb("neg_sink", [P, 2, PAIRS])
        ss = sb("ss", [P, NB])
        ms = sb("ms", [P, NB])
        rstd = sb("rstd", [P, NB])
        minus_half = sb("minus_half", [P, 1])
        qss = sb("qss", [P, NB, NQ + NKV])
        qms = sb("qms", [P, NB, NQ + NKV])
        qrs = sb("qrs", [P, NB, NQ + NKV])
        neg_max = sb("neg_max", [P, 2, 2])
        row_max = sb("row_max", [P, 2, 2])
        row_sum = sb("row_sum", [P, 2, 2])
        sink_exp = sb("sink_exp", [P, 2, 2])
        den = sb("den", [P, 2, 2])
        rden = sb("rden", [P, 2, 2])
        assert base[0] <= nc.sbuf_usable_end, (base[0], nc.sbuf_usable_end)

        bank = [ctx.enter_context(nc.psum_tensor(f"bank{i}", [P, T], F32)) for i in range(8)]

        consts = sem("consts_landed")
        band_built, band_stored, bias_landed = (
            sem("band_built"), sem("band_stored"), sem("bias_landed"))
        rel_ready, band_banks = sem("rel_ready"), sem("band_banks")
        half_ready, wp_landed, wp_hi_done, wp_lo_done = (
            sem("half_ready"), sem("wp_landed"), sem("wp_hi_done"), sem("wp_lo_done"))
        landed = [sem("panel_landed_even"), sem("panel_landed_odd")]
        hi_done, lo_done, panel_used = sem("panel_hi"), sem("panel_lo"), sem("panel_used")
        ident_landed, gain_landed = sem("ident_landed"), sem("norm1_gain_landed")
        first_x = [sem(f"first_x_block{b}") for b in range(NB)]
        masked, mask_row = sem("no_keys_masked"), sem("mask_row")
        x_landed = [sem("x_landed_even"), sem("x_landed_odd")]
        sumsq, ms_done, rstd_done, xn_done, nT = (
            sem("sumsq"), sem("mean_square"), sem("rstd_done"), sem("normalised"), sem("norm_T"))
        nhi, nlo = sem("norm_hi"), sem("norm_lo")
        zq, zkv = sem("z_q_banks"), sem("z_kv_banks")
        qcopied, kvcopied, ucopied = sem("q_copied"), sem("kv_copied"), sem("u_copied")
        qsq, qred, qms_done, qrs_done, qscaled = (
            sem("qk_squares"), sem("qk_reduced"), sem("qk_ms"), sem("qk_rstd"), sem("qk_scaled"))
        qkn_done, kcarried, vcarried, vstaged, tqk, kstaged, qstaged = (
            sem("qk_normalised"), sem("k_carried"), sem("v_carried"), sem("v_staged"), sem("qk_T"),
            sem("k_staged"), sem("q_staged"))
        logits, scaled, maxed, neg_maxed, exped, summed, rden_done, pnorm = (
            sem("logits"), sem("scaled"), sem("row_maxed"), sem("neg_maxed"), sem("exped"),
            sem("summed"), sem("rden_done"), sem("probs_normalised"))
        probs_T, probsT_copied, pv, attn_hi, attn_lo = (
            sem("probs_T"), sem("probsT_copied"), sem("pv"), sem("attn_hi"), sem("attn_lo"))
        level, edged, pooled, pool_hi, pool_lo, y_done, y_hi, y_lo, u_carried = (
            sem("pool_level"), sem("pool_edge"), sem("pooled"), sem("pool_hi"), sem("pool_lo"),
            sem("pool_y"), sem("pool_y_hi"), sem("pool_y_lo"), sem("u_carried"))
        tanhed, gated, glu_free, act_hi_done, act_lo_done = (
            sem("tanhed"), sem("gated"), sem("glu_banks_free"), sem("act_hi"), sem("act_lo"))
        down, down_added = sem("down_banks"), sem("down_added")
        p_landed, pT, pT_hi, pT_lo = sem("p_landed"), sem("p_T"), sem("p_T_hi"), sem("p_T_lo")
        pp, pp_copied = sem("proj_banks"), sem("proj_copied")
        gt, sig, ple_mul, ple_out = (
            sem("gate_banks"), sem("gate_tanh"), sem("ple_multiplied"), sem("ple_added"))
        out_stored, h_landed = sem("out_stored"), sem("h_landed")
        outp, out_added = sem("out_banks"), sem("out_added")

        CONSTS = 5 * 16
        HALF_SUMS = 3

        def iter_base(t):
            return Z_P + TILE_P * t

        def ffn_base(t, last):
            return iter_base(t) + OUT_P + (0 if last else Z_P)

        def norm2_no(t, last):
            return 3 * t + (1 if last else 2)

        def table(j):
            return bass.AP(scratch, j * PAIRS * P * BAND + P - 1,
                           [[BAND - 1, P], [P * BAND, PAIRS], [1, 2 * P]])

        LAG_NORM, LAG_T, LAG_PV = 1, 2, 3

        def unit_at(b, j, lag, flowing):
            c = j - lag
            if 0 <= c < PAIRS:
                return None if isinstance(b, int) and b == NB else (b, c)
            if c < 0 and flowing and not (isinstance(b, int) and b == 0):
                return b - 1, c + PAIRS
            return None

        def k_bank(s):
            return 0 if isinstance(s, int) and s == 0 else 6

        def no_less(value):
            return max(value, 0) if isinstance(value, int) else value

        def x_block(s, b):
            return x.rearrange("(s b p) d -> s b p d", b=NB, p=P)[s, b]

        block = ctx.enter_context(nc.Block())

        @block.sync
        def _(sp):
            for b in range(NB):
                sp.dma_start(h[:, b, :], x_block(0, b)).then_inc(first_x[b], 16)
                if b == 0:
                    sp.dma_start(ident[:, :], identity).then_inc(ident_landed, 16)

            def load(i, parity, halves):
                if not (isinstance(i, int) and i < 2):
                    sp.wait_ge(lo_done, i - 1)
                for half, src in enumerate(halves):
                    n = src.shape[1]
                    dst = raw[64 * half:64 * half + 64, parity, :].rearrange("p (k n) -> p k n", k=n)
                    sp.dma_start(dst, src).then_inc(landed[parity], 16)

            def rows(w, k0, k1, cols):
                v = w.rearrange("(k h p) n -> h p k n", h=2, p=64)
                return [v[half, :, k0:k1, cols] for half in range(2)]

            def load_z(at, first):
                for c in range(4):
                    load(at + c, c % 2, rows(w_in, 2 * c, 2 * c + 2, slice(0, QW)))
                for c in range(2):
                    load(at + 4 + c, c % 2, rows(w_in, 4 * c, 4 * c + 4, slice(QW, QW + 2 * KVW)))
                for g in range(NPOOL):
                    if g == 1 and first:
                        load_bias()
                    c0 = QW + 2 * KVW + g * P
                    load(at + 6 + g, g % 2, rows(w_in, 0, KC, slice(c0, c0 + P)))

            def load_x(s, b, n_norm):
                sp.wait_ge(nT, 8 * n_norm + 2 * b - 2)
                sp.dma_start(stage[:, b % 2, :], x_block(s, b)).then_inc(x_landed[b % 2], 16)

            def load_out(at, t, norm1):
                heads = w_out[0:QW, :].rearrange("(j c p) n -> j p c n", j=2, p=HEAD_DIM)
                for e in range(2):
                    cols = slice(e * T, (e + 1) * T)
                    for r in range(4):
                        src = ([heads[j, :, 2 * r:2 * r + 2, cols] for j in range(2)] if r < 2
                               else rows(w_out, 2 * r, 2 * r + 2, cols))
                        load(at + 4 * e + r, r % 2, src)
                        if norm1 and e == 0 and r == 1:
                            sp.wait_ge(probs_T, 16 * t + 16)
                            load_x(t + 1, 0, 3 * t + 1)
                            load_x(t + 1, 1, 3 * t + 1)
                        if norm1 and e == 1 and r == 1:
                            load_x(t + 1, 2, 3 * t + 1)
                            load_x(t + 1, 3, 3 * t + 1)

            def load_gate_up(at, m):
                for n, w in enumerate((w_gate, w_up)):
                    v = w.rearrange("(k h p) (m n) -> h p k m n", h=2, p=64, n=P)
                    load(at + n, n, [v[half, :, :, m, :] for half in range(2)])

            def load_ffn(at):
                first, chunk0 = 0, 0
                for g, nk in enumerate(GROUPS):
                    if g < 2:
                        with sp.Fori(0, 2) as it:
                            for c in range(4):
                                load_gate_up(at + first + 2 * c + it * 8, it * 4 + (chunk0 + c))
                    else:
                        for c in range(nk):
                            load_gate_up(at + first + 2 * c, chunk0 + c)
                    for e in range(2):
                        for r in range(nk // 2):
                            n = e * (nk // 2) + r
                            load(at + first + 2 * nk + n, n % 2,
                                 rows(w_down, chunk0 + 2 * r, chunk0 + 2 * r + 2,
                                      slice(e * T, (e + 1) * T)))
                    first += 3 * nk
                    chunk0 += nk

            def load_ple(at):
                for e in range(2):
                    load(at + e, e, rows(w_ple_proj, 0, KP, slice(e * T, (e + 1) * T)))
                for e in range(2):
                    for r in range(4):
                        load(at + PROJ_P + 4 * e + r, r % 2,
                             rows(w_ple_gate, 2 * r, 2 * r + 2, slice(e * T, (e + 1) * T)))

            def load_bias():
                sp.wait_ge(band_built, NQ)
                sp.dma_start(scratch[:, :].rearrange("h (p s) -> p h s", s=BAND),
                             band[:, :, :]).then_inc(band_stored, 16)
                sp.wait_ge(band_stored, 16)
                for j in range(2):
                    sp.dma_start(bias[:, :, j, :], table(j)).then_inc(bias_landed, 16)

            load_z(0, True)
            with sp.Fori(0, LAST) as t:
                load_out(iter_base(t), t, True)
                load_z(iter_base(t) + OUT_P, False)
                load_ffn(ffn_base(t, False))
                load_ple(ffn_base(t, False) + FFN_P)
            load_out(iter_base(LAST), LAST, False)
            load_ffn(ffn_base(LAST, True))
            load_ple(ffn_base(LAST, True) + FFN_P)

        @block.gpsimd
        def _(pool):
            def alone(value):
                value = value if isinstance(value, int) else pool.to_reg(value)
                pool.wait_ge(half_ready, 1)
                return value

            def powers(n_norm, b):
                n = 4 * n_norm + b
                pool.wait_ge(sumsq, alone(n + 1))
                nc.gpsimd.tensor_scalar(out=ms[:, b:b + 1], in0=ss[:, b:b + 1], scalar1=1.0 / D,
                                        scalar2=EPS, op0=ALU.mult, op1=ALU.add).then_inc(ms_done, 1)
                pool.wait_ge(ms_done, n + 1)
                if not (isinstance(n_norm, int) and n < 4):
                    pool.wait_ge(xn_done, n - 3)
                nc.gpsimd.tensor_tensor(rstd[:, b:b + 1], ms[:, b:b + 1], minus_half[:, :],
                                        ALU.pow).then_inc(rstd_done, 1)

            def squares_qk(s, b):
                pool.wait_ge(kvcopied, 4 * s + b + 1)
                pool.wait_ge(qcopied, 4 * s + b + 1)
                if not (isinstance(s, int) and s == 0 and b == 0):
                    pool.wait_ge(qred, 4 * s + b)
                nc.gpsimd.tensor_tensor(qk_sq[:, :], qkv[:, b, 0:QKW], qkv[:, b, 0:QKW],
                                        ALU.mult).then_inc(qsq, 1)

            def powers_qk(s, b):
                pool.wait_ge(qred, alone(4 * s + b + 1))
                nc.gpsimd.tensor_scalar(out=qms[:, b, :], in0=qss[:, b, :], scalar1=1.0 / HEAD_DIM,
                                        scalar2=EPS, op0=ALU.mult, op1=ALU.add).then_inc(qms_done, 1)
                pool.wait_ge(qms_done, 4 * s + b + 1)
                nc.gpsimd.tensor_tensor(qrs[:, b, :], qms[:, b, :],
                                        minus_half[:, :].to_broadcast([P, NQ + NKV]),
                                        ALU.pow).then_inc(qrs_done, 1)

            def prep_qk(s):
                squares_qk(s, 0)
                squares_qk(s, 1)
                for b in range(NB):
                    powers_qk(s, b)
                    if b + 2 < NB:
                        squares_qk(s, b + 2)

            def normalise(n, c):
                pool.wait_ge(rden_done, n + 1)
                nc.gpsimd.tensor_tensor(scores[:, c, :, :], scores[:, c, :, :],
                                        rden[:, c % 2, :].unsqueeze(2).to_broadcast([P, 2, 2 * P]),
                                        ALU.mult).then_inc(pnorm, 1)

            def attention_step(s, b, j, flowing):
                at = unit_at(b, j, LAG_NORM, flowing)
                if at:
                    normalise(16 * s + 4 * at[0] + at[1], at[1])

            def pool_rest(s, g):
                pool.wait_ge(pool_hi, 4 * s + g + 1)
                nc.gpsimd.tensor_tensor(mix_lo[:, 4 + g, :], sum_a[:, CARRY:],
                                        mix_hi[:, 4 + g, :].bitcast(F32),
                                        ALU.subtract).then_inc(pool_lo, 1)

            def carry_u(s):
                pool.wait_ge(pool_lo, alone(4 * s + 4))
                nc.gpsimd.tensor_copy(u[:, :, 0:CARRY], u[:, :, T:T + CARRY]).then_inc(u_carried, 1)

            def act_rest(n, k):
                pool.wait_ge(act_hi_done, n + 1)
                nc.gpsimd.tensor_tensor(wide_lo[:, k, :], act_b[:, :],
                                        wide_hi[:, k, :].bitcast(F32),
                                        ALU.subtract).then_inc(act_lo_done, 1)

            def out_rows(t, e, b):
                pool.wait_ge(ple_out, alone(8 * t + 4 * e + b + 1))
                dst = out.rearrange("(t b p) d -> t b p d", b=NB, p=P)[t, b, :, e * T:(e + 1) * T]
                pool.dma_start(dst, h[:, b, e * T:(e + 1) * T]).then_inc(out_stored, 16)

            def load_h(t):
                pool.wait_ge(xn_done, 4)
                pool.wait_ge(out_stored, alone(128 * t + 32))
                for b in range(NB):
                    pool.dma_start(h[:, b, :], x_block(t, b)).then_inc(h_landed, 16)

            def out_section(t, norm1):
                if norm1:
                    powers(3 * t + 1, 0)
                    powers(3 * t + 1, 1)
                load_h(t)
                if norm1:
                    powers(3 * t + 1, 2)
                    powers(3 * t + 1, 3)

            def ffn_section(t, last):
                s = t + 1
                n0 = NCH * t
                for g in range(2):
                    with pool.Fori(0, 2) as it:
                        for beat in range(8):
                            if not last and beat:
                                attention_step(s, it + 2 * g, beat - 1, False)
                            if beat % 2:
                                act_rest(n0 + 8 * g + 4 * it + beat // 2, 4 * it + beat // 2)
                if last:
                    pool.wait_ge(pT, alone(2 * t))
                else:
                    pool.wait_ge(vstaged, alone(4 * s + 4))
                for b in range(NB):
                    src = p.rearrange("(t b p) d -> t b p d", b=NB, p=P)[t, b]
                    pool.dma_start(p_rows[:, b, :], src).then_inc(p_landed, 16)
                for beat in range(12):
                    if not last and beat % 2 and beat < 8:
                        pool_rest(s, beat // 2)
                    if not last and beat == 8:
                        carry_u(s)
                    if beat % 2:
                        act_rest(n0 + 16 + beat // 2, beat // 2)

            def ple_section(t, last):
                for b in range(NB):
                    powers(norm2_no(t, last) + 1, b)
                for e in range(2):
                    for b in range(NB):
                        out_rows(t, e, b)

            nc.gpsimd.memset(minus_half[:, :], -0.5).then_inc(half_ready, 1)
            pool.wait_ge(half_ready, 1)
            nc.gpsimd.memset(qz[:, :, :, :], 0.0).then_inc(sig, 8)
            nc.gpsimd.memset(kcat[:, :], 0.0).then_inc(ple_mul, 1)
            nc.gpsimd.memset(vcat[:, :, :], 0.0).then_inc(act_lo_done, 1)
            pool.wait_ge(act_lo_done, 1)
            nc.gpsimd.memset(rel_rows[N_BUCKETS:N_BUCKETS + 1, :, :], MASKED).then_inc(mask_row, 1)
            pool.wait_ge(mask_row, 1)
            nc.gpsimd.memset(u[:, :, 0:CARRY], 0.0).then_inc(u_carried, 1)
            pool.dma_start(sink[:, :, :],
                           bass.AP(sinks.tensor, sinks.offset, [[0, P], [PAIRS, 2], [1, PAIRS]])
                           ).then_inc(out_stored, 16)
            pool.dma_start(edge_sb[:, :, :],
                           bass.AP(edge.tensor, edge.offset, [[0, P], [CARRY, NPOOL], [1, CARRY]])
                           ).then_inc(out_stored, 16)
            for b in range(NB):
                powers(0, b)
            prep_qk(0)
            for j in range(PAIRS):
                attention_step(0, 0, j, True)
                pool_rest(0, j)
            carry_u(0)
            with pool.Fori(1, NB) as b:
                for j in range(PAIRS):
                    attention_step(0, b, j, True)
            for g in range(NPOOL):
                attention_step(0, NB, g, True)

            with pool.Fori(0, LAST) as t:
                out_section(t, True)
                for b in range(NB):
                    powers(3 * t + 2, b)
                prep_qk(t + 1)
                ffn_section(t, False)
                ple_section(t, False)
            out_section(LAST, False)
            for b in range(NB):
                powers(3 * LAST + 1, b)
            ffn_section(LAST, True)
            ple_section(LAST, True)
            pool.wait_ge(out_stored, 128 * NT + 32)

        @block.scalar
        def _(act):
            def bcast(v, n):
                return v.rearrange("(o n) -> o n", o=1).to_broadcast([P, n])

            act.dma_start(gains[:, 0, :], bcast(g_attn, D)).then_inc(gain_landed, 16)

            def split(i, parity):
                act.wait_ge(landed[parity], 16 * (i - parity) + 32)
                if not (isinstance(i, int) and i < 2):
                    act.wait_ge(panel_used, i - 1)
                nc.scalar.activation(w_hi[:, parity, :], raw[:, parity, :], ACT.Copy).then_inc(hi_done, 1)

            def sum_squares(n_norm, b, src):
                n = 4 * n_norm + b
                if not (isinstance(n_norm, int) and n == 0):
                    act.wait_ge(sumsq, n)
                if not (isinstance(n_norm, int) and n < 4):
                    act.wait_ge(ms_done, n - 3)
                nc.scalar.activation(squares[:, :], src, ACT.Square,
                                     accum_out=ss[:, b:b + 1]).then_inc(sumsq, 1)

            def norm_hi(n_norm, b, dst):
                for e in range(2):
                    n = 8 * n_norm + 2 * b + e
                    act.wait_ge(nT, n + 1)
                    src = bank[4 + (2 * b + e) % 4][:, :].rearrange("p (k t) -> p k t", k=4)
                    nc.scalar.activation(dst[:, 4 * e:4 * e + 4, b * P:(b + 1) * P], src,
                                         ACT.Copy).then_inc(nhi, 1)

            def copy_q(s, b, at):
                if isinstance(s, int) and b == 0:
                    act.wait_ge(band_banks, NQ)
                if b < HALF_SUMS:
                    act.wait_ge(zq, HALF_SUMS * s + b + 1)
                else:
                    act.wait_ge(panel_used, at + 4)
                nc.scalar.activation(qkv[:, b, 0:QW], bank[b][:, :], ACT.Copy).then_inc(qcopied, 1)

            def copy_u(s, g, at):
                act.wait_ge(panel_used, at + 7 + g)
                if g == 0:
                    act.wait_ge(u_carried, s + 1)
                nc.scalar.activation(u[:, g, CARRY:], bank[g][:, :], ACT.Copy).then_inc(ucopied, 1)

            def stage_q(s, b):
                act.wait_ge(tqk, 2 * (4 * s + b) + 1)
                act.wait_ge(logits, 16 * s + 4 * b)
                src = bank[7][:, :].rearrange("p (c q) -> p c q", c=PAIRS)
                nc.scalar.activation(qz[0:64, :, 0, :], src[0:64], ACT.Copy)
                nc.scalar.activation(qz[64:128, :, 1, :], src[64:128], ACT.Copy).then_inc(qstaged, 1)

            def exps(n, c):
                i = c % 2
                act.wait_ge(neg_maxed, n + 1)
                act.wait_ge(summed, no_less(n - 1))
                for j in range(2):
                    nc.scalar.activation(scores[:, c, j, :], scores[:, c, j, :], ACT.Exp,
                                         bias=neg_max[:, i, j:j + 1], accum_out=row_sum[:, i, j:j + 1])
                for j in range(2):
                    last = nc.scalar.activation(sink_exp[:, i, j:j + 1], sink[:, j, c:c + 1], ACT.Exp,
                                                bias=neg_max[:, i, j:j + 1])
                last.then_inc(exped, 1)

            def copy_probsT(n, c):
                act.wait_ge(probs_T, n + 1)
                act.wait_ge(pv, no_less(n - 1))
                nc.scalar.activation(probsT[:, c % 2, :, :].rearrange("p a b -> p (a b)"), bank[5][:, :],
                                     ACT.Copy).then_inc(probsT_copied, 1)

            def attention_hi(n, b, c):
                act.wait_ge(pv, n + 1)
                for j in range(2):
                    rows = slice(64 * j, 64 * j + 64)
                    last = nc.scalar.activation(mix_hi[rows, c, bass.ts(b, P)],
                                                bank[6][rows, j * P:(j + 1) * P], ACT.Copy)
                last.then_inc(attn_hi, 1)

            def attention_step(s, b, j, flowing):
                at = unit_at(b, j, LAG_PV, flowing)
                if at:
                    attention_hi(16 * s + 4 * at[0] + at[1], *at)
                at = unit_at(b, j, LAG_T, flowing)
                if at:
                    copy_probsT(16 * s + 4 * at[0] + at[1], at[1])
                at = unit_at(b, j, 0, flowing)
                if at:
                    exps(16 * s + 4 * at[0] + at[1], at[1])

            def pooled_hi(s, g):
                act.wait_ge(pooled, 4 * s + g + 1)
                nc.scalar.activation(mix_hi[:, 4 + g, :], sum_a[:, CARRY:], ACT.Copy).then_inc(pool_hi, 1)

            def pool_y_hi(s, g, banks):
                act.wait_ge(y_done, 4 * s + g + 1)
                nc.scalar.activation(mix_hi[:, 4 + g, :], bank[banks + g][:, :], ACT.Copy,
                                     scale=scale_sb[:, g:g + 1]).then_inc(y_hi, 1)

            def tanh_gate(n, i, parity):
                act.wait_ge(panel_used, i + 1)
                act.wait_ge(glu_free, n + 2)
                nc.scalar.activation(act_a[:, :], bank[2 * parity][:, :], ACT.Tanh,
                                     scale=0.5).then_inc(tanhed, 1)

            def p_hi_part(t, kk):
                act.wait_ge(pT, 2 * t + kk + 1)
                nc.scalar.activation(p_hi[:, kk, :], bank[4 + kk][:, :], ACT.Copy).then_inc(pT_hi, 1)

            def ffn_section(t, last):
                at, s, n0 = ffn_base(t, last), t + 1, NCH * t
                first = 0
                for g in range(2):
                    with act.Fori(0, 2) as it:
                        for beat in range(8):
                            i = at + first + beat + it * 8
                            split(i + 1, (beat + 1) % 2)
                            if not last and beat == 0:
                                stage_q(s, it + 2 * g)
                            if not last and beat:
                                attention_step(s, it + 2 * g, beat - 1, False)
                            if beat % 2:
                                tanh_gate(n0 + 8 * g + 4 * it + beat // 2, i - 1, beat // 2 % 2)
                    for n in range(8):
                        split(at + first + 16 + n + 1, (n + 1) % 2)
                    first += 24
                for beat in range(12):
                    i = at + first + beat
                    split(i + 1, (beat + 1) % 2)
                    if not last and beat % 2 and beat < 8:
                        pooled_hi(s, beat // 2)
                    if not last and beat % 2 and 2 < beat < 10:
                        pool_y_hi(s, beat // 2 - 1, 4)
                    if beat >= 10:
                        p_hi_part(t, beat - 10)
                    if beat % 2:
                        tanh_gate(n0 + 16 + beat // 2, i - 1, beat // 2 % 2)
                for n in range(6):
                    split(at + first + 12 + n + 1, (n + 1) % 2)

            def copy_proj(t, e, b, i):
                if b < HALF_SUMS:
                    act.wait_ge(pp, 2 * HALF_SUMS * t + HALF_SUMS * e + b + 1)
                else:
                    act.wait_ge(panel_used, i + 1)
                nc.scalar.activation(proj[:, b, e * T:(e + 1) * T], bank[b][:, :],
                                     ACT.Copy).then_inc(pp_copied, 1)

            def ple_section(t, last):
                at = ffn_base(t, last) + FFN_P
                n3 = norm2_no(t, last) + 1
                split(at + 1, 1)
                for b in range(NB):
                    act.wait_ge(down_added, 24 * t + 20 + b + 1)
                    sum_squares(n3, b, h[:, b, :])
                for b in range(NB):
                    copy_proj(t, 0, b, at)
                split(at + 2, 0)
                for b in range(3):
                    norm_hi(n3, b, hn_hi)
                copy_proj(t, 1, 0, at + 1)
                copy_proj(t, 1, 1, at + 1)
                norm_hi(n3, 3, hn_hi)
                copy_proj(t, 1, 2, at + 1)
                copy_proj(t, 1, 3, at + 1)
                for e in range(2):
                    for r in range(4):
                        i = at + PROJ_P + 4 * e + r
                        if not (last and e == 1 and r == 3):
                            split(i + 1, (r + 1) % 2)
                    for b in range(NB):
                        if b < HALF_SUMS:
                            act.wait_ge(gt, 2 * HALF_SUMS * t + HALF_SUMS * e + b + 1)
                        else:
                            act.wait_ge(panel_used, i + 1)
                        n = 8 * t + 4 * e + b
                        buf = (act_a, act_b)[b % 2]
                        if e or b >= 2:
                            act.wait_ge(ple_out, n - 1)
                        nc.scalar.activation(buf[:, :], bank[4 * e + b][:, :], ACT.Tanh,
                                             scale=0.5).then_inc(sig, 1)
                        if e and b == 1 and not last:
                            split(i + 2, 1)

            def out_section(t, norm1):
                at = iter_base(t)
                n1 = 3 * t + 1
                for beat in range(8):
                    if beat:
                        split(at + beat + 1, (beat + 1) % 2)
                    if norm1 and beat in (2, 4):
                        if beat == 2:
                            act.wait_ge(ple_mul, 8 * t + 1)
                        norm_hi(n1, beat - 2, wide_hi)
                        norm_hi(n1, beat - 1, wide_hi)
                    if norm1:
                        for b in {0: (0, 1), 2: (2,), 3: (3,)}.get(beat, ()):
                            act.wait_ge(x_landed[b % 2], 32 * t + 16 * (b // 2 + 1))
                            sum_squares(n1, b, stage[:, b % 2, :])

            def z_section(s, at, n2):
                for beat in range(10):
                    split(at + beat + 1, (beat + 1) % 2)
                    if n2 is not None and beat == 2:
                        act.wait_ge(band_stored, 16)
                    if n2 is not None and 2 <= beat < 4:
                        norm_hi(n2, beat - 2, hn_hi)
                    if n2 is not None and beat == 4:
                        norm_hi(n2, 2, hn_hi)
                        norm_hi(n2, 3, hn_hi)
                    if n2 is not None and beat < 4:
                        act.wait_ge(out_added, 8 * (s - 1) + 4 + beat + 1)
                        sum_squares(n2, beat, h[:, beat, :])
                    if beat == 4:
                        for b in range(NB):
                            copy_q(s, b, at)
                    if 7 <= beat:
                        copy_u(s, beat - 7, at)
                copy_u(s, 3, at)

            def load_constants():
                act.dma_start(rel_sb[:, :], rel_bias).then_inc(consts, 16)
                act.dma_start(onehot_sb[:, :], onehot).then_inc(consts, 16)
                act.dma_start(scale_sb[:, :], pool_scale.rearrange("(g p) -> p g", p=P),
                              allow_slow_non_contiguous=True).then_inc(consts, 16)
                for n, g in ((1, g_ffn), (2, g_ple)):
                    act.dma_start(gains[:, n, :], bcast(g, D)).then_inc(consts, 16)
                act.dma_start(gqk[:, 0:QW].rearrange("p (h d) -> p h d", d=HEAD_DIM),
                              bass.AP(g_q.tensor, g_q.offset, [[0, P], [0, NQ], [1, HEAD_DIM]])
                              ).then_inc(wp_landed, 16)
                act.dma_start(gqk[:, QW:QKW].rearrange("p (h d) -> p h d", d=HEAD_DIM),
                              bass.AP(g_k.tensor, g_k.offset, [[0, P], [0, NKV], [1, HEAD_DIM]])
                              ).then_inc(wp_landed, 16)
                act.dma_start(act_a[:, :].rearrange("p (g d) -> p g d", g=NPOOL),
                              w_pool.rearrange("g c d -> c g d")).then_inc(wp_landed, 16)

            for b in range(NB):
                act.wait_ge(first_x[b], 16)
                sum_squares(0, b, h[:, b, :])
                if b == 1:
                    load_constants()
                if b == 3:
                    split(0, 0)
                if b:
                    norm_hi(0, b - 1, wide_hi)
            norm_hi(0, 3, wide_hi)
            act.wait_ge(wp_landed, 48)
            nc.scalar.activation(wp_hi[:, :, :].rearrange("p g d -> p (g d)"), act_a[:, :],
                                 ACT.Copy).then_inc(wp_hi_done, 1)
            z_section(0, 0, None)
            act.wait_ge(consts, CONSTS)
            act.wait_ge(out_stored, 32)
            split(Z_P + 1, 1)
            stage_q(0, 0)

            def flowing_block(b):
                for j in range(PAIRS):
                    attention_step(0, b, j, True)
                    if isinstance(b, int) and b == 0:
                        pooled_hi(0, j)
                if not (isinstance(b, int) and b == NB - 1):
                    stage_q(0, b + 1)

            flowing_block(0)
            with act.Fori(1, NB - 1) as b:
                flowing_block(b)
            flowing_block(NB - 1)
            for g in range(NPOOL):
                attention_step(0, NB, g, True)
                pool_y_hi(0, g, 0)

            with act.Fori(0, LAST) as t:
                out_section(t, True)
                z_section(t + 1, iter_base(t) + OUT_P, 3 * t + 2)
                ffn_section(t, False)
                ple_section(t, False)
            out_section(LAST, False)
            for b in range(NB):
                act.wait_ge(out_added, 8 * LAST + 4 + b + 1)
                sum_squares(3 * LAST + 1, b, h[:, b, :])
                if b:
                    norm_hi(3 * LAST + 1, b - 1, hn_hi)
            norm_hi(3 * LAST + 1, 3, hn_hi)
            ffn_section(LAST, True)
            ple_section(LAST, True)

        @block.vector
        def _(dve):
            def split(i, parity):
                dve.wait_ge(hi_done, i + 1)
                nc.vector.tensor_tensor(w_lo[:, parity, :], raw[:, parity, :],
                                        w_hi[:, parity, :].bitcast(F32),
                                        ALU.subtract).then_inc(lo_done, 1)

            def normalise(n_norm, b, src, gain):
                n = 4 * n_norm + b
                dve.wait_ge(rstd_done, n + 1)
                if not (isinstance(n_norm, int) and n < 2):
                    dve.wait_ge(nT, 2 * n - 2)
                nc.vector.scalar_tensor_tensor(out=stage[:, b % 2, :], in0=src, scalar=rstd[:, b:b + 1],
                                               in1=gains[:, gain, :], op0=ALU.mult,
                                               op1=ALU.mult).then_inc(xn_done, 1)

            def norm_lo(n_norm, b, hi, lo):
                for e in range(2):
                    dve.wait_ge(nhi, 8 * n_norm + 2 * b + e + 1)
                    src = bank[4 + (2 * b + e) % 4][:, :].rearrange("p (k t) -> p k t", k=4)
                    at = (slice(None), slice(4 * e, 4 * e + 4), slice(b * P, (b + 1) * P))
                    nc.vector.tensor_tensor(lo[at], src, hi[at].bitcast(F32),
                                            ALU.subtract).then_inc(nlo, 1)

            def copy_kv(s, b, at):
                if b < HALF_SUMS:
                    dve.wait_ge(zkv, HALF_SUMS * s + b + 1)
                else:
                    dve.wait_ge(panel_used, at + 6)
                nc.vector.tensor_copy(qkv[:, b, QW:], bank[4 + b][:, 0:2 * KVW]).then_inc(kvcopied, 1)

            def qk_mean(s, b):
                n = 4 * s + b
                heads = NQ + NKV
                dve.wait_ge(qsq, n + 1)
                nc.vector.tensor_reduce(out=qss[:, b, :],
                                        in_=qk_sq[:, :].rearrange("p (h d) -> p h d", h=heads),
                                        axis=AX.X, op=ALU.add).then_inc(qred, 1)

            def qk_scale(s, b):
                dve.wait_ge(qrs_done, 4 * s + b + 1)
                v = qkv[:, b, 0:QKW].rearrange("p (h d) -> p h d", d=HEAD_DIM)
                nc.vector.tensor_tensor(v, v, qrs[:, b, :].unsqueeze(2).to_broadcast([P, NQ + NKV, HEAD_DIM]),
                                        ALU.mult).then_inc(qscaled, 1)

            def qk_gain(s, b):
                n = 4 * s + b
                dve.wait_ge(qscaled, n + 1)
                dve.wait_ge(tqk, 2 * n)
                q = qkv[:, b, 0:QW].rearrange("p (j c d) -> p c j d", j=2, d=HEAD_DIM)
                nc.vector.tensor_tensor(qkn[:, 0:QW].rearrange("p (c j d) -> p c j d", j=2, d=HEAD_DIM), q,
                                        gqk[:, 0:QW].rearrange("p (c j d) -> p c j d", j=2, d=HEAD_DIM),
                                        ALU.mult)
                nc.vector.tensor_tensor(qkn[:, QW:QKW], qkv[:, b, QW:QKW], gqk[:, QW:QKW],
                                        ALU.mult).then_inc(qkn_done, 1)

            def stage_k(s, b):
                n = 4 * s + b
                dve.wait_ge(logits, 4 * n)
                dve.wait_ge(kstaged, n)
                nc.vector.tensor_copy(kcat[:, 0:P], kcat[:, P:2 * P]).then_inc(kcarried, 1)
                dve.wait_ge(kcarried, n + 1)
                dve.wait_ge(tqk, 2 * n + 2)
                nc.vector.tensor_copy(kcat[:, P:2 * P], bank[k_bank(s)][:, 0:P]).then_inc(kstaged, 1)

            def stage_v(s, b):
                n = 4 * s + b
                dve.wait_ge(pv, 4 * n)
                dve.wait_ge(vstaged, n)
                nc.vector.tensor_copy(vcat[:, 0, :], vcat[:, 1, :]).then_inc(vcarried, 1)
                dve.wait_ge(vcarried, n + 1)
                nc.vector.tensor_copy(vcat[:, 1, :], qkv[:, b, QKW:]).then_inc(vstaged, 1)

            def softmax_in(n, c, halves):
                i, first = c % 2, (2 - halves) * P
                dve.wait_ge(logits, n + 1)
                dve.wait_ge(probs_T, no_less(n - 3))
                nc.vector.scalar_tensor_tensor(
                    out=scores[:, c, :, first:],
                    in0=bank[4][:, :].rearrange("p (j k) -> p j k", j=2)[:, :, first:],
                    scalar=HEAD_DIM ** -0.5, in1=bias[:, c, :, first:],
                    op0=ALU.mult, op1=ALU.add).then_inc(scaled, 1)
                dve.wait_ge(scaled, n + 1)
                nc.vector.tensor_reduce(out=row_max[:, i, :], in_=scores[:, c, :, :], axis=AX.X,
                                        op=ALU.max).then_inc(maxed, 1)
                dve.wait_ge(maxed, n + 1)
                nc.vector.scalar_tensor_tensor(out=neg_max[:, i, :], in0=row_max[:, i, :], scalar=-1.0,
                                               in1=neg_sink[:, :, c], op0=ALU.mult,
                                               op1=ALU.min).then_inc(neg_maxed, 1)

            def softmax_den(n, c):
                i = c % 2
                dve.wait_ge(exped, n + 1)
                nc.vector.tensor_tensor(den[:, i, :], row_sum[:, i, :], sink_exp[:, i, :],
                                        ALU.add).then_inc(summed, 1)
                dve.wait_ge(summed, n + 1)
                dve.wait_ge(pnorm, no_less(n - 1))
                nc.vector.reciprocal(rden[:, i, :], den[:, i, :]).then_inc(rden_done, 1)

            def attention_rest(n, b, c):
                dve.wait_ge(attn_hi, n + 1)
                for j in range(2):
                    rows = slice(64 * j, 64 * j + 64)
                    last = nc.vector.tensor_tensor(mix_lo[rows, c, bass.ts(b, P)],
                                                   bank[6][rows, j * P:(j + 1) * P],
                                                   mix_hi[rows, c, bass.ts(b, P)].bitcast(F32),
                                                   ALU.subtract)
                last.then_inc(attn_lo, 1)

            def attention_step(s, b, j, flowing):
                at = unit_at(b, j, 0, flowing)
                if at:
                    halves = 1 if isinstance(s, int) and isinstance(b, int) and s == b == 0 else 2
                    softmax_in(16 * s + 4 * at[0] + at[1], at[1], halves)
                at = unit_at(b, j, LAG_NORM, flowing)
                if at:
                    softmax_den(16 * s + 4 * at[0] + at[1], at[1])
                at = unit_at(b, j, LAG_PV, flowing)
                if at:
                    attention_rest(16 * s + 4 * at[0] + at[1], *at)
                if j == 2 and not (isinstance(b, int) and b == NB):
                    stage_v(s, b)

            def pool_sums(s, g):
                levels = g + 1
                done = s * 10 + g * (g + 1) // 2
                src = u[:, g, :]
                pair = (sum_a, sum_b) if levels % 2 else (sum_b, sum_a)
                if g == 0:
                    dve.wait_ge(ucopied, 4 * s + 4)
                if not (isinstance(s, int) and s == 0 and g == 0):
                    dve.wait_ge(pool_lo, 4 * s + g)
                lead = 0
                for n in range(levels):
                    step = 1 << n
                    dst = pair[n % 2]
                    lo = lead + step
                    if n:
                        dve.wait_ge(level, done + n)
                    nc.vector.tensor_tensor(dst[:, lo:], src[:, lo:],
                                            src[:, lo - step:CARRY + T - step],
                                            ALU.add).then_inc(level, 1)
                    src, lead = dst, lo

            def pool_mean(s, g):
                dve.wait_ge(level, 10 * s + (g + 1) * (g + 2) // 2)
                if isinstance(s, int) and s == 0:
                    nc.vector.tensor_tensor(sum_a[:, CARRY:2 * CARRY], sum_a[:, CARRY:2 * CARRY],
                                            edge_sb[:, g, :], ALU.mult).then_inc(edged, 1)
                    dve.wait_ge(edged, g + 1)
                nc.vector.scalar_tensor_tensor(out=sum_a[:, CARRY:], in0=sum_a[:, CARRY:],
                                               scalar=1.0 / POOL_SIZES[g], in1=u[:, g, CARRY:],
                                               op0=ALU.mult, op1=ALU.subtract).then_inc(pooled, 1)

            def pool_y_rest(s, g, banks):
                dve.wait_ge(y_hi, 4 * s + g + 1)
                nc.vector.scalar_tensor_tensor(out=mix_lo[:, 4 + g, :], in0=bank[banks + g][:, :],
                                               scalar=scale_sb[:, g:g + 1],
                                               in1=mix_hi[:, 4 + g, :].bitcast(F32), op0=ALU.mult,
                                               op1=ALU.subtract).then_inc(y_lo, 1)

            def gate_in(n, parity):
                dve.wait_ge(tanhed, n + 1)
                nc.vector.scalar_tensor_tensor(out=act_a[:, :], in0=act_a[:, :], scalar=1.0,
                                               in1=bank[2 * parity][:, :], op0=ALU.add,
                                               op1=ALU.mult).then_inc(gated, 1)

            def gate_up(n, i, parity, k):
                dve.wait_ge(panel_used, i + 1)
                dve.wait_ge(gated, n + 1)
                dve.wait_ge(act_lo_done, n + 1)
                nc.vector.scalar_tensor_tensor(out=act_b[:, :], in0=act_a[:, :], scalar=0.5,
                                               in1=bank[2 * parity + 1][:, :], op0=ALU.mult,
                                               op1=ALU.mult).then_inc(glu_free, 1)
                dve.wait_ge(glu_free, n + 3)
                nc.vector.tensor_copy(wide_hi[:, k, :], act_b[:, :]).then_inc(act_hi_done, 1)

            def add_down(t, g, e, i):
                for b in range(NB):
                    if b < HALF_SUMS:
                        dve.wait_ge(down, 6 * HALF_SUMS * t + HALF_SUMS * (2 * g + e) + b + 1)
                    else:
                        dve.wait_ge(panel_used, i + 1)
                    v = h[:, b, e * T:(e + 1) * T]
                    nc.vector.tensor_tensor(v, bank[4 * e + b][:, :], v, ALU.add).then_inc(down_added, 1)

            def p_lo_part(t, kk):
                dve.wait_ge(pT_hi, 2 * t + kk + 1)
                nc.vector.tensor_tensor(p_lo[:, kk, :], bank[4 + kk][:, :], p_hi[:, kk, :].bitcast(F32),
                                        ALU.subtract).then_inc(pT_lo, 1)

            def ffn_section(t, last):
                at, s, n0 = ffn_base(t, last), t + 1, NCH * t
                first = 0
                for g, nk in enumerate(GROUPS):
                    if g < 2:
                        with dve.Fori(0, 2) as it:
                            for beat in range(8):
                                i = at + first + beat + it * 8
                                if not last and beat == 0:
                                    qk_gain(s, it + 2 * g)
                                split(i + 1, (beat + 1) % 2)
                                if not last and beat == 0:
                                    stage_k(s, it + 2 * g)
                                if not last and beat:
                                    attention_step(s, it + 2 * g, beat - 1, False)
                                if beat % 2:
                                    c = beat // 2
                                    n = n0 + 8 * g + c + 4 * it
                                    gate_in(n, c % 2)
                                    gate_up(n, i, c % 2, 4 * it + c)
                    else:
                        for beat in range(12):
                            i = at + first + beat
                            split(i + 1, (beat + 1) % 2)
                            if not last and beat < 8:
                                (pool_mean if beat % 2 else pool_sums)(s, beat // 2)
                            if not last and beat % 2 and 2 < beat < 10:
                                pool_y_rest(s, beat // 2 - 1, 4)
                            if beat >= 10:
                                p_lo_part(t, beat - 10)
                            if beat % 2:
                                c = beat // 2
                                n = n0 + 16 + c
                                gate_in(n, c % 2)
                                gate_up(n, i, c % 2, c)
                    for n in range(nk):
                        i = at + first + 2 * nk + n
                        split(i + 1, (n + 1) % 2)
                        if n % (nk // 2) == nk // 2 - 1:
                            add_down(t, g, n // (nk // 2), i)
                    first += 3 * nk

            def ple_section(t, last):
                at = ffn_base(t, last) + FFN_P
                n3 = norm2_no(t, last) + 1
                split(at + 1, 1)
                if not last:
                    dve.wait_ge(probs_T, 16 * t + 32)
                for b in range(2):
                    normalise(n3, b, h[:, b, :], 2)
                split(at + 2, 0)
                normalise(n3, 2, h[:, 2, :], 2)
                norm_lo(n3, 0, hn_hi, hn_lo)
                norm_lo(n3, 1, hn_hi, hn_lo)
                normalise(n3, 3, h[:, 3, :], 2)
                norm_lo(n3, 2, hn_hi, hn_lo)
                norm_lo(n3, 3, hn_hi, hn_lo)
                for e in range(2):
                    for r in range(4):
                        if not (last and e == 1 and r == 3):
                            split(at + PROJ_P + 4 * e + r + 1, (r + 1) % 2)
                    for b in range(NB):
                        n = 8 * t + 4 * e + b
                        buf = (act_a, act_b)[b % 2]
                        dve.wait_ge(sig, n + 9)
                        dve.wait_ge(pp_copied, 8 * t + 4 * e + b + 1)
                        nc.vector.scalar_tensor_tensor(out=buf[:, :], in0=buf[:, :], scalar=1.0,
                                                       in1=proj[:, b, e * T:(e + 1) * T], op0=ALU.add,
                                                       op1=ALU.mult).then_inc(ple_mul, 1)
                        dve.wait_ge(ple_mul, n + 2)
                        v = h[:, b, e * T:(e + 1) * T]
                        nc.vector.scalar_tensor_tensor(out=v, in0=buf[:, :], scalar=0.5, in1=v,
                                                       op0=ALU.mult, op1=ALU.add).then_inc(ple_out, 1)
                        if e and b == 1 and not last:
                            split(at + PROJ_P + 9, 1)

            def add_out(t, e, at):
                for b in range(NB):
                    if b < HALF_SUMS:
                        dve.wait_ge(outp, 2 * HALF_SUMS * t + HALF_SUMS * e + b + 1)
                    else:
                        dve.wait_ge(panel_used, at + 4 * e + 4)
                    v = h[:, b, e * T:(e + 1) * T]
                    nc.vector.tensor_tensor(v, bank[4 * e + b][:, :], v, ALU.add).then_inc(out_added, 1)

            def out_section(t, norm1):
                at = iter_base(t)
                n1 = 3 * t + 1
                for beat in range(8):
                    if beat:
                        split(at + beat + 1, (beat + 1) % 2)
                    if norm1 and beat in (2, 4):
                        norm_lo(n1, beat - 2, wide_hi, wide_lo)
                        norm_lo(n1, beat - 1, wide_hi, wide_lo)
                    if norm1 and beat in (1, 3):
                        normalise(n1, beat - 1, stage[:, 0, :], 0)
                        normalise(n1, beat, stage[:, 1, :], 0)
                    if beat == 4:
                        dve.wait_ge(h_landed, 64 * (t + 1))
                        add_out(t, 0, at)
                add_out(t, 1, at)

            def z_section(s, at, n2):
                for beat in range(10):
                    split(at + beat + 1, (beat + 1) % 2)
                    if n2 is not None and beat == 2:
                        dve.wait_ge(band_stored, 16)
                    if n2 is not None and 2 <= beat < 4:
                        norm_lo(n2, beat - 2, hn_hi, hn_lo)
                    if n2 is None and beat < 4:
                        for n in (2 * beat, 2 * beat + 1):
                            dve.wait_ge(band_banks, n + 1)
                            nc.vector.tensor_copy(band[:, n, :], bank[4 + n % 4][:, 0:BAND]
                                                  ).then_inc(band_built, 1)
                    if n2 is not None and beat == 4:
                        norm_lo(n2, 2, hn_hi, hn_lo)
                        norm_lo(n2, 3, hn_hi, hn_lo)
                    if n2 is not None and beat < 4:
                        normalise(n2, beat, h[:, beat, :], 1)
                    if beat == 6:
                        for b in range(NB):
                            copy_kv(s, b, at)
                    if beat == 7:
                        qk_mean(s, 0)
                        qk_mean(s, 1)
                    if beat == 8:
                        qk_scale(s, 0)
                        qk_mean(s, 2)
                        qk_scale(s, 1)
                    if beat == 9:
                        qk_mean(s, 3)
                        qk_scale(s, 2)
                        qk_scale(s, 3)

            dve.wait_ge(gain_landed, 16)
            for b in range(NB):
                normalise(0, b, h[:, b, :], 0)
                if b == 3:
                    split(0, 0)
                if b:
                    norm_lo(0, b - 1, wide_hi, wide_lo)
            norm_lo(0, 3, wide_hi, wide_lo)
            dve.wait_ge(consts, CONSTS)
            dve.wait_ge(out_stored, 32)
            dve.wait_ge(mask_row, 1)
            nc.vector.tensor_copy(rel_rows[0:N_BUCKETS, :, :],
                                  rel_sb[:, :].unsqueeze(2).to_broadcast([N_BUCKETS, NQ, P])
                                  ).then_inc(rel_ready, 1)
            nc.vector.tensor_scalar(out=neg_sink[:, :, :], in0=sink[:, :, :], scalar1=-1.0, scalar2=None,
                                    op0=ALU.mult).then_inc(glu_free, 2)
            dve.wait_ge(wp_hi_done, 1)
            nc.vector.tensor_tensor(wp_lo[:, :, :].rearrange("p g d -> p (g d)"), act_a[:, :],
                                    wp_hi[:, :, :].rearrange("p g d -> p (g d)").bitcast(F32),
                                    ALU.subtract).then_inc(wp_lo_done, 1)
            dve.wait_ge(nT, 8)
            nc.vector.memset(scores[:, :, :, 0:P], MASKED).then_inc(masked, 1)
            z_section(0, 0, None)
            dve.wait_ge(bias_landed, 32)
            dve.wait_ge(masked, 1)
            split(Z_P + 1, 1)
            qk_gain(0, 0)
            stage_k(0, 0)

            def flowing_block(b):
                for j in range(PAIRS):
                    attention_step(0, b, j, True)
                    if j == 1 and not (isinstance(b, int) and b == NB - 1):
                        qk_gain(0, b + 1)
                    if isinstance(b, int) and b == 0:
                        pool_sums(0, j)
                        pool_mean(0, j)
                if not (isinstance(b, int) and b == NB - 1):
                    stage_k(0, b + 1)

            flowing_block(0)
            with dve.Fori(1, NB - 1) as b:
                flowing_block(b)
            flowing_block(NB - 1)
            for g in range(NPOOL):
                attention_step(0, NB, g, True)
                pool_y_rest(0, g, 0)

            with dve.Fori(0, LAST) as t:
                out_section(t, True)
                z_section(t + 1, iter_base(t) + OUT_P, 3 * t + 2)
                ffn_section(t, False)
                ple_section(t, False)
            out_section(LAST, False)
            for b in range(NB):
                normalise(3 * LAST + 1, b, h[:, b, :], 1)
                if b:
                    norm_lo(3 * LAST + 1, b - 1, hn_hi, hn_lo)
            norm_lo(3 * LAST + 1, 3, hn_hi, hn_lo)
            ffn_section(LAST, True)
            ple_section(LAST, True)

        @block.tensor
        def _(pe):
            mm = nc.tensor.matmul

            def alone(value):
                value = value if isinstance(value, int) else pe.to_reg(value)
                pe.wait_ge(rel_ready, 1)
                return value

            def rows_panel(i, parity, xh, xl, ks, banks, first, last, signal, free=None, width=T):
                pe.wait_ge(lo_done, i + 1)
                for b in range(NB):
                    if first and free is not None:
                        free(b)
                    out_ap = banks[b][:, 0:width]
                    tok = slice(b * P, (b + 1) * P)
                    for kk, k in enumerate(ks):
                        cols = slice(kk * width, (kk + 1) * width)
                        wh, wl = w_hi[:, parity, cols], w_lo[:, parity, cols]
                        mm(out_ap, xh[:, k, tok], wh, start=first and kk == 0, stop=False)
                        mm(out_ap, xh[:, k, tok], wl, start=False, stop=False)
                        ins = mm(out_ap, xl[:, k, tok], wh, start=False,
                                 stop=last and kk == len(ks) - 1)
                    if last and b < HALF_SUMS:
                        ins.then_inc(signal, 1)
                ins.then_inc(panel_used, 1)

            def features_panel(i, parity, xh, xl, dst, halfway=None):
                pe.wait_ge(lo_done, i + 1)
                for k in range(KC):
                    if k == KC // 2 and halfway is not None:
                        halfway()
                    cols = slice(k * P, (k + 1) * P)
                    wh, wl = w_hi[:, parity, cols], w_lo[:, parity, cols]
                    mm(dst[:, :], wh, xh[:, k, :], start=k == 0, stop=False)
                    mm(dst[:, :], wh, xl[:, k, :], start=False, stop=False)
                    ins = mm(dst[:, :], wl, xh[:, k, :], start=False, stop=k == KC - 1)
                ins.then_inc(panel_used, 1)

            def transpose_norm(n_norm, b, free=None):
                pe.wait_ge(xn_done, 4 * n_norm + b + 1)
                for e in range(2):
                    if b < 2:
                        if free is not None:
                            free((2 * b + e) % 4)
                    else:
                        pe.wait_ge(nlo, 8 * n_norm + 2 * b + e - 3)
                    dst = bank[4 + (2 * b + e) % 4]
                    for k in range(4):
                        c = (4 * e + k) * P
                        ins = nc.tensor.transpose(dst[:, k * P:(k + 1) * P],
                                                  stage[:, b % 2, c:c + P], ident[:, :])
                    ins.then_inc(nT, 1)

            def transpose_qk(s, b):
                n = 4 * s + b
                pe.wait_ge(qkn_done, n + 1)
                pe.wait_ge(qstaged, n)
                for c in range(PAIRS):
                    ins = nc.tensor.transpose(bank[7][:, c * P:(c + 1) * P], qkn[:, c * P:(c + 1) * P],
                                              ident[:, :])
                ins.then_inc(tqk, 1)
                pe.wait_ge(kstaged, n)
                if k_bank(s) == 6:
                    pe.wait_ge(attn_lo, 4 * n)
                nc.tensor.transpose(bank[k_bank(s)][:, 0:P], qkn[:, QW:QKW], ident[:, :]
                                    ).then_inc(tqk, 1)

            def logits_of(s, b, c):
                n = 16 * s + 4 * b + c
                if c == 0:
                    pe.wait_ge(qstaged, 4 * s + b + 1)
                    pe.wait_ge(kstaged, 4 * s + b + 1)
                pe.wait_ge(scaled, n)
                for j in range(2):
                    ins = mm(bank[4][:, j * 2 * P:(j + 1) * 2 * P], qz[:, c, j, :], kcat[:, :],
                             start=True, stop=True)
                ins.then_inc(logits, 1)

            def transpose_probs(n, c):
                pe.wait_ge(pnorm, n + 1)
                pe.wait_ge(probsT_copied, n)
                for half in range(2):
                    for j in range(2):
                        at = (2 * half + j) * P
                        ins = nc.tensor.transpose(bank[5][:, at:at + P],
                                                  scores[:, c, j, half * P:(half + 1) * P], ident[:, :])
                ins.then_inc(probs_T, 1)

            def attend(s, b, c):
                n = 16 * s + 4 * b + c
                if c == 0:
                    pe.wait_ge(vstaged, 4 * s + b + 1)
                pe.wait_ge(probsT_copied, n + 1)
                pe.wait_ge(attn_lo, n)
                for half in range(2):
                    ins = mm(bank[6][:, 0:2 * P], vcat[:, half, :], probsT[:, c % 2, half, :],
                             start=half == 0, stop=half == 1)
                ins.then_inc(pv, 1)

            def attention_step(s, b, j, flowing):
                at = unit_at(b, j, 0, flowing)
                if at:
                    logits_of(s, *at)
                at = unit_at(b, j, LAG_PV, flowing)
                if at:
                    attend(s, *at)
                at = unit_at(b, j, LAG_T, flowing)
                if at:
                    transpose_probs(16 * s + 4 * at[0] + at[1], at[1])

            def pool_y(s, g, banks):
                pe.wait_ge(pool_lo, 4 * s + g + 1)
                dst = bank[banks + g]
                mm(dst[:, :], wp_hi[:, g, :], mix_hi[:, 4 + g, :], start=True, stop=False)
                mm(dst[:, :], wp_hi[:, g, :], mix_lo[:, 4 + g, :], start=False, stop=False)
                mm(dst[:, :], wp_lo[:, g, :], mix_hi[:, 4 + g, :], start=False,
                   stop=True).then_inc(y_done, 1)

            def transpose_p(t, kk):
                pe.wait_ge(p_landed, 64 * (t + 1))
                for b in range(NB):
                    ins = nc.tensor.transpose(bank[4 + kk][:, b * P:(b + 1) * P],
                                              p_rows[:, b, kk * P:(kk + 1) * P], ident[:, :])
                ins.then_inc(pT, 1)

            def attention_banks_free(s, blocks, b):
                if b == 0:
                    pe.wait_ge(scaled, 16 * s + 4 * blocks)
                elif b == 1:
                    pe.wait_ge(probsT_copied, 16 * s + 4 * blocks)
                elif b == 2:
                    pe.wait_ge(attn_lo, 16 * s + 4 * blocks)
                else:
                    pe.wait_ge(qstaged, 4 * s + blocks)

            def ffn_section(t, last):
                at, s, n0 = ffn_base(t, last), t + 1, NCH * t
                first = 0
                if last:
                    pe.wait_ge(out_added, alone(8 * t + 4))
                else:
                    pe.wait_ge(ucopied, alone(4 * s + 2))
                    pe.wait_ge(kvcopied, 4 * s + 4)
                pe.wait_ge(nlo, 8 * norm2_no(t, last) + 8)
                for g, nk in enumerate(GROUPS):
                    if g:
                        pe.wait_ge(down_added, alone(24 * t + 8 * g))
                    if g < 2:
                        with pe.Fori(0, 2) as it:
                            for beat in range(8):
                                c = beat // 2
                                n = n0 + 8 * g + c + 4 * it
                                if beat % 2 == 0:
                                    pe.wait_ge(glu_free, n + 1)
                                if beat == 2 and not last:
                                    pe.wait_ge(ucopied, 4 * s + 4)
                                if not last and beat:
                                    attention_step(s, it + 2 * g, beat - 1, False)
                                features_panel(at + first + beat + it * 8, beat % 2, hn_hi, hn_lo,
                                               bank[2 * (c % 2) + beat % 2],
                                               (lambda: transpose_qk(s, it + 2 * g))
                                               if not last and beat == 0 else None)
                    else:
                        for beat in range(12):
                            c = beat // 2
                            if beat % 2 == 0:
                                pe.wait_ge(glu_free, n0 + 16 + c + 1)
                            features_panel(at + first + beat, beat % 2, hn_hi, hn_lo,
                                           bank[2 * (c % 2) + beat % 2])
                            if not last and beat % 2 == 0 and 2 <= beat <= 8:
                                pool_y(s, beat // 2 - 1, 4)
                            if beat >= 9 and beat < 11:
                                if not last:
                                    pe.wait_ge(y_lo, 4 * s + beat - 9 + 1)
                                transpose_p(t, beat - 9)
                    done = n0 + 8 * g + nk
                    for e in range(2):
                        for r in range(nk // 2):
                            n = e * (nk // 2) + r
                            if e == 0:
                                pe.wait_ge(act_lo_done, n0 + 8 * g + 2 * r + 3)

                            def free(b):
                                if e == 0:
                                    pe.wait_ge(glu_free, done + 2 - (1 if b < 2 else 0))
                                elif g < 2 and not last:
                                    attention_banks_free(s, 2 * g + 2, b)
                                elif g == 2 and b < 2:
                                    pe.wait_ge(pT_lo, 2 * t + b + 1)
                                elif g == 2 and not last:
                                    pe.wait_ge(y_lo, 4 * s + b + 1)

                            rows_panel(at + first + 2 * nk + n, n % 2, wide_hi, wide_lo,
                                       (2 * r, 2 * r + 1), bank[4 * e:4 * e + 4], r == 0,
                                       r == nk // 2 - 1, down, free)
                    first += 3 * nk

            def ple_section(t, last):
                at = ffn_base(t, last) + FFN_P
                n3 = norm2_no(t, last) + 1
                pe.wait_ge(pT_lo, 2 * t + 2)

                def norm3(b):
                    transpose_norm(n3, b, lambda q: pe.wait_ge(down_added, 24 * t + 20 + q + 1))

                for e in range(2):
                    def free(b):
                        if e == 1 and b == 2:
                            norm3(1)
                        pe.wait_ge(*((down_added, 24 * t + 16 + b + 1) if e == 0
                                     else (pp_copied, 8 * t + b + 1)))
                    rows_panel(at + e, e, p_hi, p_lo, range(KP), bank[0:4], True, True, pp, free)
                    if e == 0:
                        norm3(0)
                norm3(2)
                norm3(3)
                pe.wait_ge(nlo, 8 * n3 + 8)
                for e in range(2):
                    for r in range(4):
                        def free(b):
                            if e == 0:
                                pe.wait_ge(pp_copied, 8 * t + 4 + b + 1)
                        rows_panel(at + PROJ_P + 4 * e + r, r % 2, hn_hi, hn_lo, (2 * r, 2 * r + 1),
                                   bank[4 * e:4 * e + 4], r == 0, r == 3, gt, free)

            def out_section(t, norm1):
                at = iter_base(t)
                n1 = 3 * t + 1
                pe.wait_ge(y_lo, 4)
                for e in range(2):
                    for r in range(4):
                        if e == 0 and r == 2:
                            pe.wait_ge(y_lo, 4 * t + 4)

                        def free(b):
                            pe.wait_ge(sig, 8 * t + 4 * e + b + 1)
                            if e == 0:
                                pe.wait_ge(attn_lo, 16 * t + 4 * b + 4)
                            if e == 1 and norm1:
                                pe.wait_ge(nlo, 8 * n1 + 4 + b + 1)
                        rows_panel(at + 4 * e + r, r % 2, mix_hi, mix_lo, (2 * r, 2 * r + 1),
                                   bank[4 * e:4 * e + 4], r == 0, r == 3, outp, free)
                        if norm1 and e == 0:
                            for b in {1: (0, 1), 3: (2, 3)}.get(r, ()):
                                transpose_norm(n1, b, lambda q: pe.wait_ge(sig, 8 * t + 4 + q + 1))

            def z_section(s, at, n2, n_before):
                for c in range(4):
                    def free(b):
                        if n2 is not None:
                            pe.wait_ge(out_added, 8 * (s - 1) + b + 1)
                        else:
                            if b in (1, 2):
                                transpose_norm(0, b + 1)
                            pe.wait_ge(nlo, 2 * b + 2)
                    rows_panel(at + c, c % 2, wide_hi, wide_lo, (2 * c, 2 * c + 1), bank[0:4],
                               c == 0, c == 3, zq, free)
                    if n2 is None:
                        for n in (2 * c, 2 * c + 1):
                            if n == 0:
                                pe.wait_ge(rel_ready, 1)
                            if n < 4:
                                pe.wait_ge(nlo, 4 + n + 1)
                            else:
                                pe.wait_ge(band_built, n - 3)
                            mm(bank[4 + n % 4][:, 0:3 * P], rel_rows[0:N_BUCKETS + 1, n, :],
                               onehot_sb[:, :], start=True, stop=True).then_inc(band_banks, 1)
                    if n2 is not None:
                        for b in {1: (0,), 2: (1,), 3: (2, 3)}.get(c, ()):
                            transpose_norm(n2, b,
                                           lambda q: pe.wait_ge(out_added, 8 * (s - 1) + 4 + q + 1))
                for c in range(2):
                    def free(b):
                        pe.wait_ge(nlo, 8 * n_before + 4 + b + 1)
                        if n2 is None:
                            pe.wait_ge(band_built, 4 + b + 1)
                    rows_panel(at + 4 + c, c % 2, wide_hi, wide_lo, range(4 * c, 4 * c + 4), bank[4:8],
                               c == 0, c == 1, zkv, free, width=2 * KVW)
                for g in range(NPOOL):
                    pe.wait_ge(qcopied, 4 * s + g + 1)
                    features_panel(at + 6 + g, g % 2, wide_hi, wide_lo, bank[g])

            pe.wait_ge(ident_landed, 16)
            transpose_norm(0, 0)
            transpose_norm(0, 1)
            z_section(0, 0, None, 0)
            transpose_qk(0, 0)

            def flowing_block(b):
                for j in range(PAIRS):
                    attention_step(0, b, j, True)
                if not (isinstance(b, int) and b == NB - 1):
                    transpose_qk(0, b + 1)

            flowing_block(0)
            with pe.Fori(1, NB - 1) as b:
                flowing_block(b)
            flowing_block(NB - 1)
            pe.wait_ge(wp_lo_done, 1)
            for g in range(NPOOL):
                attention_step(0, NB, g, True)
                pool_y(0, g, 0)

            with pe.Fori(0, LAST) as t:
                out_section(t, True)
                z_section(t + 1, iter_base(t) + OUT_P, 3 * t + 2, 3 * t + 2)
                ffn_section(t, False)
                ple_section(t, False)
            out_section(LAST, False)
            for b in range(NB):
                transpose_norm(3 * LAST + 1, b,
                               lambda q: pe.wait_ge(out_added, 8 * LAST + 4 + q + 1))
            ffn_section(LAST, True)
            ple_section(LAST, True)


def bucket_of(dist):
    n = np.maximum(dist, 0)
    exact = N_BUCKETS // 2
    far = exact + (np.log(np.maximum(n, 1).astype(np.float64) / exact)
                   / np.log(MAX_DISTANCE / exact) * (N_BUCKETS - exact)).astype(np.int64)
    return np.where(n < exact, n, np.minimum(far, N_BUCKETS - 1))


def kernel(**inputs):
    import concourse.bacc as _bacc
    from concourse.bass_utils import run_bass_kernel_spmd as _run

    nc = _bacc.Bacc("TRN2", target_bir_lowering=False, num_devices=1, dynamic_dma_scratch_size=4096)
    names = ["x", "p", "w_in", "w_out", "g_attn_norm", "g_q", "g_k", "attn_sinks", "rel_bias", "w_pool",
             "pool_scale", "g_ffn_norm", "w_gate", "w_up", "w_down", "g_ple_norm", "w_ple_gate",
             "w_ple_proj"]
    arrays = {}
    for name in names:
        a = np.ascontiguousarray(inputs[name])
        if name == "p":
            a = a[0, 0]
        elif name != "rel_bias":
            a = a[0]
        arrays[name] = a
    dist = 2 * P - 1 - np.arange(3 * P)
    inside = (dist >= 0) & (dist < WINDOW)
    row = np.where(inside, bucket_of(dist), N_BUCKETS)
    arrays["onehot"] = (row[None, :] == np.arange(N_BUCKETS + 1)[:, None]).astype(np.float32)
    arrays["identity"] = np.eye(P, dtype=np.float32)
    arrays["edge"] = np.array([[w / min(i + 1, w) for i in range(CARRY)] for w in POOL_SIZES],
                              dtype=np.float32)
    aps = [nc.dram_tensor(f"in_{n}", a.shape, F32, kind="ExternalInput").ap()
           for n, a in arrays.items()]
    out = nc.dram_tensor("out_h", arrays["x"].shape, F32, kind="ExternalOutput").ap()
    by = dict(zip(arrays, aps))
    build(nc, by["x"], by["p"], by["w_in"], by["w_out"], by["g_attn_norm"], by["g_q"], by["g_k"],
          by["attn_sinks"], by["rel_bias"], by["w_pool"], by["pool_scale"], by["g_ffn_norm"],
          by["w_gate"], by["w_up"], by["w_down"], by["g_ple_norm"], by["w_ple_gate"],
          by["w_ple_proj"], by["identity"], by["onehot"], by["edge"], out)
    r = _run(nc, [{f"in_{n}": a for n, a in arrays.items()}], core_ids=[0])
    return r.results[0]["out_h"][None]
```

```python
import numpy as np
from contextlib import ExitStack

import concourse.bass as bass
from concourse import mybir

F32 = mybir.dt.float32
F32R = mybir.dt.float32r
BF16 = mybir.dt.bfloat16
ALU = mybir.AluOpType
ACT = mybir.ActivationFunctionType
AX = mybir.AxisListType

P = 128
HEAD_DIM = 64
NQ = 8
NKV = 2
PAIRS = NQ // NKV
QW = NQ * HEAD_DIM
KVW = NKV * HEAD_DIM
QKW = QW + KVW
WINDOW = 128
POOL_SIZES = (2, 4, 8, 16)
NPOOL = len(POOL_SIZES)
CARRY = 16
N_BUCKETS = 32
MAX_DISTANCE = 128
EPS = 1e-6
MASKED = -1e30
BAND = 3 * P - 1
T = 512
NB = T // P
PANEL = 1024
GROUPS = (8, 8, 6)
OUT_P, Z_P, FFN_P, PROJ_P, GATE_P = 8, 10, 3 * sum(GROUPS), 2, 8
TILE_P = OUT_P + Z_P + FFN_P + PROJ_P + GATE_P


def build(nc, x, p, w_in, w_out, g_attn, g_q, g_k, sinks, rel_bias, w_pool, pool_scale, g_ffn,
          w_gate, w_up, w_down, g_ple, w_ple_gate, w_ple_proj, identity, onehot, edge, out):
    S, D = x.shape
    KC = D // P
    NT = S // T
    LAST = NT - 1
    NCH = sum(GROUPS)
    KP = w_ple_proj.shape[0] // P
    scratch = nc.dram_tensor("band_rows", (NQ, P * BAND), F32, kind="Internal")

    ctx = ExitStack()
    with ctx:
        base = [(nc.sbuf_base + 63) // 64 * 64]

        def sb(name, shape, dt=F32, at=None):
            size = int(np.prod(shape[1:])) * (2 if dt == BF16 else 4)
            where = at if at is not None else base[0]
            if at is None:
                base[0] += (size + 31) // 32 * 32
            return nc.alloc_sbuf_tensor_at(name, list(shape), dt, offset=where)

        def sem(name):
            return ctx.enter_context(nc.semaphore(name))

        wide_at = base[0]
        wide_hi = sb("wide_hi", [P, KC, T], F32R)
        wide_lo = sb("wide_lo", [P, KC, T], F32R)
        proj = sb("proj", [P, NB, D], F32, at=wide_at)
        mix_hi = sb("mix_hi", [P, KC, T], F32R)
        mix_lo = sb("mix_lo", [P, KC, T], F32R)
        hn_at = base[0]
        hn_hi = sb("hn_hi", [P, KC, T], F32R)
        hn_lo = sb("hn_lo", [P, KC, T], F32R)
        h = sb("h", [P, NB, D])
        rel_rows = sb("rel_rows", [P, NQ, P], at=hn_at)
        band = sb("band", [P, NQ, BAND], at=hn_at + NQ * P * 4)
        first_sq = band[:, :, :].rearrange("p h s -> p (h s)")[:, 0:NB * QKW].rearrange(
            "p (b n) -> p b n", b=NB)
        stage = sb("stage", [P, 2, D])
        scores = stage[:, :, :].rearrange("p b (c j k) -> p (b c) j k", j=2, k=2 * P)
        squares = sb("squares", [P, D], BF16)
        gains = sb("gains", [P, 3, D])
        u = sb("u", [P, NPOOL, CARRY + T])
        sums = sb("sums", [P, 2 * (CARRY + T)])
        sum_a, sum_b = sums[:, 0:CARRY + T], sums[:, CARRY + T:2 * (CARRY + T)]
        qkv_at = base[0]
        qkv = sb("qkv", [P, NB, QKW + KVW])
        p_rows = qkv[:, :, :].rearrange("p b n -> p (b n)")[:, 0:NB * KP * P].rearrange(
            "p (b n) -> p b n", b=NB)
        p_hi = sb("p_hi", [P, KP, T], F32R, at=qkv_at + NB * KP * P * 4)
        p_lo = sb("p_lo", [P, KP, T], F32R, at=qkv_at + NB * KP * P * 4 + KP * T * 4)
        qk_sq = sums[:, 0:QKW]
        qkn = sb("qkn", [P, QKW])
        qT_hi = sb("qT_hi", [P, PAIRS, P], F32R)
        qT_lo = sb("qT_lo", [P, PAIRS, P], F32R)
        kT_hi = sb("kT_hi", [P, NKV, 2 * P], F32R)
        kT_lo = sb("kT_lo", [P, NKV, 2 * P], F32R)
        v_at = base[0]
        v_hi = sb("v_hi", [P, 2, KVW], F32R)
        v_lo = sb("v_lo", [P, 2, KVW], F32R)
        probsT_at = base[0]
        probsT_hi = sb("probsT_hi", [P, 2, 2 * P], F32R)
        probsT_lo = sb("probsT_lo", [P, 2, 2 * P], F32R)
        v_whole = sb("v_whole", [P, 2, KVW], at=v_at)
        probsT_whole = sb("probsT_whole", [P, 2, 2, 2 * P], at=probsT_at)
        bias = sb("bias", [P, PAIRS, 2, 2 * P])
        gqk = sb("gqk", [P, QKW])
        wp_hi = sb("wp_hi", [P, NPOOL, P], F32R)
        wp_lo = sb("wp_lo", [P, NPOOL, P], F32R)
        act_a = sb("act_a", [P, T])
        act_b = sb("act_b", [P, T])
        raw = sb("raw", [P, 2, PANEL])
        w_hi = sb("w_hi", [P, 2, PANEL], F32R)
        w_lo = sb("w_lo", [P, 2, PANEL], F32R)
        ident = sb("ident", [P, P])
        onehot_sb = qkv[0:N_BUCKETS + 1, 0, 0:3 * P]
        rel_sb = sb("rel_sb", [N_BUCKETS, NQ])
        edge_sb = sb("edge_sb", [P, NPOOL, CARRY])
        scale_sb = sb("scale_sb", [P, NPOOL])
        sink = sb("sink", [P, 2, PAIRS])
        neg_sink = sb("neg_sink", [P, 2, PAIRS])
        ss = sb("ss", [P, NB])
        ms = sb("ms", [P, NB])
        rstd = sb("rstd", [P, NB])
        minus_half = sb("minus_half", [P, 1])
        qss = sb("qss", [P, NB, NQ + NKV])
        qms = sb("qms", [P, NB, NQ + NKV])
        qrs = sb("qrs", [P, NB, NQ + NKV])
        neg_max = sb("neg_max", [P, 2, 2])
        row_max = sb("row_max", [P, 2, 2])
        row_sum = sb("row_sum", [P, 2, 2])
        sink_shift = sb("sink_shift", [P, 2, 2])
        sink_exp = sb("sink_exp", [P, 2, 2])
        den = sb("den", [P, 2, 2])
        rden = sb("rden", [P, 2, 2])
        assert base[0] <= nc.sbuf_usable_end, (base[0], nc.sbuf_usable_end)

        bank = [ctx.enter_context(nc.psum_tensor(f"bank{i}", [P, T], F32)) for i in range(8)]

        consts = sem("consts_landed")
        band_built, band_stored, bias_landed = (
            sem("band_built"), sem("band_stored"), sem("bias_landed"))
        rel_ready, band_banks = sem("rel_ready"), sem("band_banks")
        half_ready, wp_landed, wp_hi_done, wp_lo_done = (
            sem("half_ready"), sem("wp_landed"), sem("wp_hi_done"), sem("wp_lo_done"))
        landed = [sem("panel_landed_even"), sem("panel_landed_odd")]
        hi_done, lo_done, panel_used = sem("panel_hi"), sem("panel_lo"), sem("panel_used")
        ident_landed, gain_landed = sem("ident_landed"), sem("norm1_gain_landed")
        first_x = [sem(f"first_x_block{b}") for b in range(NB)]
        masked, mask_row = sem("no_keys_masked"), sem("mask_row")
        x_landed = [sem("x_landed_even"), sem("x_landed_odd")]
        sumsq, ms_done, rstd_done, xn_done, nT = (
            sem("sumsq"), sem("mean_square"), sem("rstd_done"), sem("normalised"), sem("norm_T"))
        nhi, nlo = sem("norm_hi"), sem("norm_lo")
        zq, zkv = sem("z_q_banks"), sem("z_kv_banks")
        qcopied, kvcopied, ucopied = sem("q_copied"), sem("kv_copied"), sem("u_copied")
        qsq, qred, qms_done, qrs_done, qscaled = (
            sem("qk_squares"), sem("qk_reduced"), sem("qk_ms"), sem("qk_rstd"), sem("qk_scaled"))
        v_hi_done, v_split = sem("v_hi"), sem("first_v_split")
        qkn_done, kcarried, vcarried, vstaged, tqk, kstaged, qstaged = (
            sem("qk_normalised"), sem("k_carried"), sem("v_carried"), sem("v_staged"), sem("qk_T"),
            sem("k_staged"), sem("q_staged"))
        logits, scaled, maxed, neg_maxed, shifted, exped, summed, rden_done, pnorm = (
            sem("logits"), sem("scaled"), sem("row_maxed"), sem("neg_maxed"), sem("sink_shifted"),
            sem("exped"), sem("summed"), sem("rden_done"), sem("probs_normalised"))
        q_hi_done, k_hi_done, probsT_hi_done = (
            sem("q_T_hi"), sem("k_T_hi"), sem("probs_T_hi"))
        probs_T, probsT_copied, pv, attn_hi, attn_lo = (
            sem("probs_T"), sem("probsT_copied"), sem("pv"), sem("attn_hi"), sem("attn_lo"))
        level, edged, pooled, pool_hi, pool_lo, y_done, y_hi, y_lo, u_carried = (
            sem("pool_level"), sem("pool_edge"), sem("pooled"), sem("pool_hi"), sem("pool_lo"),
            sem("pool_y"), sem("pool_y_hi"), sem("pool_y_lo"), sem("u_carried"))
        tanhed, gated, glu_free, act_hi_done, act_lo_done = (
            sem("tanhed"), sem("gated"), sem("glu_banks_free"), sem("act_hi"), sem("act_lo"))
        down, down_added = sem("down_banks"), sem("down_added")
        p_landed, pT, pT_hi, pT_lo = sem("p_landed"), sem("p_T"), sem("p_T_hi"), sem("p_T_lo")
        pp, pp_copied = sem("proj_banks"), sem("proj_copied")
        gt, sig, ple_mul, ple_out = (
            sem("gate_banks"), sem("gate_tanh"), sem("ple_multiplied"), sem("ple_added"))
        out_stored, h_landed = sem("out_stored"), sem("h_landed")
        outp, out_added = sem("out_banks"), sem("out_added")

        CONSTS = 5 * 16
        HALF_SUMS = 3

        def iter_base(t):
            return Z_P + TILE_P * t

        def ffn_base(t, last):
            return iter_base(t) + OUT_P + (0 if last else Z_P)

        def norm2_no(t, last):
            return 3 * t + (1 if last else 2)

        def table(j):
            return bass.AP(scratch, j * PAIRS * P * BAND + P - 1,
                           [[BAND - 1, P], [P * BAND, PAIRS], [1, 2 * P]])

        LAG_NORM, LAG_T, LAG_PV = 1, 2, 3

        def unit_at(b, j, lag, flowing):
            c = j - lag
            if 0 <= c < PAIRS:
                return None if isinstance(b, int) and b == NB else (b, c)
            if c < 0 and flowing and not (isinstance(b, int) and b == 0):
                return b - 1, c + PAIRS
            return None

        def first_tile(s):
            return isinstance(s, int) and s == 0

        def y_bank(s, g):
            return g if first_tile(s) else 4 + g

        STEPS_IN_Z = {(7, 1): (0, 0), (8, 0): (0, 1), (8, 1): (0, 2), (9, 0): (0, 3), (9, 1): (1, 0)}
        STEPS_AFTER_Z = [(b, j) for b in range(NB) for j in range(PAIRS)
                         if (b, j) not in STEPS_IN_Z.values()]
        SUMS_AT = {(1, 1): ((0, 0),), (1, 3): ((1, 0), (1, 1)), (2, 1): ((2, 0),),
                   (2, 2): ((2, 1), (2, 2)), (3, 0): ((3, 0),), (3, 1): ((3, 1), (3, 2)),
                   (3, 2): ((3, 3),)}
        MEAN_AT = {(1, 2): 0, (2, 0): 1, (2, 3): 2, (3, 3): 3}
        REST_AT = {(1, 3): 0, (2, 1): 1, (3, 0): 2, (NB, 0): 3}

        def sum_level(engine, ops, s, g, n):
            before = s * 10 + g * (g + 1) // 2 + n
            pair = (sum_a, sum_b) if (g + 1) % 2 else (sum_b, sum_a)
            step = 1 << n
            lo = 2 * step - 1
            if n == 0:
                src = u[:, g, :]
                engine.wait_ge(ucopied, 4 * s + 4)
                engine.wait_ge(qred, 4 * s + 4)
                if not (isinstance(s, int) and s == 0 and g == 0):
                    engine.wait_ge(pool_lo, 4 * s + g)
            else:
                src = pair[(n - 1) % 2]
                engine.wait_ge(level, before)
            ops.tensor_tensor(pair[n % 2][:, lo:], src[:, lo:], src[:, lo - step:CARRY + T - step],
                              ALU.add).then_inc(level, 1)

        def no_less(value):
            return max(value, 0) if isinstance(value, int) else value

        def x_block(s, b):
            return x.rearrange("(s b p) d -> s b p d", b=NB, p=P)[s, b]

        block = ctx.enter_context(nc.Block())

        @block.sync
        def _(sp):
            for b in range(NB):
                sp.dma_start(h[:, b, :], x_block(0, b)).then_inc(first_x[b], 16)
                if b == 0:
                    sp.dma_start(ident[:, :], identity).then_inc(ident_landed, 16)

            def load(i, parity, halves):
                if not (isinstance(i, int) and i < 2):
                    sp.wait_ge(lo_done, i - 1)
                for half, src in enumerate(halves):
                    n = src.shape[1]
                    dst = raw[64 * half:64 * half + 64, parity, :].rearrange("p (k n) -> p k n", k=n)
                    sp.dma_start(dst, src).then_inc(landed[parity], 16)

            def rows(w, k0, k1, cols):
                v = w.rearrange("(k h p) n -> h p k n", h=2, p=64)
                return [v[half, :, k0:k1, cols] for half in range(2)]

            def load_z(at):
                for c in range(4):
                    load(at + c, c % 2, rows(w_in, 2 * c, 2 * c + 2, slice(0, QW)))
                for c in range(2):
                    load(at + 4 + c, c % 2, rows(w_in, 4 * c, 4 * c + 4, slice(QW, QW + 2 * KVW)))
                for g in range(NPOOL):
                    c0 = QW + 2 * KVW + g * P
                    load(at + 6 + g, g % 2, rows(w_in, 0, KC, slice(c0, c0 + P)))

            def load_x(s, b, n_norm):
                sp.wait_ge(nT, 8 * n_norm + 2 * b - 2)
                sp.dma_start(stage[:, b % 2, :], x_block(s, b)).then_inc(x_landed[b % 2], 16)

            def load_out(at, t, norm1):
                heads = w_out[0:QW, :].rearrange("(j c p) n -> j p c n", j=2, p=HEAD_DIM)
                for e in range(2):
                    cols = slice(e * T, (e + 1) * T)
                    for r in range(4):
                        src = ([heads[j, :, 2 * r:2 * r + 2, cols] for j in range(2)] if r < 2
                               else rows(w_out, 2 * r, 2 * r + 2, cols))
                        load(at + 4 * e + r, r % 2, src)
                        if norm1 and e == 0 and r == 1:
                            sp.wait_ge(probs_T, 16 * t + 16)
                            load_x(t + 1, 0, 3 * t + 1)
                            load_x(t + 1, 1, 3 * t + 1)
                        if norm1 and e == 1 and r == 0:
                            load_x(t + 1, 2, 3 * t + 1)
                            load_x(t + 1, 3, 3 * t + 1)

            def load_gate_up(at, m):
                for n, w in enumerate((w_gate, w_up)):
                    v = w.rearrange("(k h p) (m n) -> h p k m n", h=2, p=64, n=P)
                    load(at + n, n, [v[half, :, :, m, :] for half in range(2)])

            def load_ffn(at):
                first, chunk0 = 0, 0
                for g, nk in enumerate(GROUPS):
                    if g < 2:
                        with sp.Fori(0, 2) as it:
                            for c in range(4):
                                load_gate_up(at + first + 2 * c + it * 8, it * 4 + (chunk0 + c))
                    else:
                        for c in range(nk):
                            load_gate_up(at + first + 2 * c, chunk0 + c)
                    for e in range(2):
                        for r in range(nk // 2):
                            n = e * (nk // 2) + r
                            load(at + first + 2 * nk + n, n % 2,
                                 rows(w_down, chunk0 + 2 * r, chunk0 + 2 * r + 2,
                                      slice(e * T, (e + 1) * T)))
                    first += 3 * nk
                    chunk0 += nk

            def load_ple(at):
                for e in range(2):
                    load(at + e, e, rows(w_ple_proj, 0, KP, slice(e * T, (e + 1) * T)))
                for e in range(2):
                    for r in range(4):
                        load(at + PROJ_P + 4 * e + r, r % 2,
                             rows(w_ple_gate, 2 * r, 2 * r + 2, slice(e * T, (e + 1) * T)))

            load_z(0)
            with sp.Fori(0, LAST) as t:
                load_out(iter_base(t), t, True)
                load_z(iter_base(t) + OUT_P)
                load_ffn(ffn_base(t, False))
                load_ple(ffn_base(t, False) + FFN_P)
            load_out(iter_base(LAST), LAST, False)
            load_ffn(ffn_base(LAST, True))
            load_ple(ffn_base(LAST, True) + FFN_P)

        @block.gpsimd
        def _(pool):
            def alone(value):
                value = value if isinstance(value, int) else pool.to_reg(value)
                pool.wait_ge(half_ready, 1)
                return value

            def powers(n_norm, b):
                n = 4 * n_norm + b
                pool.wait_ge(sumsq, alone(n + 1))
                nc.gpsimd.tensor_scalar(out=ms[:, b:b + 1], in0=ss[:, b:b + 1], scalar1=1.0 / D,
                                        scalar2=EPS, op0=ALU.mult, op1=ALU.add).then_inc(ms_done, 1)
                pool.wait_ge(ms_done, n + 1)
                if not (isinstance(n_norm, int) and n < 4):
                    pool.wait_ge(xn_done, n - 3)
                nc.gpsimd.tensor_tensor(rstd[:, b:b + 1], ms[:, b:b + 1], minus_half[:, :],
                                        ALU.pow).then_inc(rstd_done, 1)

            def squares_qk(s, b):
                pool.wait_ge(kvcopied, 4 * s + b + 1)
                pool.wait_ge(qcopied, 4 * s + b + 1)
                if not (isinstance(s, int) and s == 0 and b == 0):
                    pool.wait_ge(qred, 4 * s + b)
                nc.gpsimd.tensor_tensor(qk_sq[:, :], qkv[:, b, 0:QKW], qkv[:, b, 0:QKW],
                                        ALU.mult).then_inc(qsq, 1)

            def powers_qk(s, b):
                pool.wait_ge(qred, alone(4 * s + b + 1))
                nc.gpsimd.tensor_scalar(out=qms[:, b, :], in0=qss[:, b, :], scalar1=1.0 / HEAD_DIM,
                                        scalar2=EPS, op0=ALU.mult, op1=ALU.add).then_inc(qms_done, 1)
                pool.wait_ge(qms_done, 4 * s + b + 1)
                nc.gpsimd.tensor_tensor(qrs[:, b, :], qms[:, b, :],
                                        minus_half[:, :].to_broadcast([P, NQ + NKV]),
                                        ALU.pow).then_inc(qrs_done, 1)

            def prep_qk(s):
                squares_qk(s, 0)
                squares_qk(s, 1)
                for b in range(NB):
                    powers_qk(s, b)
                    if b + 2 < NB:
                        squares_qk(s, b + 2)

            def normalise(n, c):
                pool.wait_ge(rden_done, n + 1)
                nc.gpsimd.tensor_tensor(scores[:, c, :, :], scores[:, c, :, :],
                                        rden[:, c % 2, :].unsqueeze(2).to_broadcast([P, 2, 2 * P]),
                                        ALU.mult).then_inc(pnorm, 1)

            def attention_step(s, b, j, flowing):
                at = unit_at(b, j, LAG_NORM, flowing)
                if at:
                    normalise(16 * s + 4 * at[0] + at[1], at[1])

            def pool_rest(s, g):
                pool.wait_ge(pool_hi, 4 * s + g + 1)
                nc.gpsimd.tensor_tensor(mix_lo[:, 4 + g, :], sum_a[:, CARRY:],
                                        mix_hi[:, 4 + g, :].bitcast(F32),
                                        ALU.subtract).then_inc(pool_lo, 1)

            def carry_u(s):
                pool.wait_ge(pool_lo, alone(4 * s + 4))
                nc.gpsimd.tensor_copy(u[:, :, 0:CARRY], u[:, :, T:T + CARRY]).then_inc(u_carried, 1)

            def act_rest(n, k):
                pool.wait_ge(act_hi_done, n + 1)
                nc.gpsimd.tensor_tensor(wide_lo[:, k, :], act_b[:, :],
                                        wide_hi[:, k, :].bitcast(F32),
                                        ALU.subtract).then_inc(act_lo_done, 1)

            def out_rows(t, e, b):
                pool.wait_ge(ple_out, alone(8 * t + 4 * e + b + 1))
                dst = out.rearrange("(t b p) d -> t b p d", b=NB, p=P)[t, b, :, e * T:(e + 1) * T]
                pool.dma_start(dst, h[:, b, e * T:(e + 1) * T]).then_inc(out_stored, 16)

            def load_h(t):
                pool.wait_ge(xn_done, 4)
                pool.wait_ge(out_stored, alone(128 * t + 32))
                for b in range(NB):
                    pool.dma_start(h[:, b, :], x_block(t, b)).then_inc(h_landed, 16)

            def out_section(t, norm1):
                if norm1:
                    powers(3 * t + 1, 0)
                    powers(3 * t + 1, 1)
                    pool.wait_ge(nT, alone(24 * t + 12))
                load_h(t)
                if norm1:
                    powers(3 * t + 1, 2)
                    powers(3 * t + 1, 3)

            def ffn_section(t, last):
                s = t + 1
                n0 = NCH * t
                for g in range(2):
                    with pool.Fori(0, 2) as it:
                        for beat in range(8):
                            if not last and beat:
                                attention_step(s, it + 2 * g, beat - 1, False)
                            if beat % 2:
                                act_rest(n0 + 8 * g + 4 * it + beat // 2, 4 * it + beat // 2)
                if last:
                    pool.wait_ge(pT, alone(2 * t))
                else:
                    pool.wait_ge(vstaged, alone(4 * s + 4))
                for b in range(NB):
                    src = p.rearrange("(t b p) d -> t b p d", b=NB, p=P)[t, b]
                    pool.dma_start(p_rows[:, b, :], src).then_inc(p_landed, 16)
                for beat in range(12):
                    if not last and beat % 2 and beat < 8:
                        pool_rest(s, beat // 2)
                    if not last and beat == 8:
                        carry_u(s)
                    if beat % 2:
                        act_rest(n0 + 16 + beat // 2, beat // 2)

            def ple_section(t, last):
                for b in range(NB):
                    powers(norm2_no(t, last) + 1, b)
                for e in range(2):
                    for b in range(NB):
                        out_rows(t, e, b)

            nc.gpsimd.memset(minus_half[:, :], -0.5).then_inc(half_ready, 1)
            pool.wait_ge(half_ready, 1)
            nc.gpsimd.memset(kT_hi[:, :, :].bitcast(F32), 0.0).then_inc(sig, 8)
            nc.gpsimd.memset(kT_lo[:, :, :].bitcast(F32), 0.0).then_inc(ple_mul, 1)
            nc.gpsimd.memset(v_whole[:, :, :], 0.0).then_inc(act_lo_done, 1)
            pool.wait_ge(act_lo_done, 1)
            nc.gpsimd.memset(rel_rows[N_BUCKETS:N_BUCKETS + 1, :, :], MASKED).then_inc(mask_row, 1)
            pool.wait_ge(mask_row, 1)
            nc.gpsimd.memset(u[:, :, 0:CARRY], 0.0).then_inc(u_carried, 1)
            pool.dma_start(sink[:, :, :],
                           bass.AP(sinks.tensor, sinks.offset, [[0, P], [PAIRS, 2], [1, PAIRS]])
                           ).then_inc(out_stored, 16)
            pool.dma_start(edge_sb[:, :, :],
                           bass.AP(edge.tensor, edge.offset, [[0, P], [CARRY, NPOOL], [1, CARRY]])
                           ).then_inc(out_stored, 16)
            for b in range(NB):
                powers(0, b)
            pool.wait_ge(band_built, NQ)
            pool.dma_start(scratch[:, :].rearrange("h (p s) -> p h s", s=BAND),
                           band[:, :, :]).then_inc(band_stored, 16)
            pool.wait_ge(band_stored, 16)
            for j in range(2):
                pool.dma_start(bias[:, :, j, :], table(j)).then_inc(bias_landed, 16)
            for b in range(NB):
                powers_qk(0, b)
            for b, j in [*STEPS_IN_Z.values(), *STEPS_AFTER_Z, (NB, 0)]:
                attention_step(0, b, j, True)
                if (b, j) in REST_AT:
                    pool_rest(0, REST_AT[b, j])
                for g, n in SUMS_AT.get((b, j), ()):
                    sum_level(pool, nc.gpsimd, 0, g, n)
            carry_u(0)

            with pool.Fori(0, LAST) as t:
                out_section(t, True)
                for b in range(NB):
                    powers(3 * t + 2, b)
                prep_qk(t + 1)
                ffn_section(t, False)
                ple_section(t, False)
            out_section(LAST, False)
            for b in range(NB):
                powers(3 * LAST + 1, b)
            ffn_section(LAST, True)
            ple_section(LAST, True)
            pool.wait_ge(out_stored, 128 * NT + 32)

        @block.scalar
        def _(act):
            def bcast(v, n):
                return v.rearrange("(o n) -> o n", o=1).to_broadcast([P, n])

            act.dma_start(gains[:, 0, :], bcast(g_attn, D)).then_inc(gain_landed, 16)

            def split(i, parity):
                act.wait_ge(landed[parity], 16 * (i - parity) + 32)
                if not (isinstance(i, int) and i < 2):
                    act.wait_ge(panel_used, i - 1)
                nc.scalar.activation(w_hi[:, parity, :], raw[:, parity, :], ACT.Copy).then_inc(hi_done, 1)

            def sum_squares(n_norm, b, src):
                n = 4 * n_norm + b
                if not (isinstance(n_norm, int) and n == 0):
                    act.wait_ge(sumsq, n)
                if not (isinstance(n_norm, int) and n < 4):
                    act.wait_ge(ms_done, n - 3)
                nc.scalar.activation(squares[:, :], src, ACT.Square,
                                     accum_out=ss[:, b:b + 1]).then_inc(sumsq, 1)

            def norm_hi(n_norm, b, dst):
                for e in range(2):
                    n = 8 * n_norm + 2 * b + e
                    act.wait_ge(nT, n + 1)
                    src = bank[4 + (2 * b + e) % 4][:, :].rearrange("p (k t) -> p k t", k=4)
                    nc.scalar.activation(dst[:, 4 * e:4 * e + 4, b * P:(b + 1) * P], src,
                                         ACT.Copy).then_inc(nhi, 1)

            def copy_q(s, b, at):
                if isinstance(s, int) and b == 0:
                    act.wait_ge(band_banks, NQ)
                if b < HALF_SUMS:
                    act.wait_ge(zq, HALF_SUMS * s + b + 1)
                else:
                    act.wait_ge(panel_used, at + 4)
                nc.scalar.activation(qkv[:, b, 0:QW], bank[b][:, :], ACT.Copy).then_inc(qcopied, 1)

            def copy_u(s, g, at):
                act.wait_ge(panel_used, at + 7 + g)
                if g == 0:
                    act.wait_ge(u_carried, s + 1)
                nc.scalar.activation(u[:, g, CARRY:], bank[g][:, :], ACT.Copy).then_inc(ucopied, 1)

            def stage_q(s, b):
                n = 4 * s + b
                act.wait_ge(tqk, 2 * n + 1)
                act.wait_ge(logits, 16 * s + 4 * b)
                nc.scalar.activation(qT_hi[:, :, :].rearrange("p c q -> p (c q)"), bank[7][:, :],
                                     ACT.Copy).then_inc(q_hi_done, 1)
                act.wait_ge(tqk, 2 * n + 2)
                act.wait_ge(kcarried, n + 1)
                for j in range(NKV):
                    rows = slice(64 * j, 64 * j + 64)
                    last = nc.scalar.activation(kT_hi[rows, j, P:2 * P], bank[5][rows, 0:P], ACT.Copy)
                last.then_inc(k_hi_done, 1)

            def exps(n, c):
                i = c % 2
                act.wait_ge(neg_maxed, n + 1)
                act.wait_ge(summed, no_less(n - 1))
                for j in range(2):
                    nc.scalar.activation(scores[:, c, j, :], scores[:, c, j, :], ACT.Exp,
                                         bias=neg_max[:, i, j:j + 1], accum_out=row_sum[:, i, j:j + 1])
                act.wait_ge(shifted, n + 1)
                nc.scalar.activation(sink_exp[:, i, :], sink_shift[:, i, :], ACT.Exp).then_inc(exped, 1)

            def copy_probsT(s, n, c):
                act.wait_ge(probs_T, n + 1)
                if first_tile(s):
                    act.wait_ge(pv, no_less(n - 1))
                    nc.scalar.activation(probsT_whole[:, c % 2, :, :].rearrange("p a b -> p (a b)"),
                                         bank[5][:, :], ACT.Copy).then_inc(probsT_copied, 1)
                else:
                    act.wait_ge(pv, n)
                    nc.scalar.activation(probsT_hi[:, :, :].rearrange("p a b -> p (a b)"),
                                         bank[5][:, :], ACT.Copy).then_inc(probsT_hi_done, 1)

            def attention_hi(n, b, c):
                act.wait_ge(pv, n + 1)
                for j in range(2):
                    rows = slice(64 * j, 64 * j + 64)
                    last = nc.scalar.activation(mix_hi[rows, c, bass.ts(b, P)],
                                                bank[6][rows, j * P:(j + 1) * P], ACT.Copy)
                last.then_inc(attn_hi, 1)

            def attention_step(s, b, j, flowing):
                at = unit_at(b, j, LAG_PV, flowing)
                if at:
                    attention_hi(16 * s + 4 * at[0] + at[1], *at)
                at = unit_at(b, j, LAG_T, flowing)
                if at:
                    copy_probsT(s, 16 * s + 4 * at[0] + at[1], at[1])
                at = unit_at(b, j, 0, flowing)
                if at:
                    exps(16 * s + 4 * at[0] + at[1], at[1])

            def pooled_hi(s, g):
                act.wait_ge(pooled, 4 * s + g + 1)
                nc.scalar.activation(mix_hi[:, 4 + g, :], sum_a[:, CARRY:], ACT.Copy).then_inc(pool_hi, 1)

            def pool_y_hi(s, g):
                act.wait_ge(y_done, 4 * s + g + 1)
                nc.scalar.activation(mix_hi[:, 4 + g, :], bank[y_bank(s, g)][:, :], ACT.Copy,
                                     scale=scale_sb[:, g:g + 1]).then_inc(y_hi, 1)

            def tanh_gate(n, i, parity):
                act.wait_ge(panel_used, i + 1)
                act.wait_ge(glu_free, n + 2)
                nc.scalar.activation(act_a[:, :], bank[2 * parity][:, :], ACT.Tanh,
                                     scale=0.5).then_inc(tanhed, 1)

            def p_hi_part(t, kk):
                act.wait_ge(pT, 2 * t + kk + 1)
                nc.scalar.activation(p_hi[:, kk, :], bank[4 + kk][:, :], ACT.Copy).then_inc(pT_hi, 1)

            def ffn_section(t, last):
                at, s, n0 = ffn_base(t, last), t + 1, NCH * t
                first = 0
                for g in range(2):
                    with act.Fori(0, 2) as it:
                        for beat in range(8):
                            i = at + first + beat + it * 8
                            split(i + 1, (beat + 1) % 2)
                            if not last and beat == 0:
                                stage_q(s, it + 2 * g)
                            if not last and beat:
                                attention_step(s, it + 2 * g, beat - 1, False)
                            if beat % 2:
                                tanh_gate(n0 + 8 * g + 4 * it + beat // 2, i - 1, beat // 2 % 2)
                    for n in range(8):
                        split(at + first + 16 + n + 1, (n + 1) % 2)
                    first += 24
                for beat in range(12):
                    i = at + first + beat
                    split(i + 1, (beat + 1) % 2)
                    if not last and beat % 2 and beat < 8:
                        pooled_hi(s, beat // 2)
                    if not last and beat % 2 and 2 < beat < 10:
                        pool_y_hi(s, beat // 2 - 1)
                    if beat >= 10:
                        p_hi_part(t, beat - 10)
                    if beat % 2:
                        tanh_gate(n0 + 16 + beat // 2, i - 1, beat // 2 % 2)
                for n in range(6):
                    split(at + first + 12 + n + 1, (n + 1) % 2)

            def copy_proj(t, e, b, i):
                if b < HALF_SUMS:
                    act.wait_ge(pp, 2 * HALF_SUMS * t + HALF_SUMS * e + b + 1)
                else:
                    act.wait_ge(panel_used, i + 1)
                nc.scalar.activation(proj[:, b, e * T:(e + 1) * T], bank[b][:, :],
                                     ACT.Copy).then_inc(pp_copied, 1)

            def ple_section(t, last):
                at = ffn_base(t, last) + FFN_P
                n3 = norm2_no(t, last) + 1
                for b in range(NB):
                    if b == 3:
                        split(at + 1, 1)
                    act.wait_ge(down_added, 24 * t + 20 + b + 1)
                    sum_squares(n3, b, h[:, b, :])
                norm_hi(n3, 0, hn_hi)
                for b in range(NB):
                    copy_proj(t, 0, b, at)
                norm_hi(n3, 1, hn_hi)
                split(at + 2, 0)
                norm_hi(n3, 2, hn_hi)
                for b in range(NB):
                    copy_proj(t, 1, b, at + 1)
                norm_hi(n3, 3, hn_hi)
                for e in range(2):
                    for r in range(4):
                        i = at + PROJ_P + 4 * e + r
                        if not (last and e == 1 and r == 3):
                            split(i + 1, (r + 1) % 2)
                    for b in range(NB):
                        if b < HALF_SUMS:
                            act.wait_ge(gt, 2 * HALF_SUMS * t + HALF_SUMS * e + b + 1)
                        else:
                            act.wait_ge(panel_used, i + 1)
                        n = 8 * t + 4 * e + b
                        buf = (act_a, act_b)[b % 2]
                        if e or b >= 2:
                            act.wait_ge(ple_out, n - 1)
                        nc.scalar.activation(buf[:, :], bank[4 * e + b][:, :], ACT.Tanh,
                                             scale=0.5).then_inc(sig, 1)
                        if e and b == 1 and not last:
                            split(i + 2, 1)

            def out_section(t, norm1):
                at = iter_base(t)
                n1 = 3 * t + 1
                for beat in range(8):
                    if beat:
                        split(at + beat + 1, (beat + 1) % 2)
                    if norm1 and beat == 2:
                        act.wait_ge(ple_mul, 8 * t + 1)
                        norm_hi(n1, 0, wide_hi)
                        norm_hi(n1, 1, wide_hi)
                    if norm1 and beat == 4:
                        norm_hi(n1, 3, wide_hi)
                    if norm1:
                        for b in {0: (0, 1), 2: (2,), 3: (3,)}.get(beat, ()):
                            act.wait_ge(x_landed[b % 2], 32 * t + 16 * (b // 2 + 1))
                            sum_squares(n1, b, stage[:, b % 2, :])
                    if norm1 and beat == 3:
                        norm_hi(n1, 2, wide_hi)

            def step_of_first(b, j):
                if j == 3 and b + 1 < NB:
                    stage_q(0, b + 1)
                attention_step(0, b, j, True)
                if (b, j) in MEAN_AT:
                    pooled_hi(0, MEAN_AT[b, j])

            def squares_of_first(b):
                act.wait_ge(kvcopied, b + 1)
                nc.scalar.activation(first_sq[:, b, :], qkv[:, b, 0:QKW], ACT.Square).then_inc(qsq, 1)

            def z_section(s, at, n2):
                for beat in range(10):
                    split(at + beat + 1, (beat + 1) % 2)
                    if n2 is not None and beat < 2:
                        for b in (2 * beat, 2 * beat + 1):
                            act.wait_ge(out_added, 8 * (s - 1) + 4 + b + 1)
                            sum_squares(n2, b, h[:, b, :])
                    if n2 is not None and beat == 1:
                        act.wait_ge(band_stored, 16)
                    if n2 is not None:
                        for b in {1: (0,), 2: (1, 2), 3: (3,)}.get(beat, ()):
                            norm_hi(n2, b, hn_hi)
                    if beat == 4:
                        for b in range(NB):
                            copy_q(s, b, at)
                    if 7 <= beat:
                        copy_u(s, beat - 7, at)
                    if n2 is None and beat == 6:
                        act.wait_ge(bias_landed, 32)
                        for b in range(NB):
                            squares_of_first(b)
                    if n2 is None and beat == 7:
                        act.wait_ge(consts, CONSTS)
                        act.wait_ge(out_stored, 32)
                        stage_q(0, 0)
                    if n2 is None:
                        for half in range(2):
                            if (beat, half) in STEPS_IN_Z:
                                step_of_first(*STEPS_IN_Z[beat, half])
                copy_u(s, 3, at)

            def load_constants():
                act.dma_start(rel_sb[:, :], rel_bias).then_inc(consts, 16)
                act.dma_start(onehot_sb[:, :], onehot).then_inc(consts, 16)
                act.dma_start(scale_sb[:, :], pool_scale.rearrange("(g p) -> p g", p=P),
                              allow_slow_non_contiguous=True).then_inc(consts, 16)
                for n, g in ((1, g_ffn), (2, g_ple)):
                    act.dma_start(gains[:, n, :], bcast(g, D)).then_inc(consts, 16)
                act.dma_start(gqk[:, 0:QW].rearrange("p (h d) -> p h d", d=HEAD_DIM),
                              bass.AP(g_q.tensor, g_q.offset, [[0, P], [0, NQ], [1, HEAD_DIM]])
                              ).then_inc(wp_landed, 16)
                act.dma_start(gqk[:, QW:QKW].rearrange("p (h d) -> p h d", d=HEAD_DIM),
                              bass.AP(g_k.tensor, g_k.offset, [[0, P], [0, NKV], [1, HEAD_DIM]])
                              ).then_inc(wp_landed, 16)
                act.dma_start(act_a[:, :].rearrange("p (g d) -> p g d", g=NPOOL),
                              w_pool.rearrange("g c d -> c g d")).then_inc(wp_landed, 16)

            for b in range(NB):
                act.wait_ge(first_x[b], 16)
                sum_squares(0, b, h[:, b, :])
                if b == 1:
                    load_constants()
                if b == 2:
                    split(0, 0)
                if b:
                    norm_hi(0, b - 1, wide_hi)
            norm_hi(0, 3, wide_hi)
            act.wait_ge(wp_landed, 48)
            nc.scalar.activation(wp_hi[:, :, :].rearrange("p g d -> p (g d)"), act_a[:, :],
                                 ACT.Copy).then_inc(wp_hi_done, 1)
            z_section(0, 0, None)
            split(Z_P + 1, 1)
            for b, j in STEPS_AFTER_Z:
                step_of_first(b, j)
            for g in range(NPOOL):
                attention_step(0, NB, g, True)
                pool_y_hi(0, g)

            with act.Fori(0, LAST) as t:
                out_section(t, True)
                z_section(t + 1, iter_base(t) + OUT_P, 3 * t + 2)
                ffn_section(t, False)
                ple_section(t, False)
            out_section(LAST, False)
            for b in range(NB):
                act.wait_ge(out_added, 8 * LAST + 4 + b + 1)
                sum_squares(3 * LAST + 1, b, h[:, b, :])
                if b:
                    norm_hi(3 * LAST + 1, b - 1, hn_hi)
            norm_hi(3 * LAST + 1, 3, hn_hi)
            ffn_section(LAST, True)
            ple_section(LAST, True)

        @block.vector
        def _(dve):
            def split(i, parity):
                dve.wait_ge(hi_done, i + 1)
                nc.vector.tensor_tensor(w_lo[:, parity, :], raw[:, parity, :],
                                        w_hi[:, parity, :].bitcast(F32),
                                        ALU.subtract).then_inc(lo_done, 1)

            def normalise(n_norm, b, src, gain):
                n = 4 * n_norm + b
                dve.wait_ge(rstd_done, n + 1)
                if not (isinstance(n_norm, int) and n < 2):
                    dve.wait_ge(nT, 2 * n - 2)
                nc.vector.scalar_tensor_tensor(out=stage[:, b % 2, :], in0=src, scalar=rstd[:, b:b + 1],
                                               in1=gains[:, gain, :], op0=ALU.mult,
                                               op1=ALU.mult).then_inc(xn_done, 1)

            def norm_lo(n_norm, b, hi, lo):
                for e in range(2):
                    dve.wait_ge(nhi, 8 * n_norm + 2 * b + e + 1)
                    src = bank[4 + (2 * b + e) % 4][:, :].rearrange("p (k t) -> p k t", k=4)
                    at = (slice(None), slice(4 * e, 4 * e + 4), slice(b * P, (b + 1) * P))
                    nc.vector.tensor_tensor(lo[at], src, hi[at].bitcast(F32),
                                            ALU.subtract).then_inc(nlo, 1)

            def copy_kv(s, b, at):
                if b < HALF_SUMS:
                    dve.wait_ge(zkv, HALF_SUMS * s + b + 1)
                else:
                    dve.wait_ge(panel_used, at + 6)
                nc.vector.tensor_copy(qkv[:, b, QW:], bank[4 + b][:, 0:2 * KVW]).then_inc(kvcopied, 1)

            def qk_mean(s, b, src=qk_sq):
                n = 4 * s + b
                heads = NQ + NKV
                dve.wait_ge(qsq, n + 1)
                nc.vector.tensor_reduce(out=qss[:, b, :],
                                        in_=src[:, :].rearrange("p (h d) -> p h d", h=heads),
                                        axis=AX.X, op=ALU.add).then_inc(qred, 1)

            def qk_scale(s, b):
                dve.wait_ge(qrs_done, 4 * s + b + 1)
                v = qkv[:, b, 0:QKW].rearrange("p (h d) -> p h d", d=HEAD_DIM)
                nc.vector.tensor_tensor(v, v, qrs[:, b, :].unsqueeze(2).to_broadcast([P, NQ + NKV, HEAD_DIM]),
                                        ALU.mult).then_inc(qscaled, 1)

            def qk_gain(s, b):
                n = 4 * s + b
                dve.wait_ge(qscaled, n + 1)
                dve.wait_ge(tqk, 2 * n)
                q = qkv[:, b, 0:QW].rearrange("p (j c d) -> p c j d", j=2, d=HEAD_DIM)
                nc.vector.tensor_tensor(qkn[:, 0:QW].rearrange("p (c j d) -> p c j d", j=2, d=HEAD_DIM), q,
                                        gqk[:, 0:QW].rearrange("p (c j d) -> p c j d", j=2, d=HEAD_DIM),
                                        ALU.mult)
                nc.vector.tensor_tensor(qkn[:, QW:QKW], qkv[:, b, QW:QKW], gqk[:, QW:QKW],
                                        ALU.mult).then_inc(qkn_done, 1)

            def stage_k(s, b):
                n = 4 * s + b
                dve.wait_ge(logits, 4 * n)
                dve.wait_ge(kstaged, n)
                nc.vector.tensor_copy(kT_hi[:, :, 0:P], kT_hi[:, :, P:2 * P])
                nc.vector.tensor_copy(kT_lo[:, :, 0:P], kT_lo[:, :, P:2 * P]).then_inc(kcarried, 1)
                dve.wait_ge(q_hi_done, n + 1)
                nc.vector.tensor_tensor(qT_lo[:, :, :].rearrange("p c q -> p (c q)"), bank[7][:, :],
                                        qT_hi[:, :, :].rearrange("p c q -> p (c q)").bitcast(F32),
                                        ALU.subtract).then_inc(qstaged, 1)
                dve.wait_ge(k_hi_done, n + 1)
                dve.wait_ge(kcarried, n + 1)
                for j in range(NKV):
                    rows = slice(64 * j, 64 * j + 64)
                    last = nc.vector.tensor_tensor(kT_lo[rows, j, P:2 * P], bank[5][rows, 0:P],
                                                   kT_hi[rows, j, P:2 * P].bitcast(F32), ALU.subtract)
                last.then_inc(kstaged, 1)

            def split_v(b, done):
                nc.vector.tensor_copy(v_hi[:, 1, :], qkv[:, b, QKW:]).then_inc(v_hi_done, 1)
                dve.wait_ge(v_hi_done, done + 1)
                return nc.vector.tensor_tensor(v_lo[:, 1, :], qkv[:, b, QKW:],
                                               v_hi[:, 1, :].bitcast(F32), ALU.subtract)

            def stage_v(s, b):
                n = 4 * s + b
                dve.wait_ge(pv, 4 * n)
                dve.wait_ge(vstaged, n)
                if first_tile(s):
                    nc.vector.tensor_copy(v_whole[:, 0, :], v_whole[:, 1, :]).then_inc(vcarried, 1)
                    dve.wait_ge(vcarried, n + 1)
                    nc.vector.tensor_copy(v_whole[:, 1, :], qkv[:, b, QKW:]).then_inc(vstaged, 1)
                else:
                    nc.vector.tensor_copy(v_hi[:, 0, :], v_hi[:, 1, :])
                    nc.vector.tensor_copy(v_lo[:, 0, :], v_lo[:, 1, :]).then_inc(vcarried, 1)
                    dve.wait_ge(vcarried, n + 1)
                    split_v(b, n - 3).then_inc(vstaged, 1)

            def probsT_rest(n):
                dve.wait_ge(probsT_hi_done, n - 15)
                nc.vector.tensor_tensor(probsT_lo[:, :, :].rearrange("p a b -> p (a b)"), bank[5][:, :],
                                        probsT_hi[:, :, :].rearrange("p a b -> p (a b)").bitcast(F32),
                                        ALU.subtract).then_inc(probsT_copied, 1)

            def softmax_in(n, c, halves):
                i, first = c % 2, (2 - halves) * P
                dve.wait_ge(logits, n + 1)
                dve.wait_ge(probs_T, no_less(n - 3))
                nc.vector.scalar_tensor_tensor(
                    out=scores[:, c, :, first:],
                    in0=bank[4][:, :].rearrange("p (j k) -> p j k", j=2)[:, :, first:],
                    scalar=HEAD_DIM ** -0.5, in1=bias[:, c, :, first:],
                    op0=ALU.mult, op1=ALU.add).then_inc(scaled, 1)
                dve.wait_ge(scaled, n + 1)
                nc.vector.tensor_reduce(out=row_max[:, i, :], in_=scores[:, c, :, :], axis=AX.X,
                                        op=ALU.max).then_inc(maxed, 1)
                dve.wait_ge(maxed, n + 1)
                nc.vector.scalar_tensor_tensor(out=neg_max[:, i, :], in0=row_max[:, i, :], scalar=-1.0,
                                               in1=neg_sink[:, :, c], op0=ALU.mult,
                                               op1=ALU.min).then_inc(neg_maxed, 1)
                dve.wait_ge(neg_maxed, n + 1)
                nc.vector.tensor_tensor(sink_shift[:, i, :], sink[:, :, c], neg_max[:, i, :],
                                        ALU.add).then_inc(shifted, 1)

            def softmax_den(n, c):
                i = c % 2
                dve.wait_ge(exped, n + 1)
                nc.vector.tensor_tensor(den[:, i, :], row_sum[:, i, :], sink_exp[:, i, :],
                                        ALU.add).then_inc(summed, 1)
                dve.wait_ge(summed, n + 1)
                dve.wait_ge(pnorm, no_less(n - 1))
                nc.vector.reciprocal(rden[:, i, :], den[:, i, :]).then_inc(rden_done, 1)

            def attention_rest(n, b, c):
                dve.wait_ge(attn_hi, n + 1)
                for j in range(2):
                    rows = slice(64 * j, 64 * j + 64)
                    last = nc.vector.tensor_tensor(mix_lo[rows, c, bass.ts(b, P)],
                                                   bank[6][rows, j * P:(j + 1) * P],
                                                   mix_hi[rows, c, bass.ts(b, P)].bitcast(F32),
                                                   ALU.subtract)
                last.then_inc(attn_lo, 1)

            def attention_step(s, b, j, flowing, next_keys=False):
                at = unit_at(b, j, 0, flowing)
                if at:
                    halves = 1 if isinstance(s, int) and isinstance(b, int) and s == b == 0 else 2
                    softmax_in(16 * s + 4 * at[0] + at[1], at[1], halves)
                if next_keys:
                    stage_k(s, b + 1)
                at = unit_at(b, j, LAG_NORM, flowing)
                if at:
                    softmax_den(16 * s + 4 * at[0] + at[1], at[1])
                at = unit_at(b, j, LAG_T, flowing)
                if at and not first_tile(s):
                    probsT_rest(16 * s + 4 * at[0] + at[1])
                at = unit_at(b, j, LAG_PV, flowing)
                if at:
                    attention_rest(16 * s + 4 * at[0] + at[1], *at)
                if j == 2 and not (isinstance(b, int) and b == NB):
                    stage_v(s, b)

            def pool_mean(s, g):
                dve.wait_ge(level, 10 * s + (g + 1) * (g + 2) // 2)
                if first_tile(s):
                    nc.vector.tensor_tensor(sum_a[:, CARRY:2 * CARRY], sum_a[:, CARRY:2 * CARRY],
                                            edge_sb[:, g, :], ALU.mult).then_inc(edged, 1)
                    dve.wait_ge(edged, g + 1)
                nc.vector.scalar_tensor_tensor(out=sum_a[:, CARRY:], in0=sum_a[:, CARRY:],
                                               scalar=1.0 / POOL_SIZES[g], in1=u[:, g, CARRY:],
                                               op0=ALU.mult, op1=ALU.subtract).then_inc(pooled, 1)

            def pool_y_rest(s, g):
                dve.wait_ge(y_hi, 4 * s + g + 1)
                nc.vector.scalar_tensor_tensor(out=mix_lo[:, 4 + g, :], in0=bank[y_bank(s, g)][:, :],
                                               scalar=scale_sb[:, g:g + 1],
                                               in1=mix_hi[:, 4 + g, :].bitcast(F32), op0=ALU.mult,
                                               op1=ALU.subtract).then_inc(y_lo, 1)

            def gate_in(n, parity):
                dve.wait_ge(tanhed, n + 1)
                nc.vector.scalar_tensor_tensor(out=act_a[:, :], in0=act_a[:, :], scalar=1.0,
                                               in1=bank[2 * parity][:, :], op0=ALU.add,
                                               op1=ALU.mult).then_inc(gated, 1)

            def gate_up(n, i, parity, k):
                dve.wait_ge(panel_used, i + 1)
                dve.wait_ge(gated, n + 1)
                dve.wait_ge(act_lo_done, n + 1)
                nc.vector.scalar_tensor_tensor(out=act_b[:, :], in0=act_a[:, :], scalar=0.5,
                                               in1=bank[2 * parity + 1][:, :], op0=ALU.mult,
                                               op1=ALU.mult).then_inc(glu_free, 1)
                dve.wait_ge(glu_free, n + 3)
                nc.vector.tensor_copy(wide_hi[:, k, :], act_b[:, :]).then_inc(act_hi_done, 1)

            def add_down(t, g, e, i):
                for b in range(NB):
                    if b < HALF_SUMS:
                        dve.wait_ge(down, 6 * HALF_SUMS * t + HALF_SUMS * (2 * g + e) + b + 1)
                    else:
                        dve.wait_ge(panel_used, i + 1)
                    v = h[:, b, e * T:(e + 1) * T]
                    nc.vector.tensor_tensor(v, bank[4 * e + b][:, :], v, ALU.add).then_inc(down_added, 1)

            def p_lo_part(t, kk):
                dve.wait_ge(pT_hi, 2 * t + kk + 1)
                nc.vector.tensor_tensor(p_lo[:, kk, :], bank[4 + kk][:, :], p_hi[:, kk, :].bitcast(F32),
                                        ALU.subtract).then_inc(pT_lo, 1)

            def ffn_section(t, last):
                at, s, n0 = ffn_base(t, last), t + 1, NCH * t
                first = 0
                for g, nk in enumerate(GROUPS):
                    if g < 2:
                        with dve.Fori(0, 2) as it:
                            for beat in range(8):
                                i = at + first + beat + it * 8
                                if not last and beat == 0:
                                    qk_gain(s, it + 2 * g)
                                split(i + 1, (beat + 1) % 2)
                                if not last and beat == 0:
                                    stage_k(s, it + 2 * g)
                                if not last and beat:
                                    attention_step(s, it + 2 * g, beat - 1, False)
                                if beat % 2:
                                    c = beat // 2
                                    n = n0 + 8 * g + c + 4 * it
                                    gate_in(n, c % 2)
                                    gate_up(n, i, c % 2, 4 * it + c)
                    else:
                        for beat in range(12):
                            i = at + first + beat
                            split(i + 1, (beat + 1) % 2)
                            if not last and beat < 8:
                                if beat % 2:
                                    pool_mean(s, beat // 2)
                                else:
                                    for n in range(beat // 2 + 1):
                                        sum_level(dve, nc.vector, s, beat // 2, n)
                            if not last and beat % 2 and 2 < beat < 10:
                                pool_y_rest(s, beat // 2 - 1)
                            if beat >= 10:
                                p_lo_part(t, beat - 10)
                            if beat % 2:
                                c = beat // 2
                                n = n0 + 16 + c
                                gate_in(n, c % 2)
                                gate_up(n, i, c % 2, c)
                    for n in range(nk):
                        i = at + first + 2 * nk + n
                        split(i + 1, (n + 1) % 2)
                        if n % (nk // 2) == nk // 2 - 1:
                            add_down(t, g, n // (nk // 2), i)
                    first += 3 * nk

            def ple_section(t, last):
                at = ffn_base(t, last) + FFN_P
                n3 = norm2_no(t, last) + 1
                if not last:
                    dve.wait_ge(probs_T, 16 * t + 32)
                normalise(n3, 0, h[:, 0, :], 2)
                split(at + 1, 1)
                normalise(n3, 1, h[:, 1, :], 2)
                normalise(n3, 2, h[:, 2, :], 2)
                norm_lo(n3, 0, hn_hi, hn_lo)
                normalise(n3, 3, h[:, 3, :], 2)
                norm_lo(n3, 1, hn_hi, hn_lo)
                split(at + 2, 0)
                norm_lo(n3, 2, hn_hi, hn_lo)
                norm_lo(n3, 3, hn_hi, hn_lo)
                for e in range(2):
                    for r in range(4):
                        if not (last and e == 1 and r == 3):
                            split(at + PROJ_P + 4 * e + r + 1, (r + 1) % 2)
                    for b in range(NB):
                        n = 8 * t + 4 * e + b
                        buf = (act_a, act_b)[b % 2]
                        dve.wait_ge(sig, n + 9)
                        dve.wait_ge(pp_copied, 8 * t + 4 * e + b + 1)
                        nc.vector.scalar_tensor_tensor(out=buf[:, :], in0=buf[:, :], scalar=1.0,
                                                       in1=proj[:, b, e * T:(e + 1) * T], op0=ALU.add,
                                                       op1=ALU.mult).then_inc(ple_mul, 1)
                        dve.wait_ge(ple_mul, n + 2)
                        v = h[:, b, e * T:(e + 1) * T]
                        nc.vector.scalar_tensor_tensor(out=v, in0=buf[:, :], scalar=0.5, in1=v,
                                                       op0=ALU.mult, op1=ALU.add).then_inc(ple_out, 1)
                        if e and b == 1 and not last:
                            split(at + PROJ_P + 9, 1)

            def add_out(t, e, at):
                for b in range(NB):
                    if b < HALF_SUMS:
                        dve.wait_ge(outp, 2 * HALF_SUMS * t + HALF_SUMS * e + b + 1)
                    else:
                        dve.wait_ge(panel_used, at + 4 * e + 4)
                    v = h[:, b, e * T:(e + 1) * T]
                    nc.vector.tensor_tensor(v, bank[4 * e + b][:, :], v, ALU.add).then_inc(out_added, 1)

            def out_section(t, norm1):
                at = iter_base(t)
                n1 = 3 * t + 1
                for beat in range(8):
                    if beat:
                        split(at + beat + 1, (beat + 1) % 2)
                    if norm1 and beat == 2:
                        norm_lo(n1, 0, wide_hi, wide_lo)
                        norm_lo(n1, 1, wide_hi, wide_lo)
                    if norm1 and beat == 4:
                        norm_lo(n1, 3, wide_hi, wide_lo)
                    if norm1 and beat in (1, 3):
                        normalise(n1, beat - 1, stage[:, 0, :], 0)
                        normalise(n1, beat, stage[:, 1, :], 0)
                    if norm1 and beat == 3:
                        norm_lo(n1, 2, wide_hi, wide_lo)
                    if beat == 4:
                        dve.wait_ge(h_landed, 64 * (t + 1))
                        add_out(t, 0, at)
                add_out(t, 1, at)

            def attention_of_first(b, j):
                attention_step(0, b, j, True, j == 3 and b + 1 < NB)
                if j == 1 and b + 1 < NB:
                    qk_gain(0, b + 1)
                if (b, j) in MEAN_AT:
                    pool_mean(0, MEAN_AT[b, j])

            def first_attention(beat):
                if beat == 6:
                    for b in range(NB):
                        qk_mean(0, b, first_sq[:, b, :])
                if beat == 7:
                    qk_scale(0, 0)
                    qk_gain(0, 0)
                    stage_k(0, 0)
                    qk_scale(0, 1)
                    dve.wait_ge(masked, 1)
                    dve.wait_ge(bias_landed, 32)
                if beat == 9:
                    qk_scale(0, 2)
                for half in range(2):
                    if (beat, half) in STEPS_IN_Z:
                        attention_of_first(*STEPS_IN_Z[beat, half])
                if beat == 9:
                    qk_scale(0, 3)

            def z_section(s, at, n2):
                for beat in range(10):
                    split(at + beat + 1, (beat + 1) % 2)
                    if n2 is not None and beat == 0:
                        dve.wait_ge(band_stored, 16)
                        normalise(n2, 0, h[:, 0, :], 1)
                        normalise(n2, 1, h[:, 1, :], 1)
                    if n2 is not None and beat == 1:
                        normalise(n2, 2, h[:, 2, :], 1)
                        norm_lo(n2, 0, hn_hi, hn_lo)
                    if n2 is not None and beat == 2:
                        normalise(n2, 3, h[:, 3, :], 1)
                        norm_lo(n2, 1, hn_hi, hn_lo)
                        norm_lo(n2, 2, hn_hi, hn_lo)
                    if n2 is not None and beat == 3:
                        norm_lo(n2, 3, hn_hi, hn_lo)
                    if n2 is None and beat < 4:
                        for n in (2 * beat, 2 * beat + 1):
                            dve.wait_ge(band_banks, n + 1)
                            nc.vector.tensor_copy(band[:, n, :], bank[4 + n % 4][:, 0:BAND]
                                                  ).then_inc(band_built, 1)
                    if beat == 6:
                        for b in range(NB):
                            copy_kv(s, b, at)
                    if n2 is None:
                        first_attention(beat)
                        continue
                    if beat == 7:
                        qk_mean(s, 0)
                        qk_mean(s, 1)
                    if beat == 8:
                        qk_scale(s, 0)
                        qk_mean(s, 2)
                        qk_scale(s, 1)
                    if beat == 9:
                        qk_mean(s, 3)
                        qk_scale(s, 2)
                        qk_scale(s, 3)

            dve.wait_ge(gain_landed, 16)
            for b in range(NB):
                normalise(0, b, h[:, b, :], 0)
                if b == 2:
                    split(0, 0)
                if b:
                    norm_lo(0, b - 1, wide_hi, wide_lo)
            norm_lo(0, 3, wide_hi, wide_lo)
            dve.wait_ge(consts, CONSTS)
            dve.wait_ge(out_stored, 32)
            dve.wait_ge(mask_row, 1)
            nc.vector.tensor_copy(rel_rows[0:N_BUCKETS, :, :],
                                  rel_sb[:, :].unsqueeze(2).to_broadcast([N_BUCKETS, NQ, P])
                                  ).then_inc(rel_ready, 1)
            nc.vector.tensor_scalar(out=neg_sink[:, :, :], in0=sink[:, :, :], scalar1=-1.0, scalar2=None,
                                    op0=ALU.mult).then_inc(glu_free, 2)
            dve.wait_ge(wp_hi_done, 1)
            nc.vector.tensor_tensor(wp_lo[:, :, :].rearrange("p g d -> p (g d)"), act_a[:, :],
                                    wp_hi[:, :, :].rearrange("p g d -> p (g d)").bitcast(F32),
                                    ALU.subtract).then_inc(wp_lo_done, 1)
            dve.wait_ge(nT, 8)
            nc.vector.memset(scores[:, :, :, 0:P], MASKED).then_inc(masked, 1)
            z_section(0, 0, None)
            split(Z_P + 1, 1)
            for b, j in STEPS_AFTER_Z:
                attention_of_first(b, j)
            for g in range(NPOOL):
                attention_step(0, NB, g, True)
                pool_y_rest(0, g)
            dve.wait_ge(pv, 16)
            split_v(NB - 1, 0).then_inc(v_split, 1)
            dve.wait_ge(v_split, 1)

            with dve.Fori(0, LAST) as t:
                out_section(t, True)
                z_section(t + 1, iter_base(t) + OUT_P, 3 * t + 2)
                ffn_section(t, False)
                ple_section(t, False)
            out_section(LAST, False)
            for b in range(NB):
                normalise(3 * LAST + 1, b, h[:, b, :], 1)
                if b:
                    norm_lo(3 * LAST + 1, b - 1, hn_hi, hn_lo)
            norm_lo(3 * LAST + 1, 3, hn_hi, hn_lo)
            ffn_section(LAST, True)
            ple_section(LAST, True)

        @block.tensor
        def _(pe):
            mm = nc.tensor.matmul

            def alone(value):
                value = value if isinstance(value, int) else pe.to_reg(value)
                pe.wait_ge(rel_ready, 1)
                return value

            def rows_panel(i, parity, xh, xl, ks, banks, first, last, signal, free=None, width=T,
                           halfway=None):
                pe.wait_ge(lo_done, i + 1)
                for b in range(NB):
                    if b == NB // 2 and halfway is not None:
                        halfway()
                    if first and free is not None:
                        free(b)
                    out_ap = banks[b][:, 0:width]
                    tok = slice(b * P, (b + 1) * P)
                    for kk, k in enumerate(ks):
                        cols = slice(kk * width, (kk + 1) * width)
                        wh, wl = w_hi[:, parity, cols], w_lo[:, parity, cols]
                        mm(out_ap, xh[:, k, tok], wh, start=first and kk == 0, stop=False)
                        mm(out_ap, xh[:, k, tok], wl, start=False, stop=False)
                        ins = mm(out_ap, xl[:, k, tok], wh, start=False,
                                 stop=last and kk == len(ks) - 1)
                    if last and b < HALF_SUMS:
                        ins.then_inc(signal, 1)
                ins.then_inc(panel_used, 1)

            def features_panel(i, parity, xh, xl, dst, halfway=None):
                pe.wait_ge(lo_done, i + 1)
                for k in range(KC):
                    if k == KC // 2 and halfway is not None:
                        halfway()
                    cols = slice(k * P, (k + 1) * P)
                    wh, wl = w_hi[:, parity, cols], w_lo[:, parity, cols]
                    mm(dst[:, :], wh, xh[:, k, :], start=k == 0, stop=False)
                    mm(dst[:, :], wh, xl[:, k, :], start=False, stop=False)
                    ins = mm(dst[:, :], wl, xh[:, k, :], start=False, stop=k == KC - 1)
                ins.then_inc(panel_used, 1)

            def transpose_norm(n_norm, b, free=None):
                pe.wait_ge(xn_done, 4 * n_norm + b + 1)
                for e in range(2):
                    if b < 2:
                        if free is not None:
                            free((2 * b + e) % 4)
                    else:
                        pe.wait_ge(nlo, 8 * n_norm + 2 * b + e - 3)
                    dst = bank[4 + (2 * b + e) % 4]
                    for k in range(4):
                        c = (4 * e + k) * P
                        ins = nc.tensor.transpose(dst[:, k * P:(k + 1) * P],
                                                  stage[:, b % 2, c:c + P], ident[:, :])
                    ins.then_inc(nT, 1)

            def transpose_qk(s, b, flowing=False):
                n = 4 * s + b
                pe.wait_ge(qkn_done, n + 1)
                pe.wait_ge(qstaged, n)
                for c in range(PAIRS):
                    ins = nc.tensor.transpose(bank[7][:, c * P:(c + 1) * P], qkn[:, c * P:(c + 1) * P],
                                              ident[:, :])
                ins.then_inc(tqk, 1)
                pe.wait_ge(probsT_copied, no_less(4 * n - 3) if flowing else 4 * n)
                nc.tensor.transpose(bank[5][:, 0:P], qkn[:, QW:QKW], ident[:, :]
                                    ).then_inc(tqk, 1)

            def logits_of(s, b, c):
                n = 16 * s + 4 * b + c
                if c == 0:
                    pe.wait_ge(qstaged, 4 * s + b + 1)
                    pe.wait_ge(kstaged, 4 * s + b + 1)
                pe.wait_ge(scaled, n)
                for j in range(2):
                    dst = bank[4][:, j * 2 * P:(j + 1) * 2 * P]
                    mm(dst, qT_hi[:, c, :], kT_hi[:, j, :], start=True, stop=False)
                    mm(dst, qT_hi[:, c, :], kT_lo[:, j, :], start=False, stop=False)
                    ins = mm(dst, qT_lo[:, c, :], kT_hi[:, j, :], start=False, stop=True)
                ins.then_inc(logits, 1)

            def transpose_probs(n, c, blocks):
                pe.wait_ge(pnorm, n + 1)
                pe.wait_ge(probsT_copied, n)
                pe.wait_ge(kstaged, blocks)
                for half in range(2):
                    for j in range(2):
                        at = (2 * half + j) * P
                        ins = nc.tensor.transpose(bank[5][:, at:at + P],
                                                  scores[:, c, j, half * P:(half + 1) * P], ident[:, :])
                ins.then_inc(probs_T, 1)

            def attend(s, b, c):
                n = 16 * s + 4 * b + c
                if c == 0:
                    pe.wait_ge(vstaged, 4 * s + b + 1)
                pe.wait_ge(probsT_copied, n + 1)
                pe.wait_ge(attn_lo, n)
                dst = bank[6][:, 0:2 * P]
                for half in range(2):
                    if first_tile(s):
                        ins = mm(dst, v_whole[:, half, :], probsT_whole[:, c % 2, half, :],
                                 start=half == 0, stop=half == 1)
                    else:
                        mm(dst, v_hi[:, half, :], probsT_hi[:, half, :], start=half == 0, stop=False)
                        mm(dst, v_hi[:, half, :], probsT_lo[:, half, :], start=False, stop=False)
                        ins = mm(dst, v_lo[:, half, :], probsT_hi[:, half, :], start=False,
                                 stop=half == 1)
                ins.then_inc(pv, 1)

            def attention_step(s, b, j, flowing):
                at = unit_at(b, j, 0, flowing)
                if at:
                    logits_of(s, *at)
                next_block = flowing and j == 3 and b + 1 < NB
                if next_block:
                    transpose_qk(s, b + 1, True)
                at = unit_at(b, j, LAG_PV, flowing)
                if at:
                    attend(s, *at)
                at = unit_at(b, j, LAG_T, flowing)
                if at:
                    blocks = 4 * s + (NB if isinstance(b, int) and b == NB else
                                      b + 2 if next_block else b + 1)
                    transpose_probs(16 * s + 4 * at[0] + at[1], at[1], blocks)

            def pool_y(s, g):
                pe.wait_ge(pool_lo, 4 * s + g + 1)
                dst = bank[y_bank(s, g)]
                mm(dst[:, :], wp_hi[:, g, :], mix_hi[:, 4 + g, :], start=True, stop=False)
                mm(dst[:, :], wp_hi[:, g, :], mix_lo[:, 4 + g, :], start=False, stop=False)
                mm(dst[:, :], wp_lo[:, g, :], mix_hi[:, 4 + g, :], start=False,
                   stop=True).then_inc(y_done, 1)

            def transpose_p(t, kk):
                pe.wait_ge(p_landed, 64 * (t + 1))
                for b in range(NB):
                    ins = nc.tensor.transpose(bank[4 + kk][:, b * P:(b + 1) * P],
                                              p_rows[:, b, kk * P:(kk + 1) * P], ident[:, :])
                ins.then_inc(pT, 1)

            def attention_banks_free(s, blocks, b):
                if b == 0:
                    pe.wait_ge(scaled, 16 * s + 4 * blocks)
                elif b == 1:
                    pe.wait_ge(probsT_copied, 16 * s + 4 * blocks)
                elif b == 2:
                    pe.wait_ge(attn_lo, 16 * s + 4 * blocks)
                else:
                    pe.wait_ge(qstaged, 4 * s + blocks)

            def ffn_section(t, last):
                at, s, n0 = ffn_base(t, last), t + 1, NCH * t
                first = 0
                if last:
                    pe.wait_ge(out_added, alone(8 * t + 4))
                else:
                    pe.wait_ge(ucopied, alone(4 * s + 2))
                    pe.wait_ge(kvcopied, 4 * s + 4)
                pe.wait_ge(nlo, 8 * norm2_no(t, last) + 8)
                for g, nk in enumerate(GROUPS):
                    if g:
                        pe.wait_ge(down_added, alone(24 * t + 8 * g - 4))

                    def high_banks_free():
                        if g:
                            pe.wait_ge(down_added, 24 * t + 8 * g)

                    if g < 2:
                        with pe.Fori(0, 2) as it:
                            for beat in range(8):
                                c = beat // 2
                                n = n0 + 8 * g + c + 4 * it
                                if beat % 2 == 0:
                                    pe.wait_ge(glu_free, n + 1)
                                if beat == 2 and not last:
                                    pe.wait_ge(ucopied, 4 * s + 4)
                                if not last and beat:
                                    attention_step(s, it + 2 * g, beat - 1, False)

                                def halfway():
                                    high_banks_free()
                                    if not last:
                                        transpose_qk(s, it + 2 * g)

                                features_panel(at + first + beat + it * 8, beat % 2, hn_hi, hn_lo,
                                               bank[2 * (c % 2) + beat % 2],
                                               halfway if beat == 0 else None)
                    else:
                        for beat in range(12):
                            c = beat // 2
                            if beat % 2 == 0:
                                pe.wait_ge(glu_free, n0 + 16 + c + 1)
                            features_panel(at + first + beat, beat % 2, hn_hi, hn_lo,
                                           bank[2 * (c % 2) + beat % 2],
                                           high_banks_free if beat == 0 else None)
                            if not last and beat % 2 == 0 and 2 <= beat <= 8:
                                pool_y(s, beat // 2 - 1)
                            if beat >= 9 and beat < 11:
                                if not last:
                                    pe.wait_ge(y_lo, 4 * s + beat - 9 + 1)
                                transpose_p(t, beat - 9)
                    done = n0 + 8 * g + nk
                    for e in range(2):
                        for r in range(nk // 2):
                            n = e * (nk // 2) + r
                            if e == 0:
                                pe.wait_ge(act_lo_done, n0 + 8 * g + 2 * r + 3)

                            def free(b):
                                if e == 0:
                                    pe.wait_ge(glu_free, done + 2 - (1 if b < 2 else 0))
                                elif g < 2 and not last:
                                    attention_banks_free(s, 2 * g + 2, b)
                                elif g == 2 and b < 2:
                                    pe.wait_ge(pT_lo, 2 * t + b + 1)
                                elif g == 2 and not last:
                                    pe.wait_ge(y_lo, 4 * s + b + 1)

                            rows_panel(at + first + 2 * nk + n, n % 2, wide_hi, wide_lo,
                                       (2 * r, 2 * r + 1), bank[4 * e:4 * e + 4], r == 0,
                                       r == nk // 2 - 1, down, free)
                    first += 3 * nk

            def ple_section(t, last):
                at = ffn_base(t, last) + FFN_P
                n3 = norm2_no(t, last) + 1
                pe.wait_ge(pT_lo, 2 * t + 2)

                def norm3(b):
                    transpose_norm(n3, b, lambda q: pe.wait_ge(down_added, 24 * t + 20 + q + 1))

                for e in range(2):
                    def free(b):
                        pe.wait_ge(*((down_added, 24 * t + 16 + b + 1) if e == 0
                                     else (pp_copied, 8 * t + b + 1)))
                    rows_panel(at + e, e, p_hi, p_lo, range(KP), bank[0:4], True, True, pp, free,
                               halfway=lambda: norm3(2 * e))
                    norm3(2 * e + 1)
                pe.wait_ge(nlo, 8 * n3 + 8)
                for e in range(2):
                    for r in range(4):
                        def free(b):
                            if e == 0:
                                pe.wait_ge(pp_copied, 8 * t + 4 + b + 1)
                        rows_panel(at + PROJ_P + 4 * e + r, r % 2, hn_hi, hn_lo, (2 * r, 2 * r + 1),
                                   bank[4 * e:4 * e + 4], r == 0, r == 3, gt, free)

            def out_section(t, norm1):
                at = iter_base(t)
                n1 = 3 * t + 1
                pe.wait_ge(y_lo, 4)
                for e in range(2):
                    for r in range(4):
                        if e == 0 and r == 2:
                            pe.wait_ge(y_lo, 4 * t + 4)

                        def free(b):
                            pe.wait_ge(sig, 8 * t + 4 * e + b + 1)
                            if e == 0:
                                pe.wait_ge(attn_lo, 16 * t + 4 * b + 4)
                            if e == 1 and norm1:
                                pe.wait_ge(nlo, 8 * n1 + 4 + b + 1)
                        def norm(b):
                            transpose_norm(n1, b, lambda q: pe.wait_ge(sig, 8 * t + 4 + q + 1))

                        rows_panel(at + 4 * e + r, r % 2, mix_hi, mix_lo, (2 * r, 2 * r + 1),
                                   bank[4 * e:4 * e + 4], r == 0, r == 3, outp, free,
                                   halfway=(lambda: norm(2)) if norm1 and e == 0 and r == 3 else None)
                        if norm1 and e == 0:
                            for b in {1: (0, 1), 3: (3,)}.get(r, ()):
                                norm(b)

            def first_attention(beat, half):
                if (beat, half) == (7, 0):
                    pe.wait_ge(kvcopied, 4)
                    transpose_qk(0, 0, True)
                if (beat, half) in STEPS_IN_Z:
                    attention_step(0, *STEPS_IN_Z[beat, half], True)

            def z_section(s, at, n2, n_before):
                for c in range(4):
                    def free(b):
                        if n2 is not None:
                            pe.wait_ge(out_added, 8 * (s - 1) + b + 1)
                        else:
                            if b in (1, 2):
                                transpose_norm(0, b + 1)
                            pe.wait_ge(nlo, 2 * b + 2)

                    def norm(b):
                        transpose_norm(n2, b, lambda q: pe.wait_ge(out_added, 8 * (s - 1) + 4 + q + 1))

                    rows_panel(at + c, c % 2, wide_hi, wide_lo, (2 * c, 2 * c + 1), bank[0:4],
                               c == 0, c == 3, zq, free,
                               halfway=(lambda: norm(2 * c - 2)) if n2 is not None and c in (1, 2)
                               else None)
                    if n2 is None:
                        for n in (2 * c, 2 * c + 1):
                            if n == 0:
                                pe.wait_ge(rel_ready, 1)
                            if n < 4:
                                pe.wait_ge(nlo, 4 + n + 1)
                            else:
                                pe.wait_ge(band_built, n - 3)
                            mm(bank[4 + n % 4][:, 0:3 * P], rel_rows[0:N_BUCKETS + 1, n, :],
                               onehot_sb[:, :], start=True, stop=True).then_inc(band_banks, 1)
                    if n2 is not None and c in (1, 2):
                        norm(2 * c - 1)
                for c in range(2):
                    def free(b):
                        pe.wait_ge(nlo, 8 * n_before + 4 + b + 1)
                        if n2 is None:
                            pe.wait_ge(band_built, 4 + b + 1)
                    rows_panel(at + 4 + c, c % 2, wide_hi, wide_lo, range(4 * c, 4 * c + 4), bank[4:8],
                               c == 0, c == 1, zkv, free, width=2 * KVW)
                for g in range(NPOOL):
                    pe.wait_ge(qcopied, 4 * s + g + 1)
                    features_panel(at + 6 + g, g % 2, wide_hi, wide_lo, bank[g],
                                   (lambda: first_attention(6 + g, 0)) if n2 is None else None)
                    if n2 is None:
                        first_attention(6 + g, 1)

            pe.wait_ge(ident_landed, 16)
            transpose_norm(0, 0)
            transpose_norm(0, 1)
            z_section(0, 0, None, 0)
            for b, j in STEPS_AFTER_Z:
                attention_step(0, b, j, True)
            pe.wait_ge(wp_lo_done, 1)
            for g in range(NPOOL):
                attention_step(0, NB, g, True)
                pool_y(0, g)

            with pe.Fori(0, LAST) as t:
                out_section(t, True)
                z_section(t + 1, iter_base(t) + OUT_P, 3 * t + 2, 3 * t + 2)
                ffn_section(t, False)
                ple_section(t, False)
            out_section(LAST, False)
            for b in range(NB):
                transpose_norm(3 * LAST + 1, b,
                               lambda q: pe.wait_ge(out_added, 8 * LAST + 4 + q + 1))
            ffn_section(LAST, True)
            ple_section(LAST, True)


def bucket_of(dist):
    n = np.maximum(dist, 0)
    exact = N_BUCKETS // 2
    far = exact + (np.log(np.maximum(n, 1).astype(np.float64) / exact)
                   / np.log(MAX_DISTANCE / exact) * (N_BUCKETS - exact)).astype(np.int64)
    return np.where(n < exact, n, np.minimum(far, N_BUCKETS - 1))


def kernel(**inputs):
    import concourse.bacc as _bacc
    from concourse.bass_utils import run_bass_kernel_spmd as _run

    nc = _bacc.Bacc("TRN2", target_bir_lowering=False, num_devices=1, dynamic_dma_scratch_size=4096)
    names = ["x", "p", "w_in", "w_out", "g_attn_norm", "g_q", "g_k", "attn_sinks", "rel_bias", "w_pool",
             "pool_scale", "g_ffn_norm", "w_gate", "w_up", "w_down", "g_ple_norm", "w_ple_gate",
             "w_ple_proj"]
    arrays = {}
    for name in names:
        a = np.ascontiguousarray(inputs[name])
        if name == "p":
            a = a[0, 0]
        elif name != "rel_bias":
            a = a[0]
        arrays[name] = a
    dist = 2 * P - 1 - np.arange(3 * P)
    inside = (dist >= 0) & (dist < WINDOW)
    row = np.where(inside, bucket_of(dist), N_BUCKETS)
    arrays["onehot"] = (row[None, :] == np.arange(N_BUCKETS + 1)[:, None]).astype(np.float32)
    arrays["identity"] = np.eye(P, dtype=np.float32)
    arrays["edge"] = np.array([[w / min(i + 1, w) for i in range(CARRY)] for w in POOL_SIZES],
                              dtype=np.float32)
    aps = [nc.dram_tensor(f"in_{n}", a.shape, F32, kind="ExternalInput").ap()
           for n, a in arrays.items()]
    out = nc.dram_tensor("out_h", arrays["x"].shape, F32, kind="ExternalOutput").ap()
    by = dict(zip(arrays, aps))
    build(nc, by["x"], by["p"], by["w_in"], by["w_out"], by["g_attn_norm"], by["g_q"], by["g_k"],
          by["attn_sinks"], by["rel_bias"], by["w_pool"], by["pool_scale"], by["g_ffn_norm"],
          by["w_gate"], by["w_up"], by["w_down"], by["g_ple_norm"], by["w_ple_gate"],
          by["w_ple_proj"], by["identity"], by["onehot"], by["edge"], out)
    r = _run(nc, [{f"in_{n}": a for n, a in arrays.items()}], core_ids=[0])
    return r.results[0]["out_h"][None]
```
